# Optimizing a Trainium2 kernel written in Bass

```python
import jax
import jax.numpy as jnp
from jax import lax
import numpy as np

D_MODEL = 1024
BATCH = 1
SEQ = 256
DEPTH = 2
DEC_BATCH = 8
DEC_SEQ = 16
PAST_LEN = 256

CHUNK = 64
N_META = 16
HEAD_DIM = 64
N_HEADS_A = D_MODEL // (2 * HEAD_DIM)
N_HEADS_B = D_MODEL // (2 * HEAD_DIM)
N_KV_B = 2
GROUP_B = N_HEADS_B // N_KV_B
WINDOW = 128
WINDOW_CHUNKS = WINDOW // CHUNK
Q_BLOCK = 128
D_FF = 2816
N_EXPERTS = 8
TOP_K = 2
MOE_FF = 1408
EPS = 1e-6
NEG = -1e30

WIDTH_A = N_HEADS_A * HEAD_DIM
WIDTH_B = N_HEADS_B * HEAD_DIM
KV_WIDTH_B = N_KV_B * HEAD_DIM
OFF_QA = 0
OFF_KA = OFF_QA + WIDTH_A
OFF_VA = OFF_KA + WIDTH_A
OFF_FA = OFF_VA + WIDTH_A
OFF_QB = OFF_FA + N_HEADS_A
OFF_KB = OFF_QB + WIDTH_B
OFF_VB = OFF_KB + KV_WIDTH_B
IN_COLS = OFF_VB + KV_WIDTH_B
N_DENSE = (DEPTH + 1) // 2
N_MOE = DEPTH // 2

kernel_name = 'hybrid_fox_swa_stream_step'

def _rmsnorm(x, g):
    xf = x.astype(jnp.float32)
    y = xf * lax.rsqrt(jnp.mean(xf * xf, axis=-1, keepdims=True) + EPS) * g.astype(jnp.float32)
    return y.astype(x.dtype)

def _alibi_slopes():
    h = jnp.arange(1, N_HEADS_B + 1, dtype=jnp.float32)
    return jnp.exp2(-8.0 * h / N_HEADS_B).reshape(N_KV_B, GROUP_B)

def _project(a, w_in, b_f, qn_a, kn_a, qn_b, kn_b):
    B, T, _ = a.shape
    p = jnp.einsum('btd,de->bte', a, w_in)
    q_a = _rmsnorm(p[..., OFF_QA:OFF_KA].reshape(B, T, N_HEADS_A, HEAD_DIM), qn_a)
    k_a = _rmsnorm(p[..., OFF_KA:OFF_VA].reshape(B, T, N_HEADS_A, HEAD_DIM), kn_a)
    v_a = p[..., OFF_VA:OFF_FA].reshape(B, T, N_HEADS_A, HEAD_DIM)
    logf = jax.nn.log_sigmoid((p[..., OFF_FA:OFF_QB] + b_f).astype(jnp.float32))
    q_b = _rmsnorm(p[..., OFF_QB:OFF_KB].reshape(B, T, N_HEADS_B, HEAD_DIM), qn_b)
    q_b = q_b.reshape(B, T, N_KV_B, GROUP_B, HEAD_DIM)
    k_b = _rmsnorm(p[..., OFF_KB:OFF_VB].reshape(B, T, N_KV_B, HEAD_DIM), kn_b)
    v_b = p[..., OFF_VB:IN_COLS].reshape(B, T, N_KV_B, HEAD_DIM)
    return q_a, k_a, v_a, logf, q_b, k_b, v_b

def _fox_attention(q, k, v, Fq, Fk, qpos, kpos):
    B, Tq, H, D = q.shape
    scale = HEAD_DIM ** -0.5
    Fk_t = jnp.transpose(Fk, (0, 2, 1))

    def block(args):
        qb, Fqb, qposb = args
        s = jnp.einsum('bqhd,bkhd->bhqk', qb, k).astype(jnp.float32) * scale
        s = s + jnp.transpose(Fqb, (0, 2, 1))[:, :, :, None] - Fk_t[:, :, None, :]
        s = jnp.where((kpos[None, :] <= qposb[:, None])[None, None], s, NEG)
        p = jax.nn.softmax(s, axis=-1)
        return jnp.einsum('bhqk,bkhd->bqhd', p.astype(v.dtype), v)

    if Tq <= Q_BLOCK:
        return block((q, Fq, qpos))
    nb = -(-Tq // Q_BLOCK)
    pad = nb * Q_BLOCK - Tq
    qp = jnp.pad(q, ((0, 0), (0, pad), (0, 0), (0, 0))).reshape(B, nb, Q_BLOCK, H, D).transpose(1, 0, 2, 3, 4)
    Fqp = jnp.pad(Fq, ((0, 0), (0, pad), (0, 0))).reshape(B, nb, Q_BLOCK, H).transpose(1, 0, 2, 3)
    qposp = jnp.pad(qpos, (0, pad)).reshape(nb, Q_BLOCK)
    out = lax.map(block, (qp, Fqp, qposp))
    return out.transpose(1, 0, 2, 3, 4).reshape(B, nb * Q_BLOCK, H, D)[:, :Tq]

def _swa_sink_attention(q, k, v, sinks, slopes, qpos, kpos, mask):
    scale = HEAD_DIM ** -0.5
    s = jnp.einsum('bnqkgd,bnskd->bnkgqs', q, k).astype(jnp.float32) * scale
    dist = jnp.abs(qpos[:, :, None] - kpos[:, None, :]).astype(jnp.float32)
    s = s - slopes[None, None, :, :, None, None] * dist[None, :, None, None, :, :]
    s = jnp.where(mask[None, :, None, None], s, NEG)
    sink = jnp.broadcast_to(sinks.astype(jnp.float32)[None, None, :, :, None, None], s.shape[:-1] + (1,))
    p = jax.nn.softmax(jnp.concatenate([s, sink], axis=-1), axis=-1)[..., :-1]
    return jnp.einsum('bnkgqs,bnskd->bnqkgd', p.astype(v.dtype), v)

def _swa_prompt(q_b, k_b, v_b, sinks, slopes):
    B, L = q_b.shape[:2]
    q_front = CHUNK - N_META
    k_front = (WINDOW_CHUNKS + 1) * CHUNK - N_META
    band_len = (WINDOW_CHUNKS + 1) * CHUNK
    nq = (L + q_front) // CHUNK
    qp = jnp.pad(q_b, ((0, 0), (q_front, 0), (0, 0), (0, 0), (0, 0)))
    qp = qp.reshape(B, nq, CHUNK, N_KV_B, GROUP_B, HEAD_DIM)
    pad_k = ((0, 0), (k_front, 0), (0, 0), (0, 0))
    kp = jnp.pad(k_b, pad_k).reshape(B, nq + WINDOW_CHUNKS, CHUNK, N_KV_B, HEAD_DIM)
    vp = jnp.pad(v_b, pad_k).reshape(B, nq + WINDOW_CHUNKS, CHUNK, N_KV_B, HEAD_DIM)
    kband = jnp.concatenate([kp[:, j:j + nq] for j in range(WINDOW_CHUNKS + 1)], axis=2)
    vband = jnp.concatenate([vp[:, j:j + nq] for j in range(WINDOW_CHUNKS + 1)], axis=2)
    qpos = jnp.arange(nq * CHUNK).reshape(nq, CHUNK) - q_front
    kidx = jnp.arange(nq)[:, None] * CHUNK + jnp.arange(band_len)[None, :]
    kpos = kidx - k_front
    mask = jnp.broadcast_to((kidx >= k_front)[:, None, :], (nq, CHUNK, band_len))
    out = _swa_sink_attention(qp, kband, vband, sinks, slopes, qpos, kpos, mask)
    return out.reshape(B, nq * CHUNK, N_KV_B, GROUP_B, HEAD_DIM)[:, q_front:]

def _swa_sample(q_b, k_b, v_b, cache_k, cache_v, sinks, slopes):
    B, T = q_b.shape[:2]
    W = cache_k.shape[1]
    k_all = jnp.concatenate([cache_k, k_b], axis=1)[:, None]
    v_all = jnp.concatenate([cache_v, v_b], axis=1)[:, None]
    qpos = (PAST_LEN + jnp.arange(T))[None]
    kpos = (PAST_LEN - W + jnp.arange(W + T))[None]
    cq = (qpos // CHUNK)[:, :, None]
    ck = (kpos // CHUNK)[:, None, :]
    mask = (ck <= cq) & (ck >= cq - WINDOW_CHUNKS)
    out = _swa_sink_attention(q_b[:, None], k_all, v_all, sinks, slopes, qpos, kpos, mask)
    return out[:, 0]

def _merge(h, y_a, y_b, w_out):
    B, T = h.shape[:2]
    y = jnp.concatenate([y_a.reshape(B, T, WIDTH_A), y_b.reshape(B, T, WIDTH_B)], axis=-1)
    return h + jnp.einsum('btc,cd->btd', y, w_out)

def _moe(c, w_router, b_router, we_gate, we_up, we_down):
    B, T, D = c.shape
    xt = c.reshape(B * T, D)
    logits = jnp.dot(xt, w_router).astype(jnp.float32) + b_router.astype(jnp.float32)
    top_v, top_i = lax.top_k(logits, TOP_K)
    g = jax.nn.softmax(top_v, axis=-1)
    gate = jnp.sum(jax.nn.one_hot(top_i, N_EXPERTS, dtype=jnp.float32) * g[..., None], axis=1)
    out = jnp.zeros_like(xt)
    for e in range(N_EXPERTS):
        hid = jax.nn.silu(jnp.dot(xt, we_gate[e])) * jnp.dot(xt, we_up[e])
        out = out + gate[:, e:e + 1].astype(xt.dtype) * jnp.dot(hid, we_down[e])
    return out.reshape(B, T, D)

def _channel(h, l, g_ffn, w_gate, w_up, w_down, w_router, b_router, we_gate, we_up, we_down):
    c = _rmsnorm(h, g_ffn[l])
    i = l // 2
    if l % 2 == 0:
        f = jnp.dot(jax.nn.silu(jnp.dot(c, w_gate[i])) * jnp.dot(c, w_up[i]), w_down[i])
    else:
        f = _moe(c, w_router[i], b_router[i], we_gate[i], we_up[i], we_down[i])
    return h + f

def setup_inputs(seed: int = 0) -> dict:
    key = jax.random.key(seed)
    ks = jax.random.split(key, 28)
    f32 = jnp.float32

    def nrm(k, shape, scale=1.0):
        return jax.random.normal(k, shape, f32) * scale

    swa_rows = min(WINDOW, PAST_LEN)
    return {
        'x_prompt': nrm(ks[0], (BATCH, SEQ, D_MODEL)),
        'x_sample': nrm(ks[1], (DEC_BATCH, DEC_SEQ, D_MODEL)),
        'cache_fox_k': nrm(ks[2], (DEPTH, DEC_BATCH, PAST_LEN, N_HEADS_A, HEAD_DIM)),
        'cache_fox_v': nrm(ks[3], (DEPTH, DEC_BATCH, PAST_LEN, N_HEADS_A, HEAD_DIM)),
        'cache_fox_logf': jax.nn.log_sigmoid(2.0 + nrm(ks[4], (DEPTH, DEC_BATCH, PAST_LEN, N_HEADS_A))),
        'cache_swa_k': nrm(ks[5], (DEPTH, DEC_BATCH, swa_rows, N_KV_B, HEAD_DIM)),
        'cache_swa_v': nrm(ks[6], (DEPTH, DEC_BATCH, swa_rows, N_KV_B, HEAD_DIM)),
        'meta_tokens': nrm(ks[7], (N_META, D_MODEL)),
        'g_attn': 1.0 + nrm(ks[8], (DEPTH, D_MODEL), 0.05),
        'w_in': nrm(ks[9], (DEPTH, D_MODEL, IN_COLS), D_MODEL ** -0.5),
        'b_f': 2.0 + nrm(ks[10], (DEPTH, N_HEADS_A), 0.1),
        'qn_a': 1.0 + nrm(ks[11], (DEPTH, HEAD_DIM), 0.05),
        'kn_a': 1.0 + nrm(ks[12], (DEPTH, HEAD_DIM), 0.05),
        'qn_b': 1.0 + nrm(ks[13], (DEPTH, HEAD_DIM), 0.05),
        'kn_b': 1.0 + nrm(ks[14], (DEPTH, HEAD_DIM), 0.05),
        'sinks': nrm(ks[15], (DEPTH, N_HEADS_B)),
        'w_out': nrm(ks[16], (DEPTH, D_MODEL, D_MODEL), D_MODEL ** -0.5),
        'g_ffn': 1.0 + nrm(ks[17], (DEPTH, D_MODEL), 0.05),
        'w_gate': nrm(ks[18], (N_DENSE, D_MODEL, D_FF), D_MODEL ** -0.5),
        'w_up': nrm(ks[19], (N_DENSE, D_MODEL, D_FF), D_MODEL ** -0.5),
        'w_down': nrm(ks[20], (N_DENSE, D_FF, D_MODEL), D_FF ** -0.5),
        'w_router': nrm(ks[21], (N_MOE, D_MODEL, N_EXPERTS), D_MODEL ** -0.5),
        'b_router': nrm(ks[22], (N_MOE, N_EXPERTS), 0.01),
        'we_gate': nrm(ks[23], (N_MOE, N_EXPERTS, D_MODEL, MOE_FF), D_MODEL ** -0.5),
        'we_up': nrm(ks[24], (N_MOE, N_EXPERTS, D_MODEL, MOE_FF), D_MODEL ** -0.5),
        'we_down': nrm(ks[25], (N_MOE, N_EXPERTS, MOE_FF, D_MODEL), MOE_FF ** -0.5),
    }

def reference(x_prompt, x_sample, cache_fox_k, cache_fox_v, cache_fox_logf, cache_swa_k, cache_swa_v,
              meta_tokens, g_attn, w_in, b_f, qn_a, kn_a, qn_b, kn_b, sinks, w_out, g_ffn,
              w_gate, w_up, w_down, w_router, b_router, we_gate, we_up, we_down):
    slopes = _alibi_slopes()
    swa_rows = cache_swa_k.shape[2]
    P = cache_fox_k.shape[2]
    Bp = x_prompt.shape[0]
    meta = jnp.broadcast_to(meta_tokens.astype(x_prompt.dtype)[None], (Bp, N_META, D_MODEL))
    h_p = jnp.concatenate([meta, x_prompt], axis=1)
    h_s = x_sample
    L = h_p.shape[1]
    T = h_s.shape[1]
    pos_p = jnp.arange(L)
    fk_p, fv_p, fl_p, sk_p, sv_p = [], [], [], [], []
    fk_s, fv_s, fl_s, sk_s, sv_s = [], [], [], [], []
    for l in range(DEPTH):
        sink_l = sinks[l].reshape(N_KV_B, GROUP_B)
        a = _rmsnorm(h_p, g_attn[l])
        q_a, k_a, v_a, logf, q_b, k_b, v_b = _project(a, w_in[l], b_f[l], qn_a[l], kn_a[l], qn_b[l], kn_b[l])
        F = jnp.cumsum(logf, axis=1)
        y_a = _fox_attention(q_a, k_a, v_a, F, F, pos_p, pos_p)
        y_b = _swa_prompt(q_b, k_b, v_b, sink_l, slopes)
        h_p = _merge(h_p, y_a, y_b, w_out[l])
        h_p = _channel(h_p, l, g_ffn, w_gate, w_up, w_down, w_router, b_router, we_gate, we_up, we_down)
        fk_p.append(k_a)
        fv_p.append(v_a)
        fl_p.append(logf)
        sk_p.append(k_b[:, L - swa_rows:])
        sv_p.append(v_b[:, L - swa_rows:])
        a = _rmsnorm(h_s, g_attn[l])
        q_a, k_a, v_a, logf, q_b, k_b, v_b = _project(a, w_in[l], b_f[l], qn_a[l], kn_a[l], qn_b[l], kn_b[l])
        kf = jnp.concatenate([cache_fox_k[l], k_a], axis=1)
        vf = jnp.concatenate([cache_fox_v[l], v_a], axis=1)
        F = jnp.cumsum(jnp.concatenate([cache_fox_logf[l].astype(jnp.float32), logf], axis=1), axis=1)
        y_a = _fox_attention(q_a, kf, vf, F[:, P:], F, P + jnp.arange(T), jnp.arange(P + T))
        y_b = _swa_sample(q_b, k_b, v_b, cache_swa_k[l], cache_swa_v[l], sink_l, slopes)
        h_s = _merge(h_s, y_a, y_b, w_out[l])
        h_s = _channel(h_s, l, g_ffn, w_gate, w_up, w_down, w_router, b_router, we_gate, we_up, we_down)
        fk_s.append(k_a)
        fv_s.append(v_a)
        fl_s.append(logf)
        sk_s.append(k_b)
        sv_s.append(v_b)
    y_prompt = h_p[:, N_META:]
    y_sample = h_s
    fox_k_prompt = jnp.stack(fk_p)
    fox_v_prompt = jnp.stack(fv_p)
    fox_logf_prompt = jnp.stack(fl_p)
    swa_k_prompt = jnp.stack(sk_p)
    swa_v_prompt = jnp.stack(sv_p)
    fox_k_sample = jnp.stack(fk_s)
    fox_v_sample = jnp.stack(fv_s)
    fox_logf_sample = jnp.stack(fl_s)
    swa_k_sample = jnp.stack(sk_s)
    swa_v_sample = jnp.stack(sv_s)
    return (y_prompt, y_sample, fox_k_prompt, fox_v_prompt, fox_logf_prompt, swa_k_prompt, swa_v_prompt,
            fox_k_sample, fox_v_sample, fox_logf_sample, swa_k_sample, swa_v_sample)


_drawn_inputs = setup_inputs


def setup_inputs(seed=0):
    import zlib

    import numpy as np

    out = dict(_drawn_inputs(seed))
    spreads = {}
    factors = {'sinks': 2.748}
    for name, (base, spread) in spreads.items():
        noise = np.random.default_rng([zlib.crc32(name.encode()), seed]).standard_normal(out[name].shape)
        drawn = base * np.exp(spread * noise) if base else spread * noise
        out[name] = jnp.asarray(drawn.astype(out[name].dtype))
    for name, factor in factors.items():
        out[name] = (out[name] * factor).astype(out[name].dtype)
    return out
```

```python
from contextlib import ExitStack

import numpy as np

import concourse.bass as bass
from concourse import mybir

ALU = mybir.AluOpType
ACT = mybir.ActivationFunctionType
F32 = mybir.dt.float32
U32 = mybir.dt.uint32
I32 = mybir.dt.int32
AX_X = mybir.AxisListType.X

P = 128
DEPTH = 2
D = 1024
KD = D // P
HD = 64
NMETA, SEQ = 16, 256
TP = NMETA + SEQ
BS, TSEQ = 8, 16
TSM = BS * TSEQ
T = TP + TSM
PAST = 256
CHUNK = 64
H = 8
NPAIR = 4
FF = 2816
FCH = FF // P
E = 8
MFF = 1408
MCH = MFF // P
MBLK = 4
MB = MFF // MBLK
EPS = 1e-6
BIG = 1e33
OOB = 8192
NEG = -1e30

RING = 6
SLOT = KD * MB
assert SLOT == FCH * P == MCH * 256

QT = [(0, 128), (128, 128), (256, 16), (TP, TSM)]
TT = [(0, 128), (128, 128), (256, 128), (384, 16)]
MAXR = -(-T // P)

PC = {}
_o = 0
for _n, _w in (("g_attn", KD), ("g_ffn", KD), ("qn_a", 1), ("kn_a", 1), ("qn_b", 1), ("kn_b", 1), ("b_f", H),
               ("sink", 16), ("b_r", E)):
    PC[_n] = _o
    _o += _w
NPAR = _o

DA, DB, DC, DS = 0, 80, 80 + 208, 80 + 208 + TP
NDIST = DS + 2 * 256


def shape_tables():
    f = np.float32
    ident = np.eye(P, dtype=f)
    pm = np.zeros((P, P), f)
    pm[:HD, :HD] = 1.0 / HD
    pm[HD:, HD:] = 1.0 / HD
    p = np.arange(P)
    t = np.arange(TP)
    negtri = np.zeros((P, 3, TP), f)
    for i in range(3):
        negtri[:, i, :] = -1.0 * ((128 * i + p)[:, None] <= t[None, :])
    b, q = p // TSEQ, p % TSEQ
    newtri = -1.0 * ((b[:, None] == b[None, :]) & (q[:, None] <= q[None, :]))
    cmask = np.where(p[None, :] > p[:, None], NEG, 0.0)
    row_b4, row_h, row_q = p // 32, (p // 16) % 2, p % 16
    smask = np.zeros((P, 2, P), f)
    dist = np.full((P, NDIST), BIG, f)
    chunk = (t + CHUNK - NMETA) // CHUNK

    def prompt_dist(rows, keys):
        ok = (chunk[keys][None] <= chunk[rows][:, None]) & (chunk[keys][None] >= chunk[rows][:, None] - 2)
        return np.where(ok, np.abs(rows[:, None] - keys[None]), BIG)
    dist[:80, DA:DA + 80] = prompt_dist(t[:80], t[:80])
    dist[:, DB:DB + 208] = prompt_dist(t[80:208], t[:208])
    dist[:, DC:DC + TP] = prompt_dist(np.concatenate([t[208:], t[208:]]), t)
    for s in range(2):
        same = (4 * s + row_b4)[:, None] == b[None, :]
        smask[:, s, :] = np.where(same & (q[None, :] <= row_q[:, None]), 0.0, NEG)
        dist[:, DS + 256 * s:DS + 256 * s + 128] = 128 + row_q[:, None] - p[None, :]
        dist[:, DS + 256 * s + 128:DS + 256 * s + 256] = np.where(same, np.abs(row_q[:, None] - q[None, :]), BIG)
    negslope = np.zeros((P, NPAIR, 4), f)
    for j in range(NPAIR):
        lo, hi = -2.0 ** -(j + 1), -2.0 ** -(j + 5)
        negslope[:, j, 0] = lo
        negslope[:, j, 1] = hi
        negslope[:, j, 2] = np.where(p < 64, lo, hi)
        negslope[:, j, 3] = np.where(row_h == 0, lo, hi)
    sel = np.zeros((64, NPAIR, 4, P), f)
    for pr in range(NPAIR):
        for s in range(2):
            sel[(4 * s + row_b4) * H + 2 * pr + row_h, pr, s, p] = 1.0
        for h2 in range(2):
            sel[2 * pr + h2, pr, 2 + h2, :] = 1.0
    bmask = (np.arange(TSM)[:, None] // TSEQ == np.arange(64)[None, :] // H).astype(f)
    tri_strict = (p[:, None] < p[None, :]).astype(f)
    iota = np.broadcast_to(p[None, :], (P, P))
    first = np.broadcast_to((np.arange(E)[None, :] < np.arange(E)[:, None]).reshape(1, 64), (P, 64))
    valid = ((np.arange(4) * P)[None, :] + p[:, None] < T)
    tokid = (np.arange(4) * P)[None, :] + p[:, None]
    parts = [("ident", ident), ("pm", pm), ("ones", np.ones((P, P))), ("negones", -np.ones((P, P))),
             ("mean", np.full((P, P), 1.0 / D)),
             ("negtri", negtri), ("newtri", newtri), ("cmask", cmask), ("smask", smask), ("dist", dist),
             ("negslope", negslope), ("bmask", bmask), ("tris", tri_strict), ("iota", iota), ("first", first),
             ("valid", valid), ("tokid", tokid), ("tok2", 2 * tokid - OOB)]
    off, cols, at = {}, [], 0
    for name, a in parts:
        a = np.asarray(a, f).reshape(P, -1)
        off[name] = (at, a.shape[1])
        cols.append(a)
        at += a.shape[1]
    return np.concatenate(cols, axis=1), off, sel.reshape(64, -1)


_TABLES, TO, _SEL = shape_tables()
NTAB = _TABLES.shape[1]
NTAB_ATT = TO["tris"][0]


def unit_plan():
    units = []
    for l in range(DEPTH):
        for kind in ("fox", "swa"):
            for pr in range(NPAIR):
                for h2 in range(2):
                    tiles = [(0, 128, 128), (128, 128, 256), (256, 16, 272)] if kind == "fox" else \
                            [(0, 80, 80), (80, 128, 208)]
                    for q0, rows, keys in tiles:
                        units.append(dict(l=l, kind=kind, pr=pr, what="prompt", h2=h2, q0=q0, rows=rows, keys=keys,
                                          d0=DA if q0 == 0 else DB))
                if kind == "swa":
                    units.append(dict(l=l, kind=kind, pr=pr, what="both", h2=0, q0=208, rows=128, keys=TP, d0=DC))
                for s in range(2):
                    units.append(dict(l=l, kind=kind, pr=pr, what="sample", h2=0, s=s, rows=128,
                                      keys=384 if kind == "fox" else 256, d0=DS + 256 * s))
                units[-1]["last"] = True
    g = 0
    for n, u in enumerate(units):
        u["n"], u["g"] = n, g
        g += u.get("last", False)
    return units


UNITS = unit_plan()
NU = len(UNITS) // DEPTH
NG = 2 * NPAIR
NCOL = NPAIR * 3 + 1


COLS = [0, 4, 1, 5, 2, 6, 3, 7, 8, 9, 10, 11, 12]
LOOP0, LOOP1 = RING, 3 * RING
OUTS_PER_LAYER = 17
SQ_PER_LAYER = 2 * KD + NCOL


def ring_plan():
    order = []
    for l in range(DEPTH):
        order += [(("vf", l, half), ("vproj_ready", 8 * (l + 1))) for half in range(2)]
        order += [(("qk", l, pr), ("col_ready", l * NCOL + 2 * pr + 2)) for pr in range(NPAIR)]
        order += [(("kb", l), ("col_ready", l * NCOL + 2 * NPAIR + 1))]
        order += [(("qb", l, j), ("col_ready", l * NCOL + 2 * NPAIR + 2 + j)) for j in range(NPAIR)]
        order += [(("wo", l, m), ("wo_done", l * KD + 2 * m + 2)) for m in range(4)]
        order += [None] * (-len(order) % RING)
        if l % 2 == 0:
            order += [(("gu", c), ("gu_done", 2 * c + 2)) for c in range(FCH)]
            order += [(("wd", m), ("down_done", m + 1)) for m in range(KD)]
    order += [(("me", x), None) for x in range(RING)]
    place, count, holds = {}, [0] * RING, [None] * RING
    for i, item in enumerate(order):
        if item:
            s = i % RING
            place[item[0]] = (s, count[s], holds[s])
            count[s] += 1
            holds[s] = item[1]
    return place


PLACE = ring_plan()


def build(nc, xT, params, w_vf, w_qk, w_kb, w_qb, w_o, w_gu, w_d, we_g, we_u, we_d, w_r, ck_fox, cv_fox, clf,
          ck_swa, cv_swa, tables, selt, o_kfox, o_vfox, o_lf, o_kswa, o_vswa, o_y):
    with ExitStack() as ctx:
        def sb(name, shape, dt=F32):
            return ctx.enter_context(nc.sbuf_tensor(name, shape, dt))

        def sem(name):
            return ctx.enter_context(nc.semaphore(name))

        bank = [ctx.enter_context(nc.psum_tensor(f"bank{i}", [P, 512], F32)) for i in range(8)]
        c_rows = nc.dram_tensor("c_rows", [T, D], F32).ap()
        y_rows = nc.dram_tensor("y_rows", [2 * T, D], F32).ap()

        hT = sb("hT", [P, KD, T])
        aT = sb("aT", [P, KD, T])
        ring = sb("ring", [P, RING, SLOT])
        tab = sb("tab", [P, NTAB])
        selb = sb("selb", [64, NPAIR, 4, P])
        par = sb("par", [P, NPAR])
        gq = sb("gq", [P, 2])
        nsink = sb("nsink", [P, 16])
        big = sb("big", [P, 13440])
        sq = sb("sq", [P, 2, T])
        rt = sb("rt", [P, 2, T])
        rs = sb("rs", [P, 2, T])
        prob = sb("prob", [P, 2, 384])
        probT = sb("probT", [P, 2, 384])
        small = sb("small", [P, 32])
        eps_col = sb("eps_col", [P, 1])
        lf = sb("lf", [P, 4, H])
        lz = sb("lz", [P, 4, H])
        le = sb("le", [P, 4, H])

        def view(t, o, *shape):
            n = int(np.prod(shape))
            v = t[:, o:o + n]
            if len(shape) == 2:
                v = v.rearrange("p (a b) -> p a b", a=shape[0])
            if len(shape) == 3:
                v = v.rearrange("p (a b c) -> p a b c", a=shape[0], b=shape[1])
            return v, o + n

        qk, _o1 = view(big, 0, NCOL, T)
        qbd, _o1 = view(big, _o1, 8, 256)
        v_tok, _o1 = view(big, _o1, 4, 512)
        vb_tok, _o1 = view(big, _o1, 4, P)
        NFp, _o1 = view(big, _o1, TP)
        NFs, _o1 = view(big, _o1, 384)
        clf_sb, _o1 = view(big, _o1, 2, 64)
        lbd, _o1 = view(big, _o1, 64)
        assert _o1 <= 13440, _o1
        kc = sb("kc", [P, 2048])
        vc = sb("vc", [P, 2048])
        ksw = sb("ksw", [P, 1024])
        vsw = sb("vsw", [P, 1024])
        hid, _o2 = view(big, 0, FCH, T)
        assert _o2 <= 13440
        xg, _o3 = view(big, 0, D)
        xgT, _o3 = view(big, _o3, KD, P)
        sg, _o3 = view(big, _o3, 2, MB)
        mh, _o3 = view(big, _o3, MFF)
        mhT, _o3 = view(big, _o3, MCH, P)
        yev, _o3 = view(big, _o3, D)
        ctk, _o3 = view(big, _o3, 2, D)
        onehot, _o3 = view(big, _o3, 2, 512)
        cmp1, _o3 = view(big, _o3, 4, 64)
        cmp2, _o3 = view(big, _o3, 4, 64)
        assert _o3 <= 13440, _o3
        y12 = big[:, 0:4 * D].rearrange("p (a b) -> p a b", a=2)
        yo = big[:, 4 * D:6 * D].rearrange("p (a b) -> p a b", a=2)
        wr = sb("wr", [P, KD, E])
        lg = sb("lg", [P, 4, E])
        rank = sb("rank", [P, 4, E])
        gate = sb("gate", [P, 4, E])
        mem = sb("mem", [P, 4, E])
        memv = sb("memv", [P, 4, E])
        sel1 = sb("sel1", [P, 4, E])
        sel2 = sb("sel2", [P, 4, E])
        posm = sb("posm", [P, 4, E])
        tmp8 = sb("tmp8", [P, 4, E])
        rden = sb("rden", [P, 8])
        gcol = sb("gcol", [P, 8])
        dstv = sb("dstv", [P, 4, E])
        slot_tok = sb("slot_tok", [P, 2 * E], U32)
        gidx = sb("gidx", [P, 1], U32)
        didx = sb("didx", [P, 1], U32)
        cnt = sb("cnt", [1, 8])
        cnt_i = sb("cnt_i", [1, 2], I32)

        def table(name, *dims):
            o, n = TO[name]
            v = tab[:, o:o + n]
            if len(dims) == 2:
                v = v.rearrange("p (a b) -> p a b", a=dims[0])
            return v

        ident, pm, ones, negones, mean = (table(x) for x in ("ident", "pm", "ones", "negones", "mean"))
        negtri = table("negtri", 3, TP)
        newtri, cmask = table("newtri"), table("cmask")
        smask = table("smask", 2, P)
        dist = table("dist")
        negslope = table("negslope", NPAIR, 4)
        bmask, tris, iota = table("bmask"), table("tris"), table("iota")
        first, valid, tokid, tok2 = table("first"), table("valid"), table("tokid"), table("tok2")

        slot_full = [sem(f"slot_full{i}") for i in range(RING)]
        x_loaded, tab_loaded = sem("x_loaded"), sem("tab_loaded")
        pool_passed = sem("pool_passed")
        tab2_loaded, eps_ready, lz_zeroed = sem("tab2_loaded"), sem("eps_ready"), sem("lz_zeroed")
        kc_loaded, vc_loaded, clf_loaded = sem("kc_loaded"), sem("vc_loaded"), sem("clf_loaded")
        va_copied, vb_copied, pe_in, pe_exp = sem("va_copied"), sem("vb_copied"), sem("pe_in"), sem("pe_exp")
        ctka_copied, ctkb_copied = sem("ctka_copied"), sem("ctkb_copied")
        par_loaded = sem("par_loaded")
        swc_loaded = sem("swc_loaded")
        gains_ready = sem("gains_ready")
        sq_ready, sq_used = sem("sq_ready"), sem("sq_used")
        ms_ready, root_ready, recip_ready, a_ready = sem("ms_ready"), sem("root_ready"), sem("recip_ready"), sem("a_ready")
        vproj_ready, v_copied = sem("vproj_ready"), sem("v_copied")
        z_ready, za_ready, ze_ready, zl_ready, logf_ready = (sem(x) for x in (
            "z_ready", "za_ready", "ze_ready", "zl_ready", "logf_ready"))
        lbd_ready, nf_done, nf_copied = sem("lbd_ready"), sem("nf_done"), sem("nf_copied")
        col_ready, colsq_ready, colms_ready, colroot_ready, colrecip_ready, col_done = (sem(x) for x in (
            "col_ready", "colsq_ready", "colms_ready", "colroot_ready", "colrecip_ready", "col_done"))
        qbd_zeroed, qbd_ready = sem("qbd_zeroed"), sem("qbd_ready")
        out_done = sem("out_done")
        scores_ready, biased, max_ready, negmax_ready = (sem(x) for x in (
            "scores_ready", "biased", "max_ready", "negmax_ready"))
        exp_ready, den_ready, recipd_ready, norm_ready = (sem(x) for x in (
            "exp_ready", "den_ready", "recipd_ready", "norm_ready"))
        probT_done, probT_copied, av_done, y_copied = (sem(x) for x in (
            "probT_done", "probT_copied", "av_done", "y_copied"))
        wo_done, h_added = sem("wo_done"), sem("h_added")
        gu_done, silu_ready, hid_ready = sem("gu_done"), sem("silu_ready"), sem("hid_ready")
        down_done, h_added2 = sem("down_done"), sem("h_added2")
        ctT_done, ctk_copied, ctk_stored = sem("ctT_done"), sem("ctk_copied"), [sem("ctk_stored0"), sem("ctk_stored1")]
        logits_done, memv_ready, pos_done, route = sem("logits_done"), sem("memv_ready"), sem("pos_done"), sem("route")
        cnt_ready = sem("cnt_ready")
        oneh_ready, oneh_used, sidx_ready = sem("oneh_ready"), sem("oneh_used"), sem("sidx_ready")
        iota_ready = sem("iota_ready")
        gidx_ready, didx_ready, xg_loaded, xgT_done, xgT_copied = (sem(x) for x in ("gidx_ready", "didx_ready", "xg_loaded", "xgT_done", "xgT_copied"))
        mgu_done, msilu_ready, mh_ready, mhT_done, mhT_copied = (sem(x) for x in (
            "mgu_done", "msilu_ready", "mh_ready", "mhT_done", "mhT_copied"))
        my_done, my_copied, my_stored = sem("my_done"), sem("my_copied"), sem("my_stored")
        y12_loaded, hT_done, y_half, y_ready, y_out = (
            [sem("y12_loaded0"), sem("y12_loaded1")], sem("hT_done"), sem("y_half"), sem("y_ready"), [sem("y_out0"), sem("y_out1")])

        block = ctx.enter_context(nc.Block())
        first_swa_unit = {l: min(u["n"] for u in UNITS if u["l"] == l and u["kind"] == "swa") for l in range(DEPTH)}
        last_unit = {l: max(u["n"] for u in UNITS if u["l"] == l) for l in range(DEPTH)}
        last_of_g = {u["g"]: u["n"] for u in UNITS if u.get("last")}

        def sink_col(u, t=None):
            x = 4 * u["pr"] + (2 if u["what"] == "both" else 3 if u["what"] == "sample" else u["h2"])
            if t is None:
                return par[0:u["rows"], PC["sink"] + x:PC["sink"] + x + 1]
            return t[0:u["rows"], x:x + 1]

        def nsink_col(u):
            return sink_col(u, nsink)

        groups = [[0, 1], [2, 3, 4], [5, 6, 7], [8, 9, 10]]

        def slot(s, o, n, a):
            return ring[:, s, o:o + n].rearrange("p (a b) -> p a b", a=a)

        done = {"vproj_ready": vproj_ready, "col_ready": col_ready, "wo_done": wo_done, "gu_done": gu_done,
                "down_done": down_done}

        @block.sync
        def _(sp):
            sp.dma_start(tab[:, 0:NTAB_ATT], tables[:, 0:NTAB_ATT]).then_inc(tab_loaded, 16)
            for k in range(KD):
                sp.dma_start(hT[:, k, :], xT[:, k, :]).then_inc(x_loaded, 16)

            def load(name, src, width):
                s, _, user = PLACE[name]
                if user:
                    sp.wait_ge(done[user[0]], user[1])
                sp.dma_start(ring[:, s, 0:width], src).then_inc(slot_full[s], 16)

            for l in range(DEPTH):
                for half in range(2):
                    load(("vf", l, half), w_vf[l, half], 4 * 648)
                for pr in range(NPAIR):
                    load(("qk", l, pr), w_qk[l, pr], 2048)
                if l == 0:
                    sp.dma_start(tab[:, NTAB_ATT:NTAB], tables[:, NTAB_ATT:NTAB]).then_inc(tab2_loaded, 16)
                    sp.dma_start(selb[:, :, :, :].rearrange("p a b c -> p (a b c)"), selt[:, :]).then_inc(tab2_loaded, 16)
                    sp.dma_start(wr[:, :, :].rearrange("p k e -> p (k e)"), w_r[:, :]).then_inc(tab2_loaded, 16)
                load(("kb", l), w_kb[l], 1024)
                for j in range(NPAIR):
                    load(("qb", l, j), w_qb[l, j], 1024)
                for m in range(4):
                    load(("wo", l, m), w_o[l, m], 2048)
                if l == 0:
                    for c in range(LOOP0):
                        load(("gu", c), w_gu[c], 2048)
                    with sp.Fori(0, (LOOP1 - LOOP0) // RING) as i:
                        for s in range(RING):
                            sp.wait_ge(gu_done, (i * RING + s) * 2 + 2)
                            sp.dma_start(ring[:, s, 0:2048], w_gu[bass.ds(i * RING + (LOOP0 + s), 1)].rearrange(
                                "o p n -> (o p) n")).then_inc(slot_full[s], 16)
                    for c in range(LOOP1, FCH):
                        load(("gu", c), w_gu[c], 2048)
                    for m in range(KD):
                        load(("wd", m), w_d[m], SLOT)

            def load_expert(e, x):
                w = we_d if x >= 8 else (we_u if x % 2 else we_g)
                b = x - 8 if x >= 8 else x // 2
                sp.dma_start(ring[:, x % RING, :], w[bass.ds(e * MBLK + b, 1)].rearrange(
                    "o p n -> (o p) n")).then_inc(slot_full[x % RING], 16)

            for x in range(RING):
                s, _, user = PLACE[("me", x)]
                sp.wait_ge(done[user[0]], user[1])
                sp.dma_start(ring[:, s, :], (we_u if x % 2 else we_g)[x // 2]).then_inc(slot_full[s], 16)

            def next_expert(e, n):
                for x in range(RING):
                    if x + RING < 8:
                        sp.wait_ge(mgu_done, n * 8 - 8 + (x + RING + 1))
                    else:
                        sp.wait_ge(my_done, n * 4 - 4 + (x + RING - 7))
                    load_expert(e, x)

            def second_half(e, n):
                for x in range(RING, 2 * RING):
                    sp.wait_ge(mgu_done, n * 8 + (x - RING + 1))
                    load_expert(e, x)

            sp.wait_ge(cnt_ready, 1)
            most = sp.value_load(cnt_i[0:1, 0:1], min_val=0, max_val=T)
            with sp.Fori(0, MAXR) as r:
                with sp.If(most > r * P):
                    with sp.Fori(0, E - 1) as e:
                        second_half(e, r * E + e)
                        next_expert(e + 1, r * E + e + 1)
                    second_half(E - 1, r * E + (E - 1))
                    with sp.If(most > r * P + P):
                        next_expert(0, r * E + E)

        def store_y(eng, i):
            t0, r = TT[i]
            eng.wait_ge(y_ready, i + 1)
            eng.dma_start(o_y[t0:t0 + r, :], yo[0:r, i % 2, :]).then_inc(y_out[i % 2], 16)

        @block.gpsimd
        def _(pool):
            for l in range(DEPTH):
                if l:
                    pool.wait_ge(h_added2, KD * l)
                pool.dma_start(par[:, :], params[l]).then_inc(par_loaded, 16)
                nc.gpsimd.memset(big[:, NCOL * T:NCOL * T + 2048], 0.0).then_inc(qbd_zeroed, 1)
                pool.dma_start(clf_sb.rearrange("p c n -> p (c n)"), clf[l]).then_inc(clf_loaded, 16)
                pool.dma_start(ksw[:, :], ck_swa[l]).then_inc(swc_loaded, 16)
                pool.dma_start(vsw[:, :], cv_swa[l]).then_inc(swc_loaded, 16)
                pool.dma_start(kc[:, :], ck_fox[l, 0]).then_inc(kc_loaded, 16)
                pool.dma_start(vc[:, :], cv_fox[l, 0]).then_inc(vc_loaded, 16)
                pool.wait_ge(va_copied, 4 * (l + 1))
                pool.wait_ge(vb_copied, 4 * (l + 1))
                for i, (t0, r) in enumerate(QT):
                    pool.dma_start(o_vfox[l, t0:t0 + r, :], v_tok[0:r, i, :]).then_inc(out_done, 16)
                    pool.dma_start(o_vswa[l, t0:t0 + r, :], vb_tok[0:r, i, :]).then_inc(out_done, 16)
                pool.wait_ge(logf_ready, l + 1)
                for i, (t0, r) in enumerate(QT):
                    pool.dma_start(o_lf[l, t0:t0 + r, :], lf[0:r, i, :]).then_inc(out_done, 16)
                pool.wait_ge(qbd_zeroed, l + 1)
                for x, c in enumerate(COLS):
                    pool.wait_ge(col_done, l * NCOL + x + 1)
                    if c < 4 or c > 8:
                        dst = qbd[:, c if c < 4 else c - 5, :].rearrange("p (b h q) -> p b h q", b=BS, h=2)
                        for h2 in range(2):
                            last = nc.gpsimd.tensor_copy(
                                dst[64 * h2:64 * h2 + 64, :, h2, :],
                                qk[64 * h2:64 * h2 + 64, c, TP:T].rearrange("p (b q) -> p b q", b=BS))
                        last.then_inc(qbd_ready, 1)
                    elif c < 8:
                        pool.dma_start(o_kfox[l, c - 4], qk[:, c, :]).then_inc(out_done, 16)
                    else:
                        pool.dma_start(o_kswa[l], qk[:, c, :]).then_inc(out_done, 16)
                pool.wait_ge(qbd_ready, 8 * (l + 1))
                for u in UNITS[l * NU:(l + 1) * NU]:
                    n, rows, keys = u["n"], u["rows"], u["keys"]
                    prev = last_of_g.get(u["g"] - 1)
                    if u["kind"] == "fox" and u["pr"] and n == prev + 1:
                        pool.wait_ge(scores_ready, prev + 1)
                        pool.dma_start(kc[:, :], ck_fox[l, u["pr"]]).then_inc(kc_loaded, 16)
                    if u["kind"] == "fox" and u["pr"] and n == prev + 4:
                        pool.wait_ge(av_done, prev + 1)
                        pool.dma_start(vc[:, :], cv_fox[l, u["pr"]]).then_inc(vc_loaded, 16)
                    pool.wait_ge(recipd_ready, n + 1)
                    nc.gpsimd.tensor_scalar(prob[0:rows, n % 2, 0:keys], prob[0:rows, n % 2, 0:keys],
                                            small[0:rows, 12 + n % 4:13 + n % 4], None, ALU.mult).then_inc(norm_ready, 1)
            for i, (t0, r) in enumerate(TT):
                pool.wait_ge(ctka_copied, i + 1)
                pool.wait_ge(ctkb_copied, i + 1)
                pool.dma_start(c_rows[t0:t0 + r, :], ctk[0:r, i % 2, :]).then_inc(ctk_stored[i % 2], 16)
            for i in range(2):
                pool.wait_ge(ctk_stored[i], 32)
            pool.wait_ge(cnt_ready, 1)
            most = pool.value_load(cnt_i[0:1, 0:1], min_val=0, max_val=T)

            def store_rows(e, n):
                pool.wait_ge(my_copied, n * 2 + 2)
                pool.sem_inc(pool_passed, 1)
                nc.gpsimd.tensor_copy(didx[:, 0:1], slot_tok[:, bass.ds(e + E, 1)]).then_inc(didx_ready, 1)
                pool.wait_ge(didx_ready, n + 1)
                pool.sem_inc(pool_passed, 1)
                nc.gpsimd.indirect_dma_start(
                    out=y_rows[:, :], out_offset=bass.IndirectOffsetOnAxis(ap=didx[:, 0:1], axis=0), in_=yev[:, :],
                    in_offset=None, bounds_check=2 * T - 1, oob_is_err=False).then_inc(my_stored, 16)

            def gather(e, n):
                pool.wait_ge(xgT_done, n * 2)
                pool.sem_inc(pool_passed, 1)
                nc.gpsimd.tensor_copy(gidx[:, 0:1], slot_tok[:, bass.ds(e, 1)]).then_inc(gidx_ready, 1)
                pool.wait_ge(gidx_ready, n + 1)
                pool.sem_inc(pool_passed, 1)
                nc.gpsimd.indirect_dma_start(
                    out=xg[:, :], out_offset=None, in_=c_rows[:, :],
                    in_offset=bass.IndirectOffsetOnAxis(ap=gidx[:, 0:1], axis=0)).then_inc(xg_loaded, 16)

            with pool.Fori(0, MAXR) as r:
                with pool.If(most > r * P):
                    pool.wait_ge(sidx_ready, r + 1)
                    gather(0, r * E)
                    with pool.Fori(1, E) as e:
                        gather(e, r * E + e)
                        store_rows(e - 1, r * E + e - 1)
                    store_rows(E - 1, r * E + (E - 1))
                    pool.wait_ge(my_stored, (r * E + E) * 16)
            for i, (t0, r) in enumerate(TT):
                if i >= 2:
                    pool.wait_ge(y_ready, i - 1)
                pool.dma_start(y12[0:r, i % 2, :], y_rows[2 * t0:2 * t0 + 2 * r, :].rearrange("(t w) d -> t (w d)", w=2)
                               ).then_inc(y12_loaded[i % 2], 16)
                if i >= 1:
                    store_y(pool, i - 1)
            store_y(pool, 3)
            for i in range(2):
                pool.wait_ge(y_out[i], 32)
            pool.wait_ge(out_done, 16 * DEPTH * OUTS_PER_LAYER)

        @block.tensor
        def _(pe):
            mm = nc.tensor.matmul

            def full(name):
                s, c, _ = PLACE[name]
                pe.wait_ge(slot_full[s], 16 * (c + 1))
                return s

            def norm(l, w):
                for k in range(KD):
                    i = l * SQ_PER_LAYER + (KD + NCOL) * w + k
                    pe.wait_ge(sq_ready, i + 1)
                    mm(bank[2][:, 0:T], mean, sq[:, i % 2, :], start=(k == 0), stop=(k == KD - 1)).then_inc(sq_used, 1)

            def dense_chunk(s, par2, waits):
                for w in range(2):
                    out = bank[2 * par2 + w]
                    for k in range(KD):
                        last = mm(out[:, 0:T], slot(s, w * 1024, 1024, KD)[:, k, :], aT[:, k, :],
                                  start=(k == 0), stop=(k == KD - 1))
                    last.then_inc(gu_done, 1)

            def scores(u):
                n, l, pr, rows, keys = u["n"], u["l"], u["pr"], u["rows"], u["keys"]
                S = bank[4 + n % 3]
                fox = u["kind"] == "fox"
                qc, kk = (pr, 4 + pr) if fox else (9 + pr, 8)
                if n % NU >= 3:
                    pe.wait_ge(exp_ready, n - 2)
                if u["what"] == "prompt":
                    h0, q0 = 64 * u["h2"], u["q0"]
                    if fox:
                        mm(S[0:rows, 0:keys], selb[0:H, pr, 2 + u["h2"], 0:rows], NFp[0:H, 0:keys], start=True, stop=False)
                    last = mm(S[0:rows, 0:keys], qk[h0:h0 + 64, qc, q0:q0 + rows], qk[h0:h0 + 64, kk, 0:keys],
                              start=not fox, stop=True)
                elif u["what"] == "both":
                    for h2 in range(2):
                        h0 = 64 * h2
                        last = mm(S[h0:h0 + 64, 0:keys], qk[h0:h0 + 64, qc, 208:TP], qk[h0:h0 + 64, kk, 0:keys],
                                  start=True, stop=True)
                else:
                    s = u["s"]
                    past = PAST if fox else 128
                    d = pr if fox else 4 + pr
                    if fox:
                        pe.wait_ge(kc_loaded, 16 * (l * NPAIR + pr + 1))
                        mm(S[:, 0:keys], selb[:, pr, s, :], NFs[0:64, 0:keys], start=True, stop=False)
                    else:
                        pe.wait_ge(swc_loaded, 32 * (l + 1))
                    pe.wait_ge(qbd_ready, l * 8 + d + 1)
                    mm(S[:, past:past + P], qbd[:, d, 128 * s:128 * s + 128], qk[:, kk, TP:T], start=not fox, stop=not fox)
                    for b4 in range(4):
                        b = 4 * s + b4
                        keysT = kc[:, 256 * b:256 * b + 256] if fox else ksw[:, 128 * b:128 * b + 128]
                        last = mm(S[32 * b4:32 * b4 + 32, 0:past], qbd[:, d, 32 * b:32 * b + 32], keysT,
                                  start=not fox, stop=True, tile_position=(0, 32 * b4))
                last.then_inc(scores_ready, 1)

            def transposes(u):
                n, rows, keys = u["n"], u["rows"], u["keys"]
                pe.wait_ge(norm_ready, n + 1)
                if n >= 2:
                    pe.wait_ge(probT_copied, n - 1)
                PT = bank[7 if n % 2 else 3]
                for i in range(-(-keys // P)):
                    w = min(P, keys - P * i)
                    last = nc.tensor.transpose(PT[0:w, P * i:P * i + rows], prob[0:rows, n % 2, P * i:P * i + w],
                                               ident[0:rows, 0:rows])
                last.then_inc(probT_done, 1)

            def av(u):
                n, l, pr, rows, keys = u["n"], u["l"], u["pr"], u["rows"], u["keys"]
                fox = u["kind"] == "fox"
                pe.wait_ge(probT_copied, n + 1)
                if n and u["g"] != UNITS[n - 1]["g"]:
                    pe.wait_ge(y_copied, u["g"])
                pT = probT[:, n % 2, :]
                values = v_tok if fox else vb_tok
                c0 = 128 * pr if fox else 0
                if u["what"] != "sample":
                    nk = -(-keys // P)
                    for h2 in ((0, 1) if u["what"] == "both" else (u["h2"],)):
                        h0, cols, x0 = 64 * h2, rows, 0
                        if u["what"] == "both":
                            cols, x0 = 64, 64 * h2
                        for i in range(nk):
                            w = min(P, keys - P * i)
                            last = mm(bank[0][h0:h0 + 64, u["q0"]:u["q0"] + cols],
                                      values[0:w, i, c0 + h0:c0 + h0 + 64], pT[0:w, P * i + x0:P * i + x0 + cols],
                                      start=(i == 0), stop=(i == nk - 1))
                else:
                    s = u["s"]
                    nk = 3 if fox else 2
                    if fox:
                        pe.wait_ge(vc_loaded, 16 * (l * NPAIR + pr + 1))
                    mm(bank[1][:, 128 * s:128 * s + 128], values[:, 3, c0:c0 + 128], pT[:, P * (nk - 1):P * nk],
                       start=True, stop=False)
                    for b4 in range(4):
                        b = 4 * s + b4
                        for i in range(nk - 1):
                            vals = vc[:, (2 * b + i) * 128:(2 * b + i) * 128 + 128] if fox else vsw[:, 128 * b:128 * b + 128]
                            last = mm(bank[1][:, 32 * b:32 * b + 32], vals, pT[:, P * i + 32 * b4:P * i + 32 * b4 + 32],
                                      start=False, stop=(b4 == 3 and i == nk - 2))
                last.then_inc(av_done, 1)

            pe.wait_ge(tab_loaded, 16)
            for l in range(DEPTH):
                norm(l, 0)
                s0, s1 = full(("vf", l, 0)), full(("vf", l, 1))
                pe.wait_ge(a_ready, 2 * l * KD + KD)
                for i, (t0, r) in enumerate(QT):
                    for w, (c0, c1) in enumerate(((0, 512), (512, 648))):
                        if i >= 2:
                            pe.wait_ge(vb_copied if w else va_copied, 4 * l + i - 1)
                        for k in range(KD):
                            last = mm(bank[4 + i % 2 + 2 * w][0:r, 0:c1 - c0], aT[:, k, t0:t0 + r],
                                      slot(s1 if k >= 4 else s0, 0, 4 * 648, 4)[:, k % 4, c0:c1],
                                      start=(k == 0), stop=(k == KD - 1))
                        last.then_inc(vproj_ready, 1)

                def head_mean(x):
                    i = l * SQ_PER_LAYER + KD + x
                    pe.wait_ge(sq_ready, i + 1)
                    if x >= 2:
                        pe.wait_ge(colroot_ready, l * NCOL + x - 1)
                    mm(bank[2 + x % 2][:, 0:T], pm, sq[:, i % 2, :], start=True, stop=True).then_inc(sq_used, 1)

                for x, c in enumerate(COLS):
                    if c < 8:
                        s, o = full(("qk", l, x // 2)), 1024 * (x % 2)
                    else:
                        s, o = full(("kb", l) if c == 8 else ("qb", l, c - 9)), 0
                    if x >= 2:
                        pe.wait_ge(col_done, l * NCOL + x - 1)
                    for k in range(KD):
                        last = mm(bank[x % 2][:, 0:T], slot(s, o, 1024, KD)[:, k, :], aT[:, k, :],
                                  start=(k == 0), stop=(k == KD - 1))
                    last.then_inc(col_ready, 1)
                    if x:
                        head_mean(x - 1)
                head_mean(NCOL - 1)
                pe.wait_ge(logf_ready, l + 1)
                pe.wait_ge(va_copied, 4 * (l + 1))
                for i, (t0, r) in enumerate(QT[:3]):
                    last = mm(bank[4][0:H, 0:TP], lf[0:r, i, :], negtri[0:r, i, :], start=(i == 0), stop=(i == 2))
                last.then_inc(nf_done, 1)
                pe.wait_ge(clf_loaded, 16 * (l + 1))
                pe.wait_ge(lbd_ready, l + 1)
                for c in range(2):
                    mm(bank[5][0:64, 0:PAST], clf_sb[:, c, :], negtri[:, c, 0:PAST], start=(c == 0), stop=(c == 1))
                for c in range(2):
                    mm(bank[5][0:64, PAST:384], clf_sb[:, c, :], negones, start=(c == 0), stop=False)
                mm(bank[5][0:64, PAST:384], lbd, newtri, start=False, stop=True).then_inc(nf_done, 1)

                if l == 0:
                    pe.wait_ge(tab2_loaded, 48)
                pe.wait_ge(nf_copied, 2 * (l + 1))
                pe.wait_ge(col_done, (l + 1) * NCOL)
                units = UNITS[l * NU:(l + 1) * NU]
                for i in range(NU + 3):
                    if i < NU:
                        scores(units[i])
                    if 2 <= i < NU + 2:
                        transposes(units[i - 2])
                    if i >= 3:
                        av(units[i - 3])

                pe.wait_ge(y_copied, (l + 1) * NG)
                for m in range(KD):
                    s = full(("wo", l, m // 2))
                    if m >= 2:
                        pe.wait_ge(h_added, l * KD + m - 1)
                    for k in range(KD):
                        last = mm(bank[m % 2][:, 0:T], slot(s, 1024 * (m % 2), 1024, KD)[:, k, :], aT[:, k, :],
                                  start=(k == 0), stop=(k == KD - 1))
                    last.then_inc(wo_done, 1)
                norm(l, 1)
                pe.wait_ge(a_ready, 2 * (l + 1) * KD)
                if l % 2 == 0:
                    for c in range(LOOP0):
                        s = full(("gu", c))
                        if c >= 2:
                            pe.wait_ge(hid_ready, c - 1)
                        dense_chunk(s, c % 2, None)
                    with pe.Fori(0, (LOOP1 - LOOP0) // RING) as i:
                        for s in range(RING):
                            pe.wait_ge(slot_full[s], i * 16 + 16 * (PLACE[("gu", s)][1] + 2))
                            pe.wait_ge(hid_ready, i * RING + (LOOP0 + s - 1))
                            dense_chunk(s, s % 2, None)
                    for c in range(LOOP1, FCH):
                        s = c % RING
                        pe.wait_ge(slot_full[s], 16 * (PLACE[("gu", c)][1] + 1))
                        pe.wait_ge(hid_ready, c - 1)
                        dense_chunk(s, c % 2, None)
                    pe.wait_ge(hid_ready, FCH)
                    for m in range(KD):
                        s = full(("wd", m))
                        if m >= 4:
                            pe.wait_ge(h_added2, m - 3)
                        for c in range(FCH):
                            last = mm(bank[4 + m % 4][:, 0:T], slot(s, 0, SLOT, FCH)[:, c, :], hid[:, c, :],
                                      start=(c == 0), stop=(c == FCH - 1))
                        last.then_inc(down_done, 1)

            for i, (t0, r) in enumerate(TT):
                for k in range(KD):
                    last = mm(bank[5][0:r, E * i:E * i + E], aT[:, k, t0:t0 + r], wr[:, k, :], start=(k == 0), stop=(k == KD - 1))
                last.then_inc(logits_done, 1)
            for i, (t0, r) in enumerate(TT):
                for hf in range(2):
                    if i >= 2:
                        pe.wait_ge(ctkb_copied if hf else ctka_copied, i - 1)
                    for k in range(4):
                        last = nc.tensor.transpose(bank[2 * (i % 2) + hf][0:r, P * k:P * k + P],
                                                   aT[:, 4 * hf + k, t0:t0 + r], ident)
                    last.then_inc(ctT_done, 1)
            pe.wait_ge(memv_ready, 1)
            for i in range(4):
                mm(bank[6][0:1, 0:E], ones[:, 0:1], memv[:, i, :], start=(i == 0), stop=(i == 3))
            for i in range(4):
                for j in range(i + 1):
                    last = mm(bank[7][:, E * i:E * i + E], tris if i == j else ones, memv[:, j, :], start=(j == 0), stop=(j == i))
            last.then_inc(pos_done, 1)
            pe.wait_ge(cnt_ready, 1)
            most = pe.value_load(cnt_i[0:1, 0:1], min_val=0, max_val=T)

            def tokens_T(n, hf):
                if hf:
                    pe.wait_ge(xgT_copied, n * 2 + 1)
                else:
                    pe.wait_ge(xg_loaded, n * 16 + 16)
                for k in range(4):
                    last = nc.tensor.transpose(bank[7][:, P * k:P * k + P], xg[:, P * (4 * hf + k):P * (4 * hf + k) + P], ident)
                last.then_inc(xgT_done, 1)

            groups = [[0, 1], [2, 3, 4], [5, 6, 7], [8, 9, 10]]
            with pe.Fori(0, MAXR) as r:
                with pe.If(most > r * P):
                    for e in range(E):
                        pe.wait_ge(oneh_ready, r * E + e + 1)
                        for w in range(2):
                            for i in range(4):
                                last = mm(bank[6][:, E * w + e:E * w + e + 1], onehot[:, e % 2, P * i:P * i + P],
                                          dstv[:, i, e:e + 1] if w else tokid[:, i:i + 1], start=(i == 0), stop=(i == 3))
                        last.then_inc(oneh_used, 1)
                    tokens_T(r * E, 0)
                    tokens_T(r * E, 1)
                    with pe.Fori(0, E) as e:
                        n = r * E + e

                        def hidden_T(j):
                            pe.wait_ge(mh_ready, n * 4 + (j + 1))
                            if j:
                                pe.wait_ge(mhT_copied, n * 4 + j)
                            for x, c in enumerate(groups[j]):
                                last = nc.tensor.transpose(bank[4][:, P * x:P * x + P], mh[:, P * c:P * c + P], ident)
                            last.then_inc(mhT_done, 1)

                        def down(m, c0, c1):
                            s = (8 + m) % RING
                            for c in range(c0, c1):
                                last = mm(bank[5 + m // 2][:, 256 * (m % 2):256 * (m % 2) + 256], mhT[:, c, :],
                                          slot(s, 0, SLOT, MCH)[:, c, :], start=(c == 0), stop=(c == MCH - 1))
                            if c1 == MCH:
                                last.then_inc(my_done, 1)

                        def loaded(x):
                            pe.wait_ge(slot_full[x % RING], (n * 2 + (PLACE[("me", x % RING)][1] + 1 + x // RING)) * 16)

                        pe.wait_ge(xgT_copied, n * 2 + 2)
                        for j in range(MBLK):
                            if j >= 2:
                                pe.wait_ge(mh_ready, n * 4 + (j - 1))
                            for w in range(2):
                                loaded(2 * j + w)
                                for k in range(KD):
                                    last = mm(bank[2 * (j % 2) + w][:, 0:MB], xgT[:, k, :],
                                              slot((2 * j + w) % RING, 0, SLOT, KD)[:, k, :], start=(k == 0), stop=(k == KD - 1))
                                last.then_inc(mgu_done, 1)
                            if j:
                                hidden_T(j - 1)
                        with pe.If(e < E - 1):
                            tokens_T(n + 1, 0)
                        pe.wait_ge(mhT_copied, n * 4 + 3)
                        pe.wait_ge(my_copied, n * 2)
                        loaded(8)
                        down(0, 0, 8)
                        hidden_T(3)
                        pe.wait_ge(mhT_copied, n * 4 + 4)
                        down(0, 8, MCH)
                        for m in range(1, 4):
                            loaded(8 + m)
                            down(m, 0, MCH)
                            if m == 1:
                                with pe.If(e < E - 1):
                                    tokens_T(n + 1, 1)
            for i, (t0, r) in enumerate(TT):
                if i >= 2:
                    pe.wait_ge(y_half, 2 * (i - 1))
                for k in range(KD):
                    last = nc.tensor.transpose(bank[2 * (i % 2) + k // 4][0:r, P * (k % 4):P * (k % 4) + P],
                                               hT[:, k, t0:t0 + r], ident)
                last.then_inc(hT_done, 1)

        @block.scalar
        def _(act):
            A = nc.scalar.activation

            def square(i, src):
                if i >= 2:
                    act.wait_ge(sq_used, i - 1)
                A(sq[:, i % 2, :], src, ACT.Square).then_inc(sq_ready, 1)

            def norm(l, w):
                for k in range(KD):
                    if w:
                        act.wait_ge(h_added, l * KD + k + 1)
                    elif l:
                        act.wait_ge(h_added2, (l - 1) * KD + k + 1)
                    square(l * SQ_PER_LAYER + (KD + NCOL) * w + k, hT[:, k, :])
                act.wait_ge(sq_used, l * SQ_PER_LAYER + (KD + NCOL) * w + KD)
                A(rt[:, 0, :], bank[2][:, 0:T], ACT.Sqrt, bias=eps_col[:, 0:1]).then_inc(root_ready, 1)

            act.wait_ge(eps_ready, 1)
            for l in range(DEPTH):
                if l == 0:
                    act.wait_ge(x_loaded, 16 * KD)
                norm(l, 0)
                if l:
                    act.wait_ge(out_done, 16 * OUTS_PER_LAYER)
                for i, (t0, r) in enumerate(QT):
                    act.wait_ge(vproj_ready, 8 * l + 2 * i + 1)
                    A(v_tok[0:r, i, :], bank[4 + i % 2][0:r, :], ACT.Copy).then_inc(va_copied, 1)
                act.wait_ge(za_ready, l + 1)
                A(le[:, :, :], le[:, :, :], ACT.Exp, scale=-1.0).then_inc(ze_ready, 1)
                act.wait_ge(ze_ready, l + 1)
                A(le[:, :, :], le[:, :, :], ACT.Ln, bias=1.0).then_inc(zl_ready, 1)

                def head_root(x):
                    act.wait_ge(sq_used, l * SQ_PER_LAYER + KD + x + 1)
                    if x >= 2:
                        act.wait_ge(colrecip_ready, l * NCOL + x - 1)
                    A(rt[:, x % 2, :], bank[2 + x % 2][:, 0:T], ACT.Sqrt, bias=eps_col[:, 0:1]).then_inc(colroot_ready, 1)

                act.wait_ge(recip_ready, 2 * l + 1)
                for x in range(NCOL):
                    act.wait_ge(col_ready, l * NCOL + x + 1)
                    square(l * SQ_PER_LAYER + KD + x, bank[x % 2][:, 0:T])
                    if x:
                        head_root(x - 1)
                head_root(NCOL - 1)

                def exps(u):
                    n, rows, keys = u["n"], u["rows"], u["keys"]
                    nm = small[0:rows, 4 + n % 4:5 + n % 4]
                    act.wait_ge(negmax_ready, n + 1)
                    if n >= 2:
                        act.wait_ge(probT_done, n - 1)
                    if u["kind"] == "swa":
                        A(small[0:rows, 16 + n % 4:17 + n % 4], sink_col(u), ACT.Exp, bias=nm)
                    A(prob[0:rows, n % 2, 0:keys], bank[4 + n % 3][0:rows, 0:keys], ACT.Exp, bias=nm,
                      accum_out=small[0:rows, 8 + n % 4:9 + n % 4]).then_inc(exp_ready, 1)

                def copy_T(u):
                    n, rows, keys = u["n"], u["rows"], u["keys"]
                    act.wait_ge(probT_done, n + 1)
                    if n >= 2:
                        act.wait_ge(av_done, n - 1)
                    PT = bank[7 if n % 2 else 3]
                    nk = keys // P
                    if nk:
                        last = A(probT[:, n % 2, 0:nk * P].rearrange("p (i w) -> p i w", i=nk)[:, :, 0:rows],
                                 PT[:, 0:nk * P].rearrange("p (i w) -> p i w", i=nk)[:, :, 0:rows], ACT.Copy)
                    if keys % P:
                        w = keys % P
                        last = A(probT[0:w, n % 2, nk * P:nk * P + rows], PT[0:w, nk * P:nk * P + rows], ACT.Copy)
                    last.then_inc(probT_copied, 1)

                units = UNITS[l * NU:(l + 1) * NU]
                for i in range(NU + 2):
                    if i < NU:
                        exps(units[i])
                    if i >= 2:
                        copy_T(units[i - 2])
                norm(l, 1)
                if l % 2 == 0:
                    def silu(par2, c):
                        act.wait_ge(gu_done, c * 2 + 1)
                        act.wait_ge(hid_ready, c - 1)
                        A(sq[:, par2, :], bank[2 * par2][:, 0:T], ACT.Silu).then_inc(silu_ready, 1)
                    for c in range(LOOP0):
                        act.wait_ge(gu_done, 2 * c + 1)
                        if c >= 2:
                            act.wait_ge(hid_ready, c - 1)
                        A(sq[:, c % 2, :], bank[2 * (c % 2)][:, 0:T], ACT.Silu).then_inc(silu_ready, 1)
                    with act.Fori(0, (LOOP1 - LOOP0) // RING) as i:
                        for s in range(RING):
                            silu(s % 2, i * RING + (LOOP0 + s))
                    for c in range(LOOP1, FCH):
                        silu(c % 2, c)
            act.wait_ge(out_done, 16 * DEPTH * OUTS_PER_LAYER)
            for i, (t0, r) in enumerate(TT):
                act.wait_ge(ctT_done, 2 * i + 1)
                if i >= 2:
                    act.wait_ge(ctk_stored[i % 2], 16 * (i // 2))
                A(ctk[0:r, i % 2, 0:512], bank[2 * (i % 2)][0:r, :], ACT.Copy).then_inc(ctka_copied, 1)
            act.wait_ge(pe_in, 1)
            A(gate[:, :, :], tmp8[:, :, :], ACT.Exp).then_inc(pe_exp, 1)
            act.wait_ge(cnt_ready, 1)
            most = act.value_load(cnt_i[0:1, 0:1], min_val=0, max_val=T)
            with act.Fori(0, MAXR) as r:
                with act.If(most > r * P):
                    def copy_xgT(n):
                        act.wait_ge(xgT_done, n * 2 + 1)
                        A(xgT[:, 0:4, :], bank[7][:, :], ACT.Copy).then_inc(xgT_copied, 1)
                    copy_xgT(r * E)
                    with act.Fori(0, E) as e:
                        n = r * E + e
                        for j in range(MBLK):
                            act.wait_ge(mgu_done, n * 8 + (2 * j + 1))
                            if j >= 2:
                                act.wait_ge(mh_ready, n * 4 + (j - 1))
                            A(sg[:, j % 2, :], bank[2 * (j % 2)][:, 0:MB], ACT.Silu).then_inc(msilu_ready, 1)
                        with act.If(e < E - 1):
                            copy_xgT(n + 1)
                        act.wait_ge(my_stored, n * 16)
                        act.wait_ge(my_done, n * 4 + 2)
                        A(yev[:, 0:512], bank[5][:, :], ACT.Copy).then_inc(my_copied, 1)

        @block.vector
        def _(dve):
            V = nc.vector
            nc.vector.memset(eps_col[:, 0:1], EPS).then_inc(eps_ready, 1)
            nc.vector.memset(lz[:, :, :], 0.0).then_inc(lz_zeroed, 1)
            nc.vector.memset(lg[:, :, :], 0.0).then_inc(lz_zeroed, 1)

            def norm(l, w):
                i = 2 * l + w
                g0 = PC["g_ffn" if w else "g_attn"]
                dve.wait_ge(root_ready, i + 1)
                V.reciprocal(rs[:, 0, :], rt[:, 0, :]).then_inc(recip_ready, 1)
                dve.wait_ge(recip_ready, i + 1)
                for k in range(KD):
                    V.scalar_tensor_tensor(aT[:, k, :], hT[:, k, :], par[:, g0 + k:g0 + k + 1], rs[:, 0, :],
                                           ALU.mult, ALU.mult).then_inc(a_ready, 1)

            for l in range(DEPTH):
                dve.wait_ge(par_loaded, 16 * (l + 1))
                for x, nm in enumerate(("qn_a", "qn_b")):
                    V.tensor_scalar(gq[:, x:x + 1], par[:, PC[nm]:PC[nm] + 1], HD ** -0.5, None, ALU.mult)
                V.tensor_scalar(nsink[:, :], par[:, PC["sink"]:PC["sink"] + 16], -1.0, None, ALU.mult).then_inc(gains_ready, 1)
                dve.wait_ge(gains_ready, l + 1)
                if l == 0:
                    dve.wait_ge(x_loaded, 16 * KD)
                norm(l, 0)
                if l:
                    dve.wait_ge(out_done, 16 * OUTS_PER_LAYER)
                if l == 0:
                    dve.wait_ge(lz_zeroed, 2)
                bf = par[:, PC["b_f"]:PC["b_f"] + H]
                for i, (t0, r) in enumerate(QT):
                    dve.wait_ge(vproj_ready, 8 * l + 2 * i + 2)
                    V.tensor_tensor(lz[0:r, i, :], bank[6 + i % 2][0:r, 128:136], bf[0:r, :], ALU.add)
                    V.tensor_copy(vb_tok[0:r, i, :], bank[6 + i % 2][0:r, 0:128]).then_inc(vb_copied, 1)
                dve.wait_ge(vb_copied, 4 * (l + 1))
                V.scalar_tensor_tensor(le[:, :, :], lz[:, :, :], -1.0, lz[:, :, :], ALU.mult, ALU.max).then_inc(za_ready, 1)
                dve.wait_ge(zl_ready, l + 1)
                V.scalar_tensor_tensor(lf[:, :, :], lz[:, :, :], 0.0, le[:, :, :], ALU.min, ALU.subtract).then_inc(logf_ready, 1)
                dve.wait_ge(logf_ready, l + 1)
                V.tensor_tensor(lbd.rearrange("p (b h) -> p b h", b=BS), bmask.rearrange("p (b h) -> p b h", b=BS),
                                lf[:, 3:4, :].to_broadcast([P, BS, H]), ALU.mult).then_inc(lbd_ready, 1)
                for x, c in enumerate(COLS):
                    i = l * NCOL + x
                    dve.wait_ge(colroot_ready, i + 1)
                    V.reciprocal(rs[:, x % 2, :], rt[:, x % 2, :]).then_inc(colrecip_ready, 1)
                    dve.wait_ge(colrecip_ready, i + 1)
                    g = (gq[:, 0:1] if c < 4 else par[:, PC["kn_a"]:PC["kn_a"] + 1] if c < 8 else
                         par[:, PC["kn_b"]:PC["kn_b"] + 1] if c == 8 else gq[:, 1:2])
                    V.scalar_tensor_tensor(qk[:, c, :], bank[x % 2][:, 0:T], g, rs[:, x % 2, :],
                                           ALU.mult, ALU.mult).then_inc(col_done, 1)
                dve.wait_ge(nf_done, 2 * l + 1)
                V.tensor_copy(NFp[0:H, :], bank[4][0:H, 0:TP]).then_inc(nf_copied, 1)
                dve.wait_ge(nf_done, 2 * l + 2)
                V.tensor_copy(NFs[0:64, :], bank[5][0:64, 0:384]).then_inc(nf_copied, 1)
                if l == 0:
                    dve.wait_ge(tab2_loaded, 48)

                def bias_max(u):
                    n, rows, keys = u["n"], u["rows"], u["keys"]
                    S = bank[4 + n % 3]
                    dve.wait_ge(scores_ready, n + 1)
                    if u["kind"] == "fox":
                        w = rows if u["what"] == "prompt" else P
                        m = cmask[0:rows, 0:w] if u["what"] == "prompt" else smask[:, u["s"], :]
                        V.tensor_tensor(S[0:rows, keys - w:keys], S[0:rows, keys - w:keys], m, ALU.add).then_inc(biased, 1)
                    else:
                        col = 2 if u["what"] == "both" else 3 if u["what"] == "sample" else u["h2"]
                        V.scalar_tensor_tensor(S[0:rows, 0:keys], dist[0:rows, u["d0"]:u["d0"] + keys],
                                               negslope[0:rows, u["pr"], col:col + 1], S[0:rows, 0:keys],
                                               ALU.mult, ALU.add).then_inc(biased, 1)
                    dve.wait_ge(biased, n + 1)
                    if u["kind"] == "fox":
                        V.tensor_reduce(small[0:rows, 4 + n % 4:5 + n % 4], S[0:rows, 0:keys], AX_X, ALU.max,
                                        negate=True).then_inc(negmax_ready, 1)
                    else:
                        V.tensor_reduce(small[0:rows, n % 4:n % 4 + 1], S[0:rows, 0:keys], AX_X, ALU.max,
                                        negate=True).then_inc(max_ready, 1)
                        dve.wait_ge(max_ready, n - (u["l"] + 1) * 8 * NPAIR + 1)
                        V.tensor_tensor(small[0:rows, 4 + n % 4:5 + n % 4], small[0:rows, n % 4:n % 4 + 1],
                                        nsink_col(u), ALU.min).then_inc(negmax_ready, 1)

                def denominator(u):
                    n, rows = u["n"], u["rows"]
                    dve.wait_ge(exp_ready, n + 1)
                    den = small[0:rows, 8 + n % 4:9 + n % 4]
                    if u["kind"] == "swa":
                        V.tensor_tensor(small[0:rows, 20 + n % 4:21 + n % 4], den, small[0:rows, 16 + n % 4:17 + n % 4],
                                        ALU.add).then_inc(den_ready, 1)
                        dve.wait_ge(den_ready, n - (u["l"] + 1) * 8 * NPAIR + 1)
                        den = small[0:rows, 20 + n % 4:21 + n % 4]
                    V.reciprocal(small[0:rows, 12 + n % 4:13 + n % 4], den).then_inc(recipd_ready, 1)

                def take_y(g):
                    dve.wait_ge(av_done, last_of_g[g] + 1)
                    k = g % NG
                    smp = bank[1][:, 0:256].rearrange("p (b h q) -> p b h q", b=BS, h=2)
                    V.tensor_copy(aT[:, k, 0:TP], bank[0][:, 0:TP])
                    for h2 in range(2):
                        last = V.tensor_copy(aT[64 * h2:64 * h2 + 64, k, TP:T].rearrange("p (b q) -> p b q", b=BS),
                                             smp[64 * h2:64 * h2 + 64, :, h2, :])
                    last.then_inc(y_copied, 1)

                units = UNITS[l * NU:(l + 1) * NU]
                taken = l * NG
                for i in range(NU + 4):
                    if i < NU:
                        bias_max(units[i])
                    if 1 <= i < NU + 1:
                        denominator(units[i - 1])
                    if taken < (l + 1) * NG and last_of_g[taken] + 3 == l * NU + i:
                        take_y(taken)
                        taken += 1
                for m in range(KD):
                    dve.wait_ge(wo_done, l * KD + m + 1)
                    V.tensor_tensor(hT[:, m, :], hT[:, m, :], bank[m % 2][:, 0:T], ALU.add).then_inc(h_added, 1)
                dve.wait_ge(h_added, (l + 1) * KD)
                norm(l, 1)
                if l % 2 == 0:
                    dve.wait_ge(out_done, 16 * OUTS_PER_LAYER)

                    def hidden(par2, c, dst):
                        dve.wait_ge(silu_ready, c + 1)
                        dve.wait_ge(gu_done, c * 2 + 2)
                        V.tensor_tensor(dst, sq[:, par2, :], bank[2 * par2 + 1][:, 0:T], ALU.mult).then_inc(hid_ready, 1)
                    for c in range(LOOP0):
                        hidden(c % 2, c, hid[:, c, :])
                    with dve.Fori(0, (LOOP1 - LOOP0) // RING) as i:
                        for s in range(RING):
                            hidden(s % 2, i * RING + (LOOP0 + s), big[:, bass.ds((i * RING + (LOOP0 + s)) * T, T)])
                    for c in range(LOOP1, FCH):
                        hidden(c % 2, c, hid[:, c, :])
                    for m in range(KD):
                        dve.wait_ge(down_done, m + 1)
                        V.tensor_tensor(hT[:, m, :], hT[:, m, :], bank[4 + m % 4][:, 0:T], ALU.add).then_inc(h_added2, 1)
                    dve.wait_ge(h_added2, KD)

            steps = [0]

            def step(ins):
                steps[0] += 1
                ins.then_inc(route, 1)
                dve.wait_ge(route, steps[0])

            def b4(ap, shape):
                return ap.to_broadcast(shape)

            dve.wait_ge(out_done, 16 * DEPTH * OUTS_PER_LAYER)
            br = par[:, PC["b_r"]:PC["b_r"] + E]
            for i, (t0, r) in enumerate(TT):
                dve.wait_ge(logits_done, len(TT))
                step(V.tensor_tensor(lg[0:r, i, :], bank[5][0:r, E * i:E * i + E], br[0:r, :], ALU.add))
            lge = lg[:, :, :].unsqueeze(3).to_broadcast([P, 4, E, E])
            lgo = lg[:, :, :].unsqueeze(2).to_broadcast([P, 4, E, E])
            c1 = cmp1[:, :, :].rearrange("p t (e o) -> p t e o", e=E)
            c2 = cmp2[:, :, :].rearrange("p t (e o) -> p t e o", e=E)
            step(V.tensor_tensor(c1, lgo, lge, ALU.is_gt))
            step(V.tensor_tensor(c2, lgo, lge, ALU.is_equal))
            step(V.tensor_tensor(cmp2[:, :, :], cmp2[:, :, :], first.unsqueeze(1).to_broadcast([P, 4, 64]), ALU.mult))
            step(V.tensor_tensor(cmp1[:, :, :], cmp1[:, :, :], cmp2[:, :, :], ALU.add))
            step(V.tensor_reduce(rank[:, :, :], c1, AX_X, ALU.add))
            step(V.tensor_scalar(mem[:, :, :], rank[:, :, :], 1.5, None, ALU.is_lt))
            V.tensor_tensor(memv[:, :, :], mem[:, :, :], valid.unsqueeze(2).to_broadcast([P, 4, E]), ALU.mult).then_inc(memv_ready, 1)
            for i, (t0, r) in enumerate(TT):
                dve.wait_ge(ctT_done, 2 * i + 2)
                if i >= 2:
                    dve.wait_ge(ctk_stored[i % 2], 16 * (i // 2))
                V.tensor_copy(ctk[0:r, i % 2, 512:1024], bank[2 * (i % 2) + 1][0:r, :]).then_inc(ctkb_copied, 1)
            step(V.tensor_scalar(sel1[:, :, :], rank[:, :, :], 0.5, None, ALU.is_lt))
            step(V.tensor_tensor(sel2[:, :, :], mem[:, :, :], sel1[:, :, :], ALU.subtract))
            step(V.tensor_reduce(rden[:, 0:4], lg[:, :, :], AX_X, ALU.max))
            V.tensor_tensor(tmp8[:, :, :], lg[:, :, :], rden[:, 0:4].unsqueeze(2).to_broadcast([P, 4, E]),
                            ALU.subtract).then_inc(pe_in, 1)
            dve.wait_ge(pe_exp, 1)
            step(V.tensor_tensor(gate[:, :, :], gate[:, :, :], mem[:, :, :], ALU.mult))
            step(V.tensor_reduce(rden[:, 0:4], gate[:, :, :], AX_X, ALU.add))
            step(V.reciprocal(rden[:, 4:8], rden[:, 0:4]))
            step(V.tensor_tensor(gate[:, :, :], gate[:, :, :], rden[:, 4:8].unsqueeze(2).to_broadcast([P, 4, E]), ALU.mult))
            for w, sel in enumerate((sel1, sel2)):
                step(V.tensor_tensor(tmp8[:, :, :], gate[:, :, :], sel[:, :, :], ALU.mult))
                step(V.tensor_reduce(gcol[:, 4 * w:4 * w + 4], tmp8[:, :, :], AX_X, ALU.add))
            dve.wait_ge(pos_done, 1)
            step(V.tensor_reduce(cnt[0:1, 0:1], bank[6][0:1, 0:E], AX_X, ALU.max))
            V.tensor_copy(cnt_i[0:1, 0:1], cnt[0:1, 0:1]).then_inc(cnt_ready, 1)
            pos = bank[7][:, 0:4 * E].rearrange("p (t e) -> p t e", t=4)
            step(V.tensor_scalar(dstv[:, :, :], rank[:, :, :], 0.5, None, ALU.is_gt))
            step(V.tensor_tensor(dstv[:, :, :], dstv[:, :, :], tok2.unsqueeze(2).to_broadcast([P, 4, E]), ALU.add))
            step(V.tensor_scalar(posm[:, :, :], memv[:, :, :], -1e6, 1e6, ALU.mult, ALU.add))
            step(V.tensor_tensor(posm[:, :, :], posm[:, :, :], pos, ALU.add))
            dve.wait_ge(cnt_ready, 1)
            most = dve.value_load(cnt_i[0:1, 0:1], min_val=0, max_val=T)
            with dve.Fori(0, MAXR) as r:
                with dve.If(most > r * P):
                    for e in range(E):
                        if e >= 2:
                            dve.wait_ge(oneh_used, r * E + (e - 1))
                        V.tensor_tensor(onehot[:, e % 2, :].rearrange("p (t s) -> p t s", t=4),
                                        iota.unsqueeze(1).to_broadcast([P, 4, P]),
                                        posm[:, :, e:e + 1].to_broadcast([P, 4, P]), ALU.is_equal).then_inc(oneh_ready, 1)
                    dve.wait_ge(oneh_ready, r * E + E)
                    V.tensor_scalar(posm[:, :, :], posm[:, :, :], -float(P), None, ALU.add).then_inc(iota_ready, 1)
                    dve.wait_ge(iota_ready, r + 1)
                    dve.wait_ge(oneh_used, r * E + E)
                    dve.wait_ge(my_stored, r * (16 * E))
                    V.tensor_copy(slot_tok[:, 0:E], bank[6][:, 0:E])
                    V.tensor_scalar(slot_tok[:, E:2 * E], bank[6][:, E:2 * E], float(OOB), None, ALU.add).then_inc(sidx_ready, 1)

                    def copy_xgT(n):
                        dve.wait_ge(xgT_done, n * 2 + 2)
                        V.tensor_copy(xgT[:, 4:8, :], bank[7][:, :].rearrange("p (k t) -> p k t", k=4)).then_inc(xgT_copied, 1)
                    copy_xgT(r * E)
                    with dve.Fori(0, E) as e:
                        n = r * E + e

                        def copy_hT(j):
                            dve.wait_ge(mhT_done, n * 4 + (j + 1))
                            c0, w = groups[j][0], len(groups[j])
                            V.tensor_copy(mhT[:, c0:c0 + w, :], bank[4][:, 0:P * w].rearrange("p (c t) -> p c t", c=w)
                                          ).then_inc(mhT_copied, 1)
                        for j in range(MBLK):
                            dve.wait_ge(msilu_ready, n * 4 + (j + 1))
                            dve.wait_ge(mgu_done, n * 8 + (2 * j + 2))
                            V.tensor_tensor(mh[:, MB * j:MB * j + MB], sg[:, j % 2, :], bank[2 * (j % 2) + 1][:, 0:MB],
                                            ALU.mult).then_inc(mh_ready, 1)
                            if j:
                                copy_hT(j - 1)
                        copy_hT(3)
                        with dve.If(e < E - 1):
                            copy_xgT(n + 1)
                        dve.wait_ge(my_stored, n * 16)
                        dve.wait_ge(my_done, n * 4 + 4)
                        V.tensor_copy(yev[:, 512:1024], bank[6][:, :]).then_inc(my_copied, 1)
            for i, (t0, r) in enumerate(TT):
                dve.wait_ge(hT_done, i + 1)
                dve.wait_ge(y12_loaded[i % 2], 16 * (i // 2 + 1))
                if i >= 2:
                    dve.wait_ge(y_out[i % 2], 16 * (i // 2))
                for hf in range(2):
                    V.scalar_tensor_tensor(yo[0:r, i % 2, 512 * hf:512 * hf + 512], y12[0:r, i % 2, 512 * hf:512 * hf + 512],
                                           gcol[0:r, i:i + 1], bank[2 * (i % 2) + hf][0:r, :], ALU.mult, ALU.add
                                           ).then_inc(y_half, 1)
                dve.wait_ge(y_half, 2 * i + 2)
                V.scalar_tensor_tensor(yo[0:r, i % 2, :], y12[0:r, i % 2, D:2 * D], gcol[0:r, 4 + i:5 + i], yo[0:r, i % 2, :],
                                       ALU.mult, ALU.add).then_inc(y_ready, 1)


def kernel(**inputs):
    import concourse.bacc as bacc
    from concourse.bass_utils import run_bass_kernel_spmd

    x = {k: np.asarray(v) for k, v in inputs.items()}
    c = np.ascontiguousarray

    def tiles(w):
        return c(w.reshape(-1, P, w.shape[-1]).transpose(1, 0, 2)).reshape(P, -1)

    A = H * HD
    tok = np.concatenate([x["meta_tokens"], x["x_prompt"][0], x["x_sample"].reshape(TSM, D)], axis=0)
    params, vf, qk, kb, qb, wo = [], [], [], [], [], []
    p = np.arange(P)
    sinks = x["sinks"]
    for l in range(DEPTH):
        w = x["w_in"][l]
        q_a, k_a, v_a, f_a, q_b, k_b, v_b = np.split(w, [A, 2 * A, 3 * A, 3 * A + H, 4 * A + H, 4 * A + H + P], axis=1)
        w648 = np.concatenate([v_a, v_b, f_a], axis=1)
        vf.append(np.stack([tiles(w648[:512]), tiles(w648[512:])]))
        qk.append(np.stack([np.concatenate([tiles(q_a[:, P * i:P * i + P]), tiles(k_a[:, P * i:P * i + P])], axis=1)
                            for i in range(NPAIR)]))
        kb.append(tiles(k_b))
        pair_cols = [np.r_[HD * j:HD * j + HD, HD * (4 + j):HD * (4 + j) + HD] for j in range(NPAIR)]
        qb.append(np.stack([tiles(q_b[:, pc]) for pc in pair_cols]))
        rows = np.concatenate([np.arange(A)] + [A + pc for pc in pair_cols])
        w_o = x["w_out"][l][rows]
        wo.append(np.stack([np.concatenate([tiles(w_o[:, P * m:P * m + P]) for m in (2 * i, 2 * i + 1)], axis=1)
                            for i in range(4)]))
        sk = np.zeros((P, NPAIR, 4), sinks.dtype)
        for j in range(NPAIR):
            sk[:, j, 0], sk[:, j, 1] = sinks[l, j], sinks[l, 4 + j]
            sk[:, j, 2] = sinks[l][np.where(p < 64, j, 4 + j)]
            sk[:, j, 3] = sinks[l][np.where((p // 16) % 2 == 0, j, 4 + j)]
        cols = [x["g_attn"][l].reshape(KD, P).T, x["g_ffn"][l].reshape(KD, P).T]
        cols += [np.tile(x[n][l], 2)[:, None] for n in ("qn_a", "kn_a", "qn_b", "kn_b")]
        cols += [np.tile(x["b_f"][l], (P, 1)), sk.reshape(P, -1), np.tile(x["b_router"][0], (P, 1))]
        params.append(np.concatenate(cols, axis=1))
    gu = np.stack([np.concatenate([tiles(x["w_gate"][0][:, P * i:P * i + P]), tiles(x["w_up"][0][:, P * i:P * i + P])], axis=1)
                   for i in range(FCH)])
    wd = np.stack([tiles(x["w_down"][0][:, P * m:P * m + P]) for m in range(KD)])

    def blocks(w, n, width):
        a = w.reshape(E, -1, P, n, width).transpose(0, 3, 2, 1, 4)
        return c(a).reshape(E * n, P, -1)

    kf, vf_c = x["cache_fox_k"], x["cache_fox_v"]
    ck = c(kf.reshape(DEPTH, BS, PAST, NPAIR, P).transpose(0, 3, 4, 1, 2)).reshape(DEPTH, NPAIR, P, -1)
    cv = c(vf_c.reshape(DEPTH, BS, 2, P, NPAIR, P).transpose(0, 4, 3, 1, 2, 5)).reshape(DEPTH, NPAIR, P, -1)
    cl = c(x["cache_fox_logf"].reshape(DEPTH, BS, 2, P, H).transpose(0, 3, 2, 1, 4)).reshape(DEPTH, P, -1)
    cks = c(x["cache_swa_k"].reshape(DEPTH, BS, P, P).transpose(0, 3, 1, 2)).reshape(DEPTH, P, -1)
    cvs = c(x["cache_swa_v"].reshape(DEPTH, BS, P, P).transpose(0, 2, 1, 3)).reshape(DEPTH, P, -1)
    arrays = {
        "xT": c(tok.T.reshape(KD, P, T).transpose(1, 0, 2)), "params": np.stack(params),
        "w_vf": np.stack(vf), "w_qk": np.stack(qk), "w_kb": np.stack(kb), "w_qb": np.stack(qb), "w_o": np.stack(wo),
        "w_gu": gu, "w_d": wd, "we_g": blocks(x["we_gate"][0], MBLK, MB), "we_u": blocks(x["we_up"][0], MBLK, MB),
        "we_d": blocks(x["we_down"][0], 4, 256), "w_r": tiles(x["w_router"][0]),
        "ck_fox": ck, "cv_fox": cv, "clf": cl, "ck_swa": cks, "cv_swa": cvs, "tables": _TABLES, "selt": _SEL,
    }
    nc = bacc.Bacc("TRN2", target_bir_lowering=False, num_devices=1)
    args = {}
    for name, a in arrays.items():
        arrays[name] = c(a)
        args[name] = nc.dram_tensor(name, a.shape, mybir.dt.from_np(a.dtype), kind="ExternalInput").ap()
    outs = {"o_kfox": (DEPTH, NPAIR, P, T), "o_vfox": (DEPTH, T, A), "o_lf": (DEPTH, T, H), "o_kswa": (DEPTH, P, T),
            "o_vswa": (DEPTH, T, P), "o_y": (T, D)}
    for name, shape in outs.items():
        args[name] = nc.dram_tensor(name, shape, F32, kind="ExternalOutput").ap()
    build(nc, **args)
    r = run_bass_kernel_spmd(nc, [arrays], core_ids=[0]).results[0]
    y = r["o_y"]
    kf = r["o_kfox"].reshape(DEPTH, H, HD, T).transpose(0, 3, 1, 2)
    vf_o = r["o_vfox"].reshape(DEPTH, T, H, HD)
    ks = r["o_kswa"].reshape(DEPTH, 2, HD, T).transpose(0, 3, 1, 2)
    vs = r["o_vswa"].reshape(DEPTH, T, 2, HD)
    lf = r["o_lf"]
    W = 128

    def prompt(a):
        return c(a[:, None, :TP])

    def sample(a):
        return c(a[:, TP:].reshape((DEPTH, BS, TSEQ) + a.shape[2:]))

    return (c(y[NMETA:TP][None]), c(y[TP:].reshape(BS, TSEQ, D)), prompt(kf), prompt(vf_o), prompt(lf),
            c(ks[:, None, TP - W:TP]), c(vs[:, None, TP - W:TP]), sample(kf), sample(vf_o), sample(lf),
            sample(ks), sample(vs))
```

```python
from contextlib import ExitStack

import numpy as np

import concourse.bass as bass
from concourse import mybir

ALU = mybir.AluOpType
ACT = mybir.ActivationFunctionType
F32 = mybir.dt.float32
F32R = mybir.dt.float32r
U32 = mybir.dt.uint32
I32 = mybir.dt.int32
AX_X = mybir.AxisListType.X

P = 128
DEPTH = 2
D = 1024
KD = D // P
HD = 64
NMETA, SEQ = 16, 256
TP = NMETA + SEQ
BS, TSEQ = 8, 16
TSM = BS * TSEQ
T = TP + TSM
PAST = 256
CHUNK = 64
H = 8
NPAIR = 4
FF = 2816
FCH = FF // P
E = 8
MFF = 1408
MCH = MFF // P
MBLK = 4
MB = MFF // MBLK
EPS = 1e-6
BIG = 1e33
OOB = 8192
NEG = -1e30

RAW = 4
SPL = 3
PIECE = 6 * 256
MD0 = 5

QT = [(0, 128), (128, 128), (256, 16), (TP, TSM)]
TT = [(0, 128), (128, 128), (256, 128), (384, 16)]
MAXR = -(-T // P)

PC = {}
_o = 0
for _n, _w in (("g_attn", KD), ("g_ffn", KD), ("qn_a", 1), ("kn_a", 1), ("qn_b", 1), ("kn_b", 1), ("b_f", H),
               ("sink", 16), ("b_r", E)):
    PC[_n] = _o
    _o += _w
NPAR = _o

DA, DB, DC, DS = 0, 80, 80 + 208, 80 + 208 + TP
NDIST = DS + 2 * 256


def shape_tables():
    f = np.float32
    ident = np.eye(P, dtype=f)
    pm = np.zeros((P, P), f)
    pm[:HD, :HD] = 1.0 / HD
    pm[HD:, HD:] = 1.0 / HD
    p = np.arange(P)
    t = np.arange(TP)
    negtri = np.zeros((P, 3, TP), f)
    for i in range(3):
        negtri[:, i, :] = -1.0 * ((128 * i + p)[:, None] <= t[None, :])
    b, q = p // TSEQ, p % TSEQ
    newtri = -1.0 * ((b[:, None] == b[None, :]) & (q[:, None] <= q[None, :]))
    cmask = np.where(p[None, :] > p[:, None], NEG, 0.0)
    row_b4, row_h, row_q = p // 32, (p // 16) % 2, p % 16
    smask = np.zeros((P, 2, P), f)
    dist = np.full((P, NDIST), BIG, f)
    chunk = (t + CHUNK - NMETA) // CHUNK

    def prompt_dist(rows, keys):
        ok = (chunk[keys][None] <= chunk[rows][:, None]) & (chunk[keys][None] >= chunk[rows][:, None] - 2)
        return np.where(ok, np.abs(rows[:, None] - keys[None]), BIG)
    dist[:80, DA:DA + 80] = prompt_dist(t[:80], t[:80])
    dist[:, DB:DB + 208] = prompt_dist(t[80:208], t[:208])
    dist[:, DC:DC + TP] = prompt_dist(np.concatenate([t[208:], t[208:]]), t)
    for s in range(2):
        same = (4 * s + row_b4)[:, None] == b[None, :]
        smask[:, s, :] = np.where(same & (q[None, :] <= row_q[:, None]), 0.0, NEG)
        dist[:, DS + 256 * s:DS + 256 * s + 128] = 128 + row_q[:, None] - p[None, :]
        dist[:, DS + 256 * s + 128:DS + 256 * s + 256] = np.where(same, np.abs(row_q[:, None] - q[None, :]), BIG)
    negslope = np.zeros((P, NPAIR, 4), f)
    for j in range(NPAIR):
        lo, hi = -2.0 ** -(j + 1), -2.0 ** -(j + 5)
        negslope[:, j, 0] = lo
        negslope[:, j, 1] = hi
        negslope[:, j, 2] = np.where(p < 64, lo, hi)
        negslope[:, j, 3] = np.where(row_h == 0, lo, hi)
    sel = np.zeros((64, NPAIR, 4, P), f)
    for pr in range(NPAIR):
        for s in range(2):
            sel[(4 * s + row_b4) * H + 2 * pr + row_h, pr, s, p] = 1.0
        for h2 in range(2):
            sel[2 * pr + h2, pr, 2 + h2, :] = 1.0
    bmask = (np.arange(TSM)[:, None] // TSEQ == np.arange(64)[None, :] // H).astype(f)
    tri_strict = (p[:, None] < p[None, :]).astype(f)
    iota = np.broadcast_to(p[None, :], (P, P))
    first = np.broadcast_to((np.arange(E)[None, :] < np.arange(E)[:, None]).reshape(1, 64), (P, 64))
    valid = ((np.arange(4) * P)[None, :] + p[:, None] < T)
    tokid = (np.arange(4) * P)[None, :] + p[:, None]
    parts = [("ident", ident), ("pm", pm), ("ones", np.ones((P, P))),
             ("mean", np.full((P, P), 1.0 / D)),
             ("negtri", negtri), ("newtri", newtri), ("cmask", cmask), ("smask", smask), ("dist", dist),
             ("negslope", negslope), ("bmask", bmask), ("tris", tri_strict), ("iota", iota), ("first", first),
             ("valid", valid), ("tokid", tokid), ("tok2", 2 * tokid - OOB)]
    off, cols, at = {}, [], 0
    for name, a in parts:
        a = np.asarray(a, f).reshape(P, -1)
        off[name] = (at, a.shape[1])
        cols.append(a)
        at += a.shape[1]
    return np.concatenate(cols, axis=1), off, sel.reshape(64, -1)


_TABLES, TO, _SEL = shape_tables()
NTAB = _TABLES.shape[1]
NTAB_ATT = TO["tris"][0]


def unit_plan():
    units = []
    for l in range(DEPTH):
        for kind in ("fox", "swa"):
            for pr in range(NPAIR):
                for h2 in range(2):
                    tiles = [(0, 128, 128), (128, 128, 256), (256, 16, 272)] if kind == "fox" else \
                            [(0, 80, 80), (80, 128, 208)]
                    for q0, rows, keys in tiles:
                        units.append(dict(l=l, kind=kind, pr=pr, what="prompt", h2=h2, q0=q0, rows=rows, keys=keys,
                                          d0=DA if q0 == 0 else DB))
                if kind == "swa":
                    units.append(dict(l=l, kind=kind, pr=pr, what="both", h2=0, q0=208, rows=128, keys=TP, d0=DC))
                for s in range(2):
                    units.append(dict(l=l, kind=kind, pr=pr, what="sample", h2=0, s=s, rows=128,
                                      keys=384 if kind == "fox" else 256, d0=DS + 256 * s))
                units[-1]["last"] = True
    g = 0
    for n, u in enumerate(units):
        u["n"], u["g"] = n, g
        g += u.get("last", False)
    return units


UNITS = unit_plan()
NU = len(UNITS) // DEPTH
NG = 2 * NPAIR
NCOL = NPAIR * 3 + 1


COLS = [0, 4, 1, 5, 2, 6, 3, 7, 8, 9, 10, 11, 12]
CBODY = 6
LOOP0, LOOP1 = CBODY, 3 * CBODY
OUTS_PER_LAYER = 17
SQ_PER_LAYER = 2 * KD + NCOL
LAG = 3

VWID, DWID, MGW = 2 * 648, FCH // 2 * P, KD // 2 * MB
WIDTH, AT = [], {}
for _l in range(DEPTH):
    AT["v", _l] = len(WIDTH)
    WIDTH += [VWID] * 4
    AT["col", _l] = len(WIDTH)
    WIDTH += [KD * P] * NCOL
    AT["wo", _l] = len(WIDTH)
    WIDTH += [KD * P] * KD
    if _l % 2 == 0:
        AT["gu"] = len(WIDTH)
        WIDTH += [KD * P] * (2 * FCH)
        AT["down"] = len(WIDTH)
        WIDTH += [DWID] * (2 * KD)
AT["moe"] = len(WIDTH)
MPER = 24
MWIDTH = [MGW] * 16 + [MD0 * 256, (MCH - MD0) * 256] * 4
WIDTH += MWIDTH + MWIDTH[:4]


def build(nc, xT, params, w_vf, w_col, w_o, w_gu, w_d, w_egu, w_ed0, w_ed1, w_r, ck_fox, cv_fox, clf,
          ck_swa, cv_swa, tables, selt, o_kfox, o_vfox, o_lf, o_kswa, o_vswa, o_y):
    with ExitStack() as ctx:
        def sb(name, shape, dt=F32):
            return ctx.enter_context(nc.sbuf_tensor(name, shape, dt))

        def sem(name):
            return ctx.enter_context(nc.semaphore(name))

        bank = [ctx.enter_context(nc.psum_tensor(f"bank{i}", [P, 512], F32)) for i in range(8)]
        c_rows = nc.dram_tensor("c_rows", [T, D], F32).ap()
        y_rows = nc.dram_tensor("y_rows", [2 * T, D], F32).ap()

        AREA = 2 * FCH * T
        area_at = nc.sbuf_base + (-nc.sbuf_base) % 64
        sb("area_fence", [P, AREA + 16])

        def place(name, o, shape, dt=F32):
            n = int(np.prod(shape[1:]))
            assert o + n <= AREA, (name, o + n)
            return nc.alloc_sbuf_tensor_at(name, shape, dt, offset=area_at + 4 * o), o + n

        hT = sb("hT", [P, KD, T])
        aH = sb("aH", [P, KD, T], F32R)
        aL = sb("aL", [P, KD, T], F32R)
        raw = sb("raw", [P, RAW, PIECE])
        WH = sb("WH", [P, SPL, PIECE], F32R)
        WL = sb("WL", [P, SPL, PIECE], F32R)
        tab = sb("tab", [P, NTAB])
        selb = sb("selb", [64, NPAIR, 4, P])
        par = sb("par", [P, NPAR])
        gq = sb("gq", [P, 2])
        nsink = sb("nsink", [P, 16])
        sq = sb("sq", [P, 2, T])
        rt = sb("rt", [P, 2, T])
        rs = sb("rs", [P, 2, T])
        prob = sb("prob", [P, 3, 384])
        probT = sb("probT", [P, 2, 384])
        small = sb("small", [P, 32])
        eps_col = sb("eps_col", [P, 1])
        lf = sb("lf", [P, 4, H])
        lz = sb("lz", [P, 4, H])
        le = sb("le", [P, 4, H])

        aT, _ = place("aT", 0, [P, KD, T])
        qk, _o = place("qk", 0, [P, NCOL, T])
        qbd, _o = place("qbd", _o, [P, 8, 256])
        v_tok, _o = place("v_tok", _o, [P, 4, 512])
        vb_tok, _o = place("vb_tok", _o, [P, 4, P])
        NFp, _o = place("NFp", _o, [P, TP])
        NFs, _o = place("NFs", _o, [P, 384])
        clf_sb, _o = place("clf_sb", _o, [P, 2, 64])
        lbd, _o = place("lbd", _o, [P, 64])
        kc, _o = place("kc", _o, [P, 2048])
        vc, _o = place("vc", _o, [P, 2048])
        ksw, _o = place("ksw", _o, [P, 1024])
        vsw, _o = place("vsw", _o, [P, 1024])
        hidH, _o = place("hidH", 0, [P, FCH * T], F32R)
        hidL, _o = place("hidL", _o, [P, FCH * T], F32R)
        xg, _o = place("xg", KD * T, [P, D])
        sg, _o = place("sg", _o, [P, 2, MB])
        mh, _o = place("mh", _o, [P, MFF])
        yev, _o = place("yev", _o, [P, D])
        ctk, _o = place("ctk", _o, [P, 2, D])
        onehot, _o = place("onehot", _o, [P, 2, 512])
        cmp1, _o = place("cmp1", _o, [P, 4, 64])
        cmp2, _o = place("cmp2", _o, [P, 4, 64])
        xTH, _o = place("xTH", _o, [P, KD, P], F32R)
        xTL, _o = place("xTL", _o, [P, KD, P], F32R)
        mTH, _o = place("mTH", _o, [P, MCH, P], F32R)
        mTL, _o = place("mTL", _o, [P, MCH, P], F32R)
        y12, _o = place("y12", 0, [P, 2, 2 * D])
        yo, _o = place("yo", _o, [P, 2, D])
        wr = sb("wr", [P, KD, E])
        lg = sb("lg", [P, 4, E])
        rank = sb("rank", [P, 4, E])
        gate = sb("gate", [P, 4, E])
        mem = sb("mem", [P, 4, E])
        memv = sb("memv", [P, 4, E])
        sel1 = sb("sel1", [P, 4, E])
        sel2 = sb("sel2", [P, 4, E])
        posm = sb("posm", [P, 4, E])
        tmp8 = sb("tmp8", [P, 4, E])
        rden = sb("rden", [P, 8])
        gcol = sb("gcol", [P, 8])
        dstv = sb("dstv", [P, 4, E])
        slot_tok = sb("slot_tok", [P, 2 * E], U32)
        gidx = sb("gidx", [P, 1], U32)
        didx = sb("didx", [P, 1], U32)
        cnt = sb("cnt", [1, 8])
        cnt_i = sb("cnt_i", [1, 2], I32)

        def table(name, *dims):
            o, n = TO[name]
            v = tab[:, o:o + n]
            if len(dims) == 2:
                v = v.rearrange("p (a b) -> p a b", a=dims[0])
            return v

        ident, pm, ones, mean = (table(x) for x in ("ident", "pm", "ones", "mean"))
        negtri = table("negtri", 3, TP)
        negones = negtri[:, 0, P:2 * P]
        newtri, cmask = table("newtri"), table("cmask")
        smask = table("smask", 2, P)
        dist = table("dist")
        negslope = table("negslope", NPAIR, 4)
        bmask, tris, iota = table("bmask"), table("tris"), table("iota")
        first, valid, tokid, tok2 = table("first"), table("valid"), table("tokid"), table("tok2")

        raw_full = [sem(f"raw_full{i}") for i in range(RAW)]
        hi_ready, lo_ready, piece_done = sem("hi_ready"), sem("lo_ready"), sem("piece_done")
        aH_ready, aL_ready, yH_ready = sem("aH_ready"), sem("aL_ready"), sem("yH_ready")
        htmp_ready, hH_ready = sem("htmp_ready"), sem("hH_ready")
        xTH_ready, xTL_ready, mTH_ready, mTL_ready = (sem(x) for x in ("xTH_ready", "xTL_ready", "mTH_ready", "mTL_ready"))
        x_loaded, tab_loaded = sem("x_loaded"), sem("tab_loaded")
        act_passed, dve_passed, pool_passed = sem("act_passed"), sem("dve_passed"), sem("pool_passed")
        tab2_loaded, eps_ready, lz_zeroed = sem("tab2_loaded"), sem("eps_ready"), sem("lz_zeroed")
        kc_loaded, vc_loaded, clf_loaded = sem("kc_loaded"), sem("vc_loaded"), sem("clf_loaded")
        va_copied, vb_copied, pe_in, pe_exp = sem("va_copied"), sem("vb_copied"), sem("pe_in"), sem("pe_exp")
        ctka_copied, ctkb_copied = sem("ctka_copied"), sem("ctkb_copied")
        par_loaded = sem("par_loaded")
        swc_loaded = sem("swc_loaded")
        gains_ready = sem("gains_ready")
        sq_ready, sq_used = sem("sq_ready"), sem("sq_used")
        root_ready, recip_ready, a_ready = sem("root_ready"), sem("recip_ready"), sem("a_ready")
        za_ready, ze_ready, zl_ready, logf_ready = (sem(x) for x in ("za_ready", "ze_ready", "zl_ready", "logf_ready"))
        lbd_ready, nf_done, nf_copied = sem("lbd_ready"), sem("nf_done"), sem("nf_copied")
        colroot_ready, colrecip_ready, col_done = sem("colroot_ready"), sem("colrecip_ready"), sem("col_done")
        qbd_zeroed, qbd_ready = sem("qbd_zeroed"), sem("qbd_ready")
        out_done = sem("out_done")
        scores_ready, biased, max_ready, negmax_ready = (sem(x) for x in (
            "scores_ready", "biased", "max_ready", "negmax_ready"))
        exp_ready, den_ready, recipd_ready, norm_ready = (sem(x) for x in (
            "exp_ready", "den_ready", "recipd_ready", "norm_ready"))
        probT_done, probT_copied, av_done, y_copied = (sem(x) for x in (
            "probT_done", "probT_copied", "av_done", "y_copied"))
        h_added = sem("h_added")
        silu_ready, hid_ready = sem("silu_ready"), sem("hid_ready")
        h_added2 = sem("h_added2")
        ctT_done, ctk_stored = sem("ctT_done"), [sem("ctk_stored0"), sem("ctk_stored1")]
        logits_done, memv_ready, pos_done, route = sem("logits_done"), sem("memv_ready"), sem("pos_done"), sem("route")
        cnt_ready = sem("cnt_ready")
        oneh_ready, oneh_used, sidx_ready = sem("oneh_ready"), sem("oneh_used"), sem("sidx_ready")
        iota_ready = sem("iota_ready")
        gidx_ready, didx_ready, xg_loaded, xgT_done = (sem(x) for x in ("gidx_ready", "didx_ready", "xg_loaded", "xgT_done"))
        msilu_ready, mh_ready, mhT_done = sem("msilu_ready"), sem("mh_ready"), sem("mhT_done")
        my_copied, my_stored = sem("my_copied"), sem("my_stored")
        y12_loaded, hT_done, y_half, y_ready, y_out = (
            [sem("y12_loaded0"), sem("y12_loaded1")], sem("hT_done"), sem("y_half"), sem("y_ready"), [sem("y_out0"), sem("y_out1")])

        SB = [4, 5, 6, 2]
        block = ctx.enter_context(nc.Block())
        first_swa_unit = {l: min(u["n"] for u in UNITS if u["l"] == l and u["kind"] == "swa") for l in range(DEPTH)}
        last_unit = {l: max(u["n"] for u in UNITS if u["l"] == l) for l in range(DEPTH)}
        last_of_g = {u["g"]: u["n"] for u in UNITS if u.get("last")}

        def sink_col(u, t=None):
            x = 4 * u["pr"] + (2 if u["what"] == "both" else 3 if u["what"] == "sample" else u["h2"])
            if t is None:
                return par[0:u["rows"], PC["sink"] + x:PC["sink"] + x + 1]
            return t[0:u["rows"], x:x + 1]

        def nsink_col(u):
            return sink_col(u, nsink)

        groups = [[0, 1], [2, 3, 4], [5, 6, 7], [8, 9, 10]]

        def count(c, it, per):
            return c if it is None else it * per + c

        def split_high(p, it=None, per=0):
            w = WIDTH[p]
            nc.scalar.wait_ge(raw_full[p % RAW], count(16 * (p // RAW + 1), it, 16 * (per // RAW)))
            if p >= SPL:
                nc.scalar.wait_ge(piece_done, count(p - SPL + 1, it, per))
            nc.scalar.activation(WH[:, p % SPL, 0:w], raw[:, p % RAW, 0:w], ACT.Copy).then_inc(hi_ready, 1)

        def split_low(p, it=None, per=0):
            w = WIDTH[p]
            nc.vector.wait_ge(hi_ready, count(p + 1, it, per))
            nc.vector.tensor_tensor(WL[:, p % SPL, 0:w], raw[:, p % RAW, 0:w], WH[:, p % SPL, 0:w].bitcast(F32),
                                    ALU.subtract).then_inc(lo_ready, 1)

        def piece(p, n):
            return (WH[:, p % SPL, 0:WIDTH[p]].rearrange("p (a b) -> p a b", a=n),
                    WL[:, p % SPL, 0:WIDTH[p]].rearrange("p (a b) -> p a b", a=n))

        @block.sync
        def _(sp):
            def load(src, p, it=None, per=0):
                if p >= RAW:
                    sp.wait_ge(lo_ready, count(p - RAW + 1, it, per))
                sp.dma_start(raw[:, p % RAW, 0:WIDTH[p]], src).then_inc(raw_full[p % RAW], 16)

            for i in range(2):
                load(w_vf[0, i], i)
            for k in range(KD):
                sp.dma_start(hT[:, k, :], xT[:, k, :]).then_inc(x_loaded, 16)
            sp.dma_start(tab[:, 0:NTAB_ATT], tables[:, 0:NTAB_ATT]).then_inc(tab_loaded, 16)
            for l in range(DEPTH):
                for i in range(2 if l == 0 else 0, 4):
                    load(w_vf[l, i], AT["v", l] + i)
                for x in range(NCOL):
                    load(w_col[l, x], AT["col", l] + x)
                    if l == 0 and x == 4:
                        sp.dma_start(tab[:, NTAB_ATT:NTAB], tables[:, NTAB_ATT:NTAB]).then_inc(tab2_loaded, 16)
                        sp.dma_start(selb[:, :, :, :].rearrange("p a b c -> p (a b c)"), selt[:, :]).then_inc(tab2_loaded, 16)
                        sp.dma_start(wr[:, :, :].rearrange("p k e -> p (k e)"), w_r[:, :]).then_inc(tab2_loaded, 16)
                for m in range(KD):
                    load(w_o[l, m], AT["wo", l] + m)
                if l % 2 == 0:
                    for x in range(2 * LOOP0):
                        load(w_gu[x], AT["gu"] + x)
                    with sp.Fori(0, (LOOP1 - LOOP0) // CBODY) as i:
                        for x in range(2 * LOOP0, 2 * LOOP0 + 2 * CBODY):
                            load(w_gu[bass.ds(i * (2 * CBODY) + x, 1)].rearrange("o p n -> (o p) n"), AT["gu"] + x,
                                 i, 2 * CBODY)
                    for x in range(2 * LOOP1, 2 * FCH):
                        load(w_gu[x], AT["gu"] + x)
                    for x in range(2 * KD):
                        load(w_d[x], AT["down"] + x)

            def load_expert(e, x, n):
                if x % MPER < 16:
                    src = w_egu[bass.ds(e * 16 + x % MPER, 1)].rearrange("o p n -> (o p) n")
                elif x % 2 == 0:
                    src = w_ed0[bass.ds(e * 4 + (x - 16) // 2, 1)].rearrange("o p n -> (o p) n")
                else:
                    src = w_ed1[bass.ds(e * 4 + (x - 16) // 2, 1)].rearrange("o p n -> (o p) n")
                load(src, AT["moe"] + x, n, MPER)

            for x in range(RAW):
                load(w_egu[x], AT["moe"] + x)
            sp.wait_ge(cnt_ready, 1)
            most = sp.value_load(cnt_i[0:1, 0:1], min_val=0, max_val=T)
            with sp.Fori(0, MAXR) as r:
                with sp.If(most > r * P):
                    with sp.Fori(0, E - 1) as e:
                        for x in range(RAW, MPER):
                            load_expert(e, x, r * E + e)
                        for x in range(MPER, MPER + RAW):
                            load_expert(e + 1, x, r * E + e)
                    for x in range(RAW, MPER):
                        load_expert(E - 1, x, r * E + (E - 1))
                    with sp.If(most > r * P + P):
                        for x in range(MPER, MPER + RAW):
                            load_expert(0, x, r * E + (E - 1))

        def store_y(eng, i):
            t0, r = TT[i]
            eng.wait_ge(y_ready, i + 1)
            eng.dma_start(o_y[t0:t0 + r, :], yo[0:r, i % 2, :]).then_inc(y_out[i % 2], 16)

        @block.gpsimd
        def _(pool):
            def low_parts(i):
                for k in range(KD):
                    pool.wait_ge(aH_ready, i * KD + k + 1)
                    nc.gpsimd.tensor_tensor(aL[:, k, :], aT[:, k, :], aH[:, k, :].bitcast(F32), ALU.subtract
                                            ).then_inc(aL_ready, 1)

            for l in range(DEPTH):
                if l:
                    pool.wait_ge(h_added2, KD * l)
                pool.dma_start(par[:, :], params[l]).then_inc(par_loaded, 16)
                nc.gpsimd.memset(qbd[:, :, :], 0.0).then_inc(qbd_zeroed, 1)
                pool.dma_start(clf_sb[:, :, :].rearrange("p c n -> p (c n)"), clf[l]).then_inc(clf_loaded, 16)
                pool.dma_start(ksw[:, :], ck_swa[l]).then_inc(swc_loaded, 16)
                pool.dma_start(vsw[:, :], cv_swa[l]).then_inc(swc_loaded, 16)
                pool.dma_start(kc[:, :], ck_fox[l, 0]).then_inc(kc_loaded, 16)
                pool.dma_start(vc[:, :], cv_fox[l, 0]).then_inc(vc_loaded, 16)
                low_parts(2 * l)
                pool.wait_ge(va_copied, 4 * (l + 1))
                pool.wait_ge(vb_copied, 4 * (l + 1))
                for i, (t0, r) in enumerate(QT):
                    pool.dma_start(o_vfox[l, t0:t0 + r, :], v_tok[0:r, i, :]).then_inc(out_done, 16)
                    pool.dma_start(o_vswa[l, t0:t0 + r, :], vb_tok[0:r, i, :]).then_inc(out_done, 16)
                pool.wait_ge(logf_ready, l + 1)
                for i, (t0, r) in enumerate(QT):
                    pool.dma_start(o_lf[l, t0:t0 + r, :], lf[0:r, i, :]).then_inc(out_done, 16)
                pool.wait_ge(qbd_zeroed, l + 1)
                for x, c in enumerate(COLS):
                    pool.wait_ge(col_done, l * NCOL + x + 1)
                    if c < 4 or c > 8:
                        dst = qbd[:, c if c < 4 else c - 5, :].rearrange("p (b h q) -> p b h q", b=BS, h=2)
                        for h2 in range(2):
                            last = nc.gpsimd.tensor_copy(
                                dst[64 * h2:64 * h2 + 64, :, h2, :],
                                qk[64 * h2:64 * h2 + 64, c, TP:T].rearrange("p (b q) -> p b q", b=BS))
                        last.then_inc(qbd_ready, 1)
                    elif c < 8:
                        pool.dma_start(o_kfox[l, c - 4], qk[:, c, :]).then_inc(out_done, 16)
                    else:
                        pool.dma_start(o_kswa[l], qk[:, c, :]).then_inc(out_done, 16)
                pool.wait_ge(qbd_ready, 8 * (l + 1))
                for u in UNITS[l * NU:(l + 1) * NU]:
                    n, rows, keys = u["n"], u["rows"], u["keys"]
                    prev = last_of_g.get(u["g"] - 1)
                    if u["kind"] == "fox" and u["pr"] and n == prev + 1:
                        pool.wait_ge(scores_ready, prev + 1)
                        pool.dma_start(kc[:, :], ck_fox[l, u["pr"]]).then_inc(kc_loaded, 16)
                    if u["kind"] == "fox" and u["pr"] and n == prev + LAG + 2:
                        pool.wait_ge(av_done, prev + 1)
                        pool.dma_start(vc[:, :], cv_fox[l, u["pr"]]).then_inc(vc_loaded, 16)
                    pool.wait_ge(recipd_ready, n + 1)
                    nc.gpsimd.tensor_scalar(prob[0:rows, n % 3, 0:keys], prob[0:rows, n % 3, 0:keys],
                                            small[0:rows, 12 + n % 4:13 + n % 4], None, ALU.mult).then_inc(norm_ready, 1)
                if l % 2 == 0:
                    low_parts(2 * l + 1)
            for i, (t0, r) in enumerate(TT):
                pool.wait_ge(ctka_copied, i + 1)
                pool.wait_ge(ctkb_copied, i + 1)
                pool.dma_start(c_rows[t0:t0 + r, :], ctk[0:r, i % 2, :]).then_inc(ctk_stored[i % 2], 16)
            for i in range(2):
                pool.wait_ge(ctk_stored[i], 32)
            pool.wait_ge(cnt_ready, 1)
            most = pool.value_load(cnt_i[0:1, 0:1], min_val=0, max_val=T)

            def store_rows(e, n):
                pool.wait_ge(my_copied, n * 2 + 2)
                pool.sem_inc(pool_passed, 1)
                nc.gpsimd.tensor_copy(didx[:, 0:1], slot_tok[:, bass.ds(e + E, 1)]).then_inc(didx_ready, 1)
                pool.wait_ge(didx_ready, n + 1)
                pool.sem_inc(pool_passed, 1)
                nc.gpsimd.indirect_dma_start(
                    out=y_rows[:, :], out_offset=bass.IndirectOffsetOnAxis(ap=didx[:, 0:1], axis=0), in_=yev[:, :],
                    in_offset=None, bounds_check=2 * T - 1, oob_is_err=False).then_inc(my_stored, 16)
                pool.wait_ge(my_stored, n * 16 + 16)
                pool.sem_inc(pool_passed, 1)

            def gather(e, n):
                if not isinstance(e, int):
                    pool.wait_ge(xgT_done, n * 2)
                    pool.sem_inc(pool_passed, 1)
                nc.gpsimd.tensor_copy(gidx[:, 0:1], slot_tok[:, bass.ds(e, 1)]).then_inc(gidx_ready, 1)
                pool.wait_ge(gidx_ready, n + 1)
                pool.sem_inc(pool_passed, 1)
                nc.gpsimd.indirect_dma_start(
                    out=xg[:, :], out_offset=None, in_=c_rows[:, :],
                    in_offset=bass.IndirectOffsetOnAxis(ap=gidx[:, 0:1], axis=0)).then_inc(xg_loaded, 16)

            with pool.Fori(0, MAXR) as r:
                with pool.If(most > r * P):
                    pool.wait_ge(sidx_ready, r + 1)
                    pool.sem_inc(pool_passed, 1)
                    gather(0, r * E)
                    with pool.Fori(1, E) as e:
                        gather(e, r * E + e)
                        store_rows(e - 1, r * E + e - 1)
                    store_rows(E - 1, r * E + (E - 1))
            for i, (t0, r) in enumerate(TT):
                if i >= 2:
                    pool.wait_ge(y_ready, i - 1)
                pool.dma_start(y12[0:r, i % 2, :], y_rows[2 * t0:2 * t0 + 2 * r, :].rearrange("(t w) d -> t (w d)", w=2)
                               ).then_inc(y12_loaded[i % 2], 16)
                if i >= 1:
                    store_y(pool, i - 1)
            store_y(pool, 3)
            for i in range(2):
                pool.wait_ge(y_out[i], 32)
            pool.wait_ge(out_done, 16 * DEPTH * OUTS_PER_LAYER)

        @block.tensor
        def _(pe):
            mm = nc.tensor.matmul

            def mm3(out, aw, bw, start, stop):
                mm(out, aw[0], bw[0], start=start, stop=False)
                mm(out, aw[0], bw[1], start=False, stop=False)
                return mm(out, aw[1], bw[0], start=False, stop=stop)

            def act_parts(k, t0=0, t1=T):
                return aH[:, k, t0:t1], aL[:, k, t0:t1]

            def split(p, it=None, per=0):
                pe.wait_ge(lo_ready, count(p + 1, it, per))

            def all_features(out, p, it=None, per=0):
                split(p, it, per)
                wh, wl = piece(p, KD)
                for k in range(KD):
                    last = mm3(out[:, 0:T], (wh[:, k, :], wl[:, k, :]), act_parts(k), k == 0, k == KD - 1)
                last.then_inc(piece_done, 1)

            def norm(l, w, ks=range(KD)):
                for k in ks:
                    i = l * SQ_PER_LAYER + (KD + NCOL) * w + k
                    pe.wait_ge(sq_ready, i + 1)
                    mm(bank[2][:, 0:T], mean, sq[:, i % 2, :], start=(k == 0), stop=(k == KD - 1)).then_inc(sq_used, 1)

            def scores(u):
                n, l, pr, rows, keys = u["n"], u["l"], u["pr"], u["rows"], u["keys"]
                S = bank[SB[n % 4]]
                fox = u["kind"] == "fox"
                qc, kk = (pr, 4 + pr) if fox else (9 + pr, 8)
                if n % NU >= 4:
                    pe.wait_ge(exp_ready, n - 3)
                if u["what"] == "prompt":
                    h0, q0 = 64 * u["h2"], u["q0"]
                    if fox:
                        mm(S[0:rows, 0:keys], selb[0:H, pr, 2 + u["h2"], 0:rows], NFp[0:H, 0:keys], start=True, stop=False)
                    last = mm(S[0:rows, 0:keys], qk[h0:h0 + 64, qc, q0:q0 + rows], qk[h0:h0 + 64, kk, 0:keys],
                              start=not fox, stop=True)
                elif u["what"] == "both":
                    for h2 in range(2):
                        h0 = 64 * h2
                        last = mm(S[h0:h0 + 64, 0:keys], qk[h0:h0 + 64, qc, 208:TP], qk[h0:h0 + 64, kk, 0:keys],
                                  start=True, stop=True)
                else:
                    s = u["s"]
                    past = PAST if fox else 128
                    d = pr if fox else 4 + pr
                    if fox:
                        pe.wait_ge(kc_loaded, 16 * (l * NPAIR + pr + 1))
                        mm(S[:, 0:keys], selb[:, pr, s, :], NFs[0:64, 0:keys], start=True, stop=False)
                    else:
                        pe.wait_ge(swc_loaded, 32 * (l + 1))
                    pe.wait_ge(qbd_ready, l * 8 + d + 1)
                    mm(S[:, past:past + P], qbd[:, d, 128 * s:128 * s + 128], qk[:, kk, TP:T], start=not fox, stop=not fox)
                    for b4 in range(4):
                        b = 4 * s + b4
                        keysT = kc[:, 256 * b:256 * b + 256] if fox else ksw[:, 128 * b:128 * b + 128]
                        last = mm(S[32 * b4:32 * b4 + 32, 0:past], qbd[:, d, 32 * b:32 * b + 32], keysT,
                                  start=not fox, stop=True, tile_position=(0, 32 * b4))
                last.then_inc(scores_ready, 1)

            def transposes(u):
                n, rows, keys = u["n"], u["rows"], u["keys"]
                pe.wait_ge(norm_ready, n + 1)
                if n >= 2:
                    pe.wait_ge(probT_copied, n - 1)
                PT = bank[7 if n % 2 else 3]
                for i in range(-(-keys // P)):
                    w = min(P, keys - P * i)
                    last = nc.tensor.transpose(PT[0:w, P * i:P * i + rows], prob[0:rows, n % 3, P * i:P * i + w],
                                               ident[0:rows, 0:rows])
                last.then_inc(probT_done, 1)

            def av(u):
                n, l, pr, rows, keys = u["n"], u["l"], u["pr"], u["rows"], u["keys"]
                fox = u["kind"] == "fox"
                pe.wait_ge(probT_copied, n + 1)
                if n and u["g"] != UNITS[n - 1]["g"]:
                    pe.wait_ge(y_copied, u["g"])
                pT = probT[:, n % 2, :]
                values = v_tok if fox else vb_tok
                c0 = 128 * pr if fox else 0
                if u["what"] != "sample":
                    nk = -(-keys // P)
                    for h2 in ((0, 1) if u["what"] == "both" else (u["h2"],)):
                        h0, cols, x0 = 64 * h2, rows, 0
                        if u["what"] == "both":
                            cols, x0 = 64, 64 * h2
                        for i in range(nk):
                            w = min(P, keys - P * i)
                            last = mm(bank[0][h0:h0 + 64, u["q0"]:u["q0"] + cols],
                                      values[0:w, i, c0 + h0:c0 + h0 + 64], pT[0:w, P * i + x0:P * i + x0 + cols],
                                      start=(i == 0), stop=(i == nk - 1))
                else:
                    s = u["s"]
                    nk = 3 if fox else 2
                    if fox:
                        pe.wait_ge(vc_loaded, 16 * (l * NPAIR + pr + 1))
                    mm(bank[1][:, 128 * s:128 * s + 128], values[:, 3, c0:c0 + 128], pT[:, P * (nk - 1):P * nk],
                       start=True, stop=False)
                    for b4 in range(4):
                        b = 4 * s + b4
                        for i in range(nk - 1):
                            vals = vc[:, (2 * b + i) * 128:(2 * b + i) * 128 + 128] if fox else vsw[:, 128 * b:128 * b + 128]
                            last = mm(bank[1][:, 32 * b:32 * b + 32], vals, pT[:, P * i + 32 * b4:P * i + 32 * b4 + 32],
                                      start=False, stop=(b4 == 3 and i == nk - 2))
                last.then_inc(av_done, 1)

            pe.wait_ge(tab_loaded, 16)
            norm(0, 0)
            for l in range(DEPTH):
                for i in range(4):
                    p = AT["v", l] + i
                    split(p)
                    wh, wl = piece(p, 2)
                    pe.wait_ge(aL_ready, 2 * l * KD + 2 * i + 2)
                    for x, (t0, r) in enumerate(QT):
                        t1 = max(t0, min(t0, T - P)) + P
                        for w, (c0, c1) in enumerate(((0, 512), (512, 648))):
                            for k in range(2):
                                last = mm3(bank[x + 4 * w][:, 0:c1 - c0], act_parts(2 * i + k, t0, t1),
                                           (wh[:, k, c0:c1], wl[:, k, c0:c1]), i + k == 0, i + k == 4)
                    last.then_inc(piece_done, 1)

                def head_mean(x):
                    i = l * SQ_PER_LAYER + KD + x
                    pe.wait_ge(sq_ready, i + 1)
                    if x >= 2:
                        pe.wait_ge(colroot_ready, l * NCOL + x - 1)
                    elif x == 0:
                        pe.wait_ge(vb_copied, 4 * (l + 1))
                    mm(bank[4 + x % 2][:, 0:T], pm, sq[:, i % 2, :], start=True, stop=True).then_inc(sq_used, 1)

                for x in range(NCOL):
                    if x < 4:
                        pe.wait_ge(va_copied, 4 * l + x + 1)
                    else:
                        pe.wait_ge(col_done, l * NCOL + x - 3)
                    all_features(bank[x % 4], AT["col", l] + x)
                    if x:
                        head_mean(x - 1)
                head_mean(NCOL - 1)
                pe.wait_ge(logf_ready, l + 1)
                pe.wait_ge(va_copied, 4 * (l + 1))
                for i, (t0, r) in enumerate(QT[:3]):
                    last = mm(bank[6][0:H, 0:TP], lf[0:r, i, :], negtri[0:r, i, :], start=(i == 0), stop=(i == 2))
                last.then_inc(nf_done, 1)
                pe.wait_ge(clf_loaded, 16 * (l + 1))
                pe.wait_ge(lbd_ready, l + 1)
                for c in range(2):
                    mm(bank[7][0:64, 0:PAST], clf_sb[:, c, :], negtri[:, c, 0:PAST], start=(c == 0), stop=(c == 1))
                for c in range(2):
                    mm(bank[7][0:64, PAST:384], clf_sb[:, c, :], negones, start=(c == 0), stop=False)
                mm(bank[7][0:64, PAST:384], lbd[:, :], newtri, start=False, stop=True).then_inc(nf_done, 1)

                if l == 0:
                    pe.wait_ge(tab2_loaded, 48)
                pe.wait_ge(nf_copied, 2 * (l + 1))
                pe.wait_ge(col_done, (l + 1) * NCOL)
                units = UNITS[l * NU:(l + 1) * NU]
                for i in range(NU + LAG + 1):
                    if i < NU:
                        scores(units[i])
                    if LAG <= i < NU + LAG:
                        transposes(units[i - LAG])
                    if i >= LAG + 1:
                        av(units[i - LAG - 1])

                pe.wait_ge(y_copied, (l + 1) * NG)
                for m in range(KD):
                    if m >= 2:
                        pe.wait_ge(h_added, l * KD + m - 1)
                    all_features(bank[m % 2], AT["wo", l] + m)
                    if m:
                        norm(l, 1, [m - 1])
                norm(l, 1, [KD - 1])
                if l % 2 == 0:
                    pe.wait_ge(aL_ready, (2 * l + 2) * KD)

                    def chunk(c, it=None):
                        if c >= 2:
                            pe.wait_ge(hid_ready, count(c - 1, it, CBODY))
                        for w in range(2):
                            all_features(bank[2 * (c % 2) + w], AT["gu"] + 2 * c + w, it, 2 * CBODY)
                    for c in range(LOOP0):
                        chunk(c)
                    with pe.Fori(0, (LOOP1 - LOOP0) // CBODY) as i:
                        for c in range(LOOP0, LOOP0 + CBODY):
                            chunk(c, i)
                    for c in range(LOOP1, FCH):
                        chunk(c)
                    pe.wait_ge(hid_ready, FCH)
                    for m in range(KD):
                        if m >= 4:
                            pe.wait_ge(h_added2, m - 3)
                        for hf in range(2):
                            p = AT["down"] + 2 * m + hf
                            split(p)
                            wh, wl = piece(p, FCH // 2)
                            for c in range(FCH // 2):
                                o = (hf * (FCH // 2) + c) * T
                                last = mm3(bank[4 + m % 4][:, 0:T], (wh[:, c, :], wl[:, c, :]),
                                           (hidH[:, o:o + T], hidL[:, o:o + T]),
                                           hf + c == 0, hf == 1 and c == FCH // 2 - 1)
                            last.then_inc(piece_done, 1)
                        if m:
                            norm(l + 1, 0, [m - 1])
                    norm(l + 1, 0, [KD - 1])

            pe.wait_ge(a_ready, 2 * DEPTH * KD)
            for i, (t0, r) in enumerate(TT):
                for k in range(KD):
                    last = mm(bank[5][0:r, E * i:E * i + E], aT[:, k, t0:t0 + r], wr[:, k, :], start=(k == 0), stop=(k == KD - 1))
                last.then_inc(logits_done, 1)
            for i, (t0, r) in enumerate(TT):
                for hf in range(2):
                    if i >= 2:
                        pe.wait_ge(ctkb_copied if hf else ctka_copied, i - 1)
                    for k in range(4):
                        last = nc.tensor.transpose(bank[2 * (i % 2) + hf][0:r, P * k:P * k + P],
                                                   aT[:, 4 * hf + k, t0:t0 + r], ident)
                    last.then_inc(ctT_done, 1)
            pe.wait_ge(memv_ready, 1)
            for i in range(4):
                mm(bank[6][0:1, 0:E], ones[:, 0:1], memv[:, i, :], start=(i == 0), stop=(i == 3))
            for i in range(4):
                for j in range(i + 1):
                    last = mm(bank[7][:, E * i:E * i + E], tris if i == j else ones, memv[:, j, :], start=(j == 0), stop=(j == i))
            last.then_inc(pos_done, 1)
            pe.wait_ge(cnt_ready, 1)
            most = pe.value_load(cnt_i[0:1, 0:1], min_val=0, max_val=T)

            def tokens_T(n, hf):
                if hf:
                    pe.wait_ge(xTL_ready, n * 2 + 1)
                else:
                    pe.wait_ge(xg_loaded, n * 16 + 16)
                for k in range(4):
                    last = nc.tensor.transpose(bank[7][:, P * k:P * k + P], xg[:, P * (4 * hf + k):P * (4 * hf + k) + P], ident)
                last.then_inc(xgT_done, 1)

            with pe.Fori(0, MAXR) as r:
                with pe.If(most > r * P):
                    for e in range(E):
                        pe.wait_ge(oneh_ready, r * E + e + 1)
                        for w in range(2):
                            for i in range(4):
                                last = mm(bank[6][:, E * w + e:E * w + e + 1], onehot[:, e % 2, P * i:P * i + P],
                                          dstv[:, i, e:e + 1] if w else tokid[:, i:i + 1], start=(i == 0), stop=(i == 3))
                        last.then_inc(oneh_used, 1)
                    tokens_T(r * E, 0)
                    tokens_T(r * E, 1)
                    with pe.Fori(0, E) as e:
                        n = r * E + e

                        def hidden_T(j):
                            pe.wait_ge(mh_ready, n * 4 + (j + 1))
                            if j in (1, 2):
                                pe.wait_ge(mTL_ready, n * 4 + j)
                            for x, c in enumerate(groups[j]):
                                last = nc.tensor.transpose(bank[0 if j == 3 else 4][:, P * x:P * x + P], mh[:, P * c:P * c + P], ident)
                            last.then_inc(mhT_done, 1)

                        def down(m, hf):
                            x = 16 + 2 * m + hf
                            split(AT["moe"] + x, n, MPER)
                            wh, wl = piece(AT["moe"] + x, MCH - MD0 if hf else MD0)
                            c0, c1 = (MD0, MCH) if hf else (0, MD0)
                            for c in range(c0, c1):
                                if m == 0 and c in (MD0, groups[3][0]):
                                    pe.wait_ge(mTL_ready, n * 4 + (3 if c == MD0 else 4))
                                last = mm3(bank[5 + m // 2][:, 256 * (m % 2):256 * (m % 2) + 256],
                                           (mTH[:, c, :], mTL[:, c, :]), (wh[:, c - c0, :], wl[:, c - c0, :]),
                                           c == 0, c == MCH - 1)
                            last.then_inc(piece_done, 1)

                        pe.wait_ge(xTL_ready, n * 2 + 2)
                        for j in range(MBLK):
                            if j >= 2:
                                pe.wait_ge(mh_ready, n * 4 + (j - 1))
                            for w in range(2):
                                for hf in range(2):
                                    p = AT["moe"] + 4 * j + 2 * w + hf
                                    split(p, n, MPER)
                                    wh, wl = piece(p, KD // 2)
                                    for k in range(KD // 2):
                                        kk = hf * (KD // 2) + k
                                        last = mm3(bank[2 * (j % 2) + w][:, 0:MB], (xTH[:, kk, :], xTL[:, kk, :]),
                                                   (wh[:, k, :], wl[:, k, :]), kk == 0, kk == KD - 1)
                                    last.then_inc(piece_done, 1)
                            if j:
                                hidden_T(j - 1)
                        with pe.If(e < E - 1):
                            tokens_T(n + 1, 0)
                        pe.wait_ge(mTL_ready, n * 4 + 2)
                        down(0, 0)
                        hidden_T(3)
                        down(0, 1)
                        down(1, 0)
                        down(1, 1)
                        with pe.If(e < E - 1):
                            tokens_T(n + 1, 1)
                        for m in (2, 3):
                            down(m, 0)
                            down(m, 1)
            for i, (t0, r) in enumerate(TT):
                if i >= 2:
                    pe.wait_ge(y_half, 2 * (i - 1))
                for k in range(KD):
                    last = nc.tensor.transpose(bank[2 * (i % 2) + k // 4][0:r, P * (k % 4):P * (k % 4) + P],
                                               hT[:, k, t0:t0 + r], ident)
                last.then_inc(hT_done, 1)

        @block.scalar
        def _(act):
            A = nc.scalar.activation

            def square(i, src):
                if i >= 2:
                    act.wait_ge(sq_used, i - 1)
                A(sq[:, i % 2, :], src, ACT.Square).then_inc(sq_ready, 1)

            def norm_square(l, w, k):
                if w:
                    act.wait_ge(h_added, l * KD + k + 1)
                elif l:
                    act.wait_ge(h_added2, (l - 1) * KD + k + 1)
                square(l * SQ_PER_LAYER + (KD + NCOL) * w + k, hT[:, k, :])

            def norm_rest(l, w):
                act.wait_ge(sq_used, l * SQ_PER_LAYER + (KD + NCOL) * w + KD)
                A(rt[:, 0, :], bank[2][:, 0:T], ACT.Sqrt, bias=eps_col[:, 0:1]).then_inc(root_ready, 1)
                for k in range(KD if 2 * l + w < 3 else 0):
                    act.wait_ge(a_ready, (2 * l + w) * KD + k + 1)
                    A(aH[:, k, :], aT[:, k, :], ACT.Copy).then_inc(aH_ready, 1)

            act.wait_ge(eps_ready, 1)
            for p in range(SPL - 1):
                split_high(p)
            act.wait_ge(x_loaded, 16 * KD)
            for k in range(KD):
                norm_square(0, 0, k)
            split_high(SPL - 1)
            for l in range(DEPTH):
                norm_rest(l, 0)
                v = AT["v", l]
                for i in range(3):
                    split_high(v + i + SPL)
                act.wait_ge(piece_done, v + 4)
                for i, (t0, r) in enumerate(QT):
                    A(v_tok[0:r, i, :], bank[i][0:r, :], ACT.Copy).then_inc(va_copied, 1)
                split_high(v + 3 + SPL)
                act.wait_ge(za_ready, l + 1)
                A(le[:, :, :], le[:, :, :], ACT.Exp, scale=-1.0).then_inc(ze_ready, 1)
                act.wait_ge(ze_ready, l + 1)
                A(le[:, :, :], le[:, :, :], ACT.Ln, bias=1.0).then_inc(zl_ready, 1)

                def head_root(x):
                    act.wait_ge(sq_used, l * SQ_PER_LAYER + KD + x + 1)
                    if x >= 2:
                        act.wait_ge(colrecip_ready, l * NCOL + x - 1)
                    A(rt[:, x % 2, :], bank[4 + x % 2][:, 0:T], ACT.Sqrt, bias=eps_col[:, 0:1]).then_inc(colroot_ready, 1)

                act.wait_ge(recip_ready, 2 * l + 1)
                for x in range(NCOL):
                    act.wait_ge(piece_done, AT["col", l] + x + 1)
                    square(l * SQ_PER_LAYER + KD + x, bank[x % 4][:, 0:T])
                    split_high(AT["col", l] + x + SPL)
                    if x:
                        head_root(x - 1)
                head_root(NCOL - 1)

                def exps(u):
                    n, rows, keys = u["n"], u["rows"], u["keys"]
                    nm = small[0:rows, 4 + n % 4:5 + n % 4]
                    act.wait_ge(negmax_ready, n + 1)
                    if n >= 3:
                        act.wait_ge(probT_done, n - 2)
                    if u["kind"] == "swa":
                        A(small[0:rows, 16 + n % 4:17 + n % 4], sink_col(u), ACT.Exp, bias=nm)
                    A(prob[0:rows, n % 3, 0:keys], bank[SB[n % 4]][0:rows, 0:keys], ACT.Exp, bias=nm,
                      accum_out=small[0:rows, 8 + n % 4:9 + n % 4]).then_inc(exp_ready, 1)

                def copy_T(u):
                    n, rows, keys = u["n"], u["rows"], u["keys"]
                    act.wait_ge(probT_done, n + 1)
                    if n >= 2:
                        act.wait_ge(av_done, n - 1)
                    PT = bank[7 if n % 2 else 3]
                    nk = keys // P
                    if nk:
                        last = A(probT[:, n % 2, 0:nk * P].rearrange("p (i w) -> p i w", i=nk)[:, :, 0:rows],
                                 PT[:, 0:nk * P].rearrange("p (i w) -> p i w", i=nk)[:, :, 0:rows], ACT.Copy)
                    if keys % P:
                        w = keys % P
                        last = A(probT[0:w, n % 2, nk * P:nk * P + rows], PT[0:w, nk * P:nk * P + rows], ACT.Copy)
                    last.then_inc(probT_copied, 1)

                def take_y(g):
                    act.wait_ge(av_done, last_of_g[g] + 1)
                    k = g % NG
                    smp = bank[1][:, 0:256].rearrange("p (b h q) -> p b h q", b=BS, h=2)
                    A(aH[:, k, 0:TP], bank[0][:, 0:TP], ACT.Copy)
                    for h2 in range(2):
                        last = A(aH[64 * h2:64 * h2 + 64, k, TP:T].rearrange("p (b q) -> p b q", b=BS),
                                 smp[64 * h2:64 * h2 + 64, :, h2, :], ACT.Copy)
                    last.then_inc(yH_ready, 1)

                units = UNITS[l * NU:(l + 1) * NU]
                taken = l * NG
                for i in range(NU + LAG + 2):
                    if i < NU:
                        exps(units[i])
                    if LAG <= i < NU + LAG:
                        copy_T(units[i - LAG])
                    if taken < (l + 1) * NG and last_of_g[taken] + LAG + 1 == l * NU + i:
                        take_y(taken)
                        taken += 1
                for m in range(KD):
                    if AT["wo", l] + m + SPL < len(WIDTH):
                        split_high(AT["wo", l] + m + SPL)
                    norm_square(l, 1, m)
                norm_rest(l, 1)
                if l % 2 == 0:
                    def chunk(c, it=None):
                        p = AT["gu"] + 2 * c
                        split_high(p + SPL, it, 2 * CBODY)
                        act.wait_ge(piece_done, count(p + 1, it, 2 * CBODY))
                        if c >= 2:
                            act.wait_ge(hid_ready, count(c - 1, it, CBODY))
                        A(sq[:, c % 2, :], bank[2 * (c % 2)][:, 0:T], ACT.Silu).then_inc(silu_ready, 1)
                        split_high(p + 1 + SPL, it, 2 * CBODY)
                    for c in range(LOOP0):
                        chunk(c)
                    with act.Fori(0, (LOOP1 - LOOP0) // CBODY) as i:
                        for c in range(LOOP0, LOOP0 + CBODY):
                            chunk(c, i)
                    for c in range(LOOP1, FCH):
                        chunk(c)
                    for m in range(KD):
                        for hf in range(2):
                            split_high(AT["down"] + 2 * m + hf + SPL)
                        norm_square(l + 1, 0, m)
            act.wait_ge(out_done, 16 * DEPTH * OUTS_PER_LAYER)
            for i, (t0, r) in enumerate(TT):
                act.wait_ge(ctT_done, 2 * i + 1)
                if i >= 2:
                    act.wait_ge(ctk_stored[i % 2], 16 * (i // 2))
                A(ctk[0:r, i % 2, 0:512], bank[2 * (i % 2)][0:r, :], ACT.Copy).then_inc(ctka_copied, 1)
            act.wait_ge(pe_in, 1)
            A(gate[:, :, :], tmp8[:, :, :], ACT.Exp).then_inc(pe_exp, 1)
            act.wait_ge(cnt_ready, 1)
            most = act.value_load(cnt_i[0:1, 0:1], min_val=0, max_val=T)
            with act.Fori(0, MAXR) as r:
                with act.If(most > r * P):
                    def copy_tokens(n, hf):
                        act.wait_ge(xgT_done, n * 2 + (hf + 1))
                        A(xTH[:, 4 * hf:4 * hf + 4, :].rearrange("p k t -> p (k t)"), bank[7][:, :], ACT.Copy).then_inc(xTH_ready, 1)
                    copy_tokens(r * E, 0)
                    copy_tokens(r * E, 1)
                    with act.Fori(0, E) as e:
                        n = r * E + e
                        M = AT["moe"] + SPL

                        def copy_hidden(j):
                            act.wait_ge(mhT_done, n * 4 + (j + 1))
                            c0, w = groups[j][0], len(groups[j])
                            A(mTH[:, c0:c0 + w, :].rearrange("p c t -> p (c t)"), bank[0 if j == 3 else 4][:, 0:P * w],
                              ACT.Copy).then_inc(mTH_ready, 1)
                        for j in range(MBLK):
                            split_high(M + 4 * j, n, MPER)
                            split_high(M + 4 * j + 1, n, MPER)
                            act.wait_ge(piece_done, count(AT["moe"] + 4 * j + 2, n, MPER))
                            if j >= 2:
                                act.wait_ge(mh_ready, n * 4 + (j - 1))
                            A(sg[:, j % 2, :], bank[2 * (j % 2)][:, 0:MB], ACT.Silu).then_inc(msilu_ready, 1)
                            split_high(M + 4 * j + 2, n, MPER)
                            split_high(M + 4 * j + 3, n, MPER)
                            if j:
                                copy_hidden(j - 1)
                        with act.If(e < E - 1):
                            copy_tokens(n + 1, 0)
                        with act.Else():
                            act.wait_ge(my_stored, n * 16)
                            act.sem_inc(act_passed, 1)
                        copy_hidden(3)
                        for x in range(16, 20):
                            split_high(M + x, n, MPER)
                        with act.If(e < E - 1):
                            copy_tokens(n + 1, 1)
                        act.wait_ge(piece_done, count(AT["moe"] + 20, n, MPER))
                        A(yev[:, 0:512], bank[5][:, :], ACT.Copy).then_inc(my_copied, 1)
                        split_high(M + 20, n, MPER)
                        with act.If(e < E - 1):
                            for x in range(21, 24):
                                split_high(M + x, n, MPER)
                    with act.If(most > r * P + P):
                        for x in range(21, 24):
                            split_high(AT["moe"] + SPL + x, r * E + (E - 1), MPER)

        @block.vector
        def _(dve):
            V = nc.vector
            nc.vector.memset(eps_col[:, 0:1], EPS).then_inc(eps_ready, 1)
            nc.vector.memset(lz[:, :, :], 0.0).then_inc(lz_zeroed, 1)
            nc.vector.memset(lg[:, :, :], 0.0).then_inc(lz_zeroed, 1)

            def norm(l, w):
                i = 2 * l + w
                g0 = PC["g_ffn" if w else "g_attn"]
                dve.wait_ge(root_ready, i + 1)
                V.reciprocal(rs[:, 0, :], rt[:, 0, :]).then_inc(recip_ready, 1)
                dve.wait_ge(recip_ready, i + 1)
                for k in range(KD):
                    V.scalar_tensor_tensor(aT[:, k, :], hT[:, k, :], par[:, g0 + k:g0 + k + 1], rs[:, 0, :],
                                           ALU.mult, ALU.mult).then_inc(a_ready, 1)

            for p in range(SPL):
                split_low(p)
            for l in range(DEPTH):
                dve.wait_ge(par_loaded, 16 * (l + 1))
                for x, nm in enumerate(("qn_a", "qn_b")):
                    V.tensor_scalar(gq[:, x:x + 1], par[:, PC[nm]:PC[nm] + 1], HD ** -0.5, None, ALU.mult)
                V.tensor_scalar(nsink[:, :], par[:, PC["sink"]:PC["sink"] + 16], -1.0, None, ALU.mult).then_inc(gains_ready, 1)
                dve.wait_ge(gains_ready, l + 1)
                if l == 0:
                    dve.wait_ge(x_loaded, 16 * KD)
                norm(l, 0)
                v = AT["v", l]
                for i in range(3):
                    split_low(v + i + SPL)
                if l == 0:
                    dve.wait_ge(lz_zeroed, 2)
                dve.wait_ge(piece_done, v + 4)
                bf = par[:, PC["b_f"]:PC["b_f"] + H]
                for i, (t0, r) in enumerate(QT):
                    V.tensor_tensor(lz[0:r, i, :], bank[4 + i][0:r, 128:136], bf[0:r, :], ALU.add)
                    V.tensor_copy(vb_tok[0:r, i, :], bank[4 + i][0:r, 0:128]).then_inc(vb_copied, 1)
                split_low(v + 3 + SPL)
                dve.wait_ge(vb_copied, 4 * (l + 1))
                V.scalar_tensor_tensor(le[:, :, :], lz[:, :, :], -1.0, lz[:, :, :], ALU.mult, ALU.max).then_inc(za_ready, 1)
                dve.wait_ge(zl_ready, l + 1)
                V.scalar_tensor_tensor(lf[:, :, :], lz[:, :, :], 0.0, le[:, :, :], ALU.min, ALU.subtract).then_inc(logf_ready, 1)
                dve.wait_ge(logf_ready, l + 1)
                V.tensor_tensor(lbd[:, :].rearrange("p (b h) -> p b h", b=BS), bmask.rearrange("p (b h) -> p b h", b=BS),
                                lf[:, 3:4, :].to_broadcast([P, BS, H]), ALU.mult).then_inc(lbd_ready, 1)
                for x in range(-1, NCOL):
                    if x + 1 < NCOL:
                        split_low(AT["col", l] + x + 1 + SPL)
                    if x < 0:
                        continue
                    c = COLS[x]
                    i = l * NCOL + x
                    dve.wait_ge(colroot_ready, i + 1)
                    V.reciprocal(rs[:, x % 2, :], rt[:, x % 2, :]).then_inc(colrecip_ready, 1)
                    dve.wait_ge(colrecip_ready, i + 1)
                    g = (gq[:, 0:1] if c < 4 else par[:, PC["kn_a"]:PC["kn_a"] + 1] if c < 8 else
                         par[:, PC["kn_b"]:PC["kn_b"] + 1] if c == 8 else gq[:, 1:2])
                    V.scalar_tensor_tensor(qk[:, c, :], bank[x % 4][:, 0:T], g, rs[:, x % 2, :],
                                           ALU.mult, ALU.mult).then_inc(col_done, 1)
                dve.wait_ge(nf_done, 2 * l + 1)
                V.tensor_copy(NFp[0:H, :], bank[6][0:H, 0:TP]).then_inc(nf_copied, 1)
                dve.wait_ge(nf_done, 2 * l + 2)
                V.tensor_copy(NFs[0:64, :], bank[7][0:64, 0:384]).then_inc(nf_copied, 1)
                if l == 0:
                    dve.wait_ge(tab2_loaded, 48)

                def bias_max(u):
                    n, rows, keys = u["n"], u["rows"], u["keys"]
                    S = bank[SB[n % 4]]
                    dve.wait_ge(scores_ready, n + 1)
                    if u["kind"] == "fox":
                        w = rows if u["what"] == "prompt" else P
                        m = cmask[0:rows, 0:w] if u["what"] == "prompt" else smask[:, u["s"], :]
                        V.tensor_tensor(S[0:rows, keys - w:keys], S[0:rows, keys - w:keys], m, ALU.add).then_inc(biased, 1)
                    else:
                        col = 2 if u["what"] == "both" else 3 if u["what"] == "sample" else u["h2"]
                        V.scalar_tensor_tensor(S[0:rows, 0:keys], dist[0:rows, u["d0"]:u["d0"] + keys],
                                               negslope[0:rows, u["pr"], col:col + 1], S[0:rows, 0:keys],
                                               ALU.mult, ALU.add).then_inc(biased, 1)
                    dve.wait_ge(biased, n + 1)
                    if u["kind"] == "fox":
                        V.tensor_reduce(small[0:rows, 4 + n % 4:5 + n % 4], S[0:rows, 0:keys], AX_X, ALU.max,
                                        negate=True).then_inc(negmax_ready, 1)
                    else:
                        V.tensor_reduce(small[0:rows, n % 4:n % 4 + 1], S[0:rows, 0:keys], AX_X, ALU.max,
                                        negate=True).then_inc(max_ready, 1)
                        dve.wait_ge(max_ready, n - (u["l"] + 1) * 8 * NPAIR + 1)
                        V.tensor_tensor(small[0:rows, 4 + n % 4:5 + n % 4], small[0:rows, n % 4:n % 4 + 1],
                                        nsink_col(u), ALU.min).then_inc(negmax_ready, 1)

                def denominator(u):
                    n, rows = u["n"], u["rows"]
                    dve.wait_ge(exp_ready, n + 1)
                    den = small[0:rows, 8 + n % 4:9 + n % 4]
                    if u["kind"] == "swa":
                        V.tensor_tensor(small[0:rows, 20 + n % 4:21 + n % 4], den, small[0:rows, 16 + n % 4:17 + n % 4],
                                        ALU.add).then_inc(den_ready, 1)
                        dve.wait_ge(den_ready, n - (u["l"] + 1) * 8 * NPAIR + 1)
                        den = small[0:rows, 20 + n % 4:21 + n % 4]
                    V.reciprocal(small[0:rows, 12 + n % 4:13 + n % 4], den).then_inc(recipd_ready, 1)

                def take_y(g):
                    dve.wait_ge(yH_ready, g + 1)
                    k = g % NG
                    smp = bank[1][:, 0:256].rearrange("p (b h q) -> p b h q", b=BS, h=2)
                    V.tensor_tensor(aL[:, k, 0:TP], bank[0][:, 0:TP], aH[:, k, 0:TP].bitcast(F32), ALU.subtract)
                    for h2 in range(2):
                        hs = slice(64 * h2, 64 * h2 + 64)
                        last = V.tensor_tensor(aL[hs, k, TP:T].rearrange("p (b q) -> p b q", b=BS), smp[hs, :, h2, :],
                                               aH[hs, k, TP:T].bitcast(F32).rearrange("p (b q) -> p b q", b=BS),
                                               ALU.subtract)
                    last.then_inc(y_copied, 1)

                units = UNITS[l * NU:(l + 1) * NU]
                taken = l * NG
                for i in range(NU + LAG + 2):
                    if i < NU:
                        bias_max(units[i])
                    if 1 <= i < NU + 1:
                        denominator(units[i - 1])
                    if taken < (l + 1) * NG and last_of_g[taken] + LAG + 1 == l * NU + i:
                        take_y(taken)
                        taken += 1
                for m in range(KD):
                    p = AT["wo", l] + m
                    dve.wait_ge(piece_done, p + 1)
                    V.tensor_tensor(hT[:, m, :], hT[:, m, :], bank[m % 2][:, 0:T], ALU.add).then_inc(h_added, 1)
                    if p + SPL < len(WIDTH):
                        split_low(p + SPL)
                dve.wait_ge(h_added, (l + 1) * KD)
                dve.wait_ge(out_done, 16 * OUTS_PER_LAYER * (l + 1))
                norm(l, 1)
                if l % 2 == 0:
                    dve.wait_ge(aL_ready, (2 * l + 2) * KD)

                    def chunk(c, it=None):
                        p = AT["gu"] + 2 * c
                        split_low(p + SPL, it, 2 * CBODY)
                        dve.wait_ge(silu_ready, count(c + 1, it, CBODY))
                        dve.wait_ge(piece_done, count(p + 2, it, 2 * CBODY))
                        up = bank[2 * (c % 2) + 1][:, 0:T]
                        if it is None:
                            high, low = hidH[:, c * T:c * T + T], hidL[:, c * T:c * T + T]
                        else:
                            at = bass.ds((it * CBODY + c) * T, T)
                            high, low = hidH[:, at], hidL[:, at]
                        V.tensor_tensor(high, sq[:, c % 2, :], up, ALU.mult).then_inc(hH_ready, 1)
                        V.tensor_tensor(rt[:, c % 2, :], sq[:, c % 2, :], up, ALU.mult).then_inc(htmp_ready, 1)
                        split_low(p + 1 + SPL, it, 2 * CBODY)
                        dve.wait_ge(hH_ready, count(c + 1, it, CBODY))
                        dve.wait_ge(htmp_ready, count(c + 1, it, CBODY))
                        V.tensor_tensor(low, rt[:, c % 2, :], high.bitcast(F32), ALU.subtract).then_inc(hid_ready, 1)
                    for c in range(LOOP0):
                        chunk(c)
                    with dve.Fori(0, (LOOP1 - LOOP0) // CBODY) as i:
                        for c in range(LOOP0, LOOP0 + CBODY):
                            chunk(c, i)
                    for c in range(LOOP1, FCH):
                        chunk(c)
                    for m in range(KD):
                        split_low(AT["down"] + 2 * m + SPL)
                        dve.wait_ge(piece_done, AT["down"] + 2 * m + 2)
                        V.tensor_tensor(hT[:, m, :], hT[:, m, :], bank[4 + m % 4][:, 0:T], ALU.add).then_inc(h_added2, 1)
                        split_low(AT["down"] + 2 * m + 1 + SPL)
                    dve.wait_ge(h_added2, KD)

            steps = [0]

            def step(ins):
                steps[0] += 1
                ins.then_inc(route, 1)
                dve.wait_ge(route, steps[0])

            def b4(ap, shape):
                return ap.to_broadcast(shape)

            dve.wait_ge(out_done, 16 * DEPTH * OUTS_PER_LAYER)
            br = par[:, PC["b_r"]:PC["b_r"] + E]
            for i, (t0, r) in enumerate(TT):
                dve.wait_ge(logits_done, len(TT))
                step(V.tensor_tensor(lg[0:r, i, :], bank[5][0:r, E * i:E * i + E], br[0:r, :], ALU.add))
            lge = lg[:, :, :].unsqueeze(3).to_broadcast([P, 4, E, E])
            lgo = lg[:, :, :].unsqueeze(2).to_broadcast([P, 4, E, E])
            c1 = cmp1[:, :, :].rearrange("p t (e o) -> p t e o", e=E)
            c2 = cmp2[:, :, :].rearrange("p t (e o) -> p t e o", e=E)
            step(V.tensor_tensor(c1, lgo, lge, ALU.is_gt))
            step(V.tensor_tensor(c2, lgo, lge, ALU.is_equal))
            step(V.tensor_tensor(cmp2[:, :, :], cmp2[:, :, :], first.unsqueeze(1).to_broadcast([P, 4, 64]), ALU.mult))
            step(V.tensor_tensor(cmp1[:, :, :], cmp1[:, :, :], cmp2[:, :, :], ALU.add))
            step(V.tensor_reduce(rank[:, :, :], c1, AX_X, ALU.add))
            step(V.tensor_scalar(mem[:, :, :], rank[:, :, :], 1.5, None, ALU.is_lt))
            V.tensor_tensor(memv[:, :, :], mem[:, :, :], valid.unsqueeze(2).to_broadcast([P, 4, E]), ALU.mult).then_inc(memv_ready, 1)
            for i, (t0, r) in enumerate(TT):
                dve.wait_ge(ctT_done, 2 * i + 2)
                if i >= 2:
                    dve.wait_ge(ctk_stored[i % 2], 16 * (i // 2))
                V.tensor_copy(ctk[0:r, i % 2, 512:1024], bank[2 * (i % 2) + 1][0:r, :]).then_inc(ctkb_copied, 1)
            step(V.tensor_scalar(sel1[:, :, :], rank[:, :, :], 0.5, None, ALU.is_lt))
            step(V.tensor_tensor(sel2[:, :, :], mem[:, :, :], sel1[:, :, :], ALU.subtract))
            step(V.tensor_reduce(rden[:, 0:4], lg[:, :, :], AX_X, ALU.max))
            V.tensor_tensor(tmp8[:, :, :], lg[:, :, :], rden[:, 0:4].unsqueeze(2).to_broadcast([P, 4, E]),
                            ALU.subtract).then_inc(pe_in, 1)
            dve.wait_ge(pe_exp, 1)
            step(V.tensor_tensor(gate[:, :, :], gate[:, :, :], mem[:, :, :], ALU.mult))
            step(V.tensor_reduce(rden[:, 0:4], gate[:, :, :], AX_X, ALU.add))
            step(V.reciprocal(rden[:, 4:8], rden[:, 0:4]))
            step(V.tensor_tensor(gate[:, :, :], gate[:, :, :], rden[:, 4:8].unsqueeze(2).to_broadcast([P, 4, E]), ALU.mult))
            for w, sel in enumerate((sel1, sel2)):
                step(V.tensor_tensor(tmp8[:, :, :], gate[:, :, :], sel[:, :, :], ALU.mult))
                step(V.tensor_reduce(gcol[:, 4 * w:4 * w + 4], tmp8[:, :, :], AX_X, ALU.add))
            dve.wait_ge(pos_done, 1)
            step(V.tensor_reduce(cnt[0:1, 0:1], bank[6][0:1, 0:E], AX_X, ALU.max))
            V.tensor_copy(cnt_i[0:1, 0:1], cnt[0:1, 0:1]).then_inc(cnt_ready, 1)
            pos = bank[7][:, 0:4 * E].rearrange("p (t e) -> p t e", t=4)
            step(V.tensor_scalar(dstv[:, :, :], rank[:, :, :], 0.5, None, ALU.is_gt))
            step(V.tensor_tensor(dstv[:, :, :], dstv[:, :, :], tok2.unsqueeze(2).to_broadcast([P, 4, E]), ALU.add))
            step(V.tensor_scalar(posm[:, :, :], memv[:, :, :], -1e6, 1e6, ALU.mult, ALU.add))
            step(V.tensor_tensor(posm[:, :, :], posm[:, :, :], pos, ALU.add))
            dve.wait_ge(cnt_ready, 1)
            most = dve.value_load(cnt_i[0:1, 0:1], min_val=0, max_val=T)
            with dve.Fori(0, MAXR) as r:
                with dve.If(most > r * P):
                    for e in range(E):
                        if e >= 2:
                            dve.wait_ge(oneh_used, r * E + (e - 1))
                        V.tensor_tensor(onehot[:, e % 2, :].rearrange("p (t s) -> p t s", t=4),
                                        iota.unsqueeze(1).to_broadcast([P, 4, P]),
                                        posm[:, :, e:e + 1].to_broadcast([P, 4, P]), ALU.is_equal).then_inc(oneh_ready, 1)
                    dve.wait_ge(oneh_ready, r * E + E)
                    V.tensor_scalar(posm[:, :, :], posm[:, :, :], -float(P), None, ALU.add).then_inc(iota_ready, 1)
                    dve.wait_ge(iota_ready, r + 1)
                    dve.wait_ge(oneh_used, r * E + E)
                    V.tensor_copy(slot_tok[:, 0:E], bank[6][:, 0:E])
                    V.tensor_scalar(slot_tok[:, E:2 * E], bank[6][:, E:2 * E], float(OOB), None, ALU.add).then_inc(sidx_ready, 1)

                    def copy_tokens(n, hf):
                        dve.wait_ge(xTH_ready, n * 2 + (hf + 1))
                        V.tensor_tensor(xTL[:, 4 * hf:4 * hf + 4, :].rearrange("p k t -> p (k t)"), bank[7][:, :],
                                        xTH[:, 4 * hf:4 * hf + 4, :].bitcast(F32).rearrange("p k t -> p (k t)"),
                                        ALU.subtract).then_inc(xTL_ready, 1)
                    copy_tokens(r * E, 0)
                    copy_tokens(r * E, 1)
                    with dve.Fori(0, E) as e:
                        n = r * E + e
                        M = AT["moe"] + SPL

                        def copy_hidden(j):
                            dve.wait_ge(mTH_ready, n * 4 + (j + 1))
                            c0, w = groups[j][0], len(groups[j])
                            V.tensor_tensor(mTL[:, c0:c0 + w, :].rearrange("p c t -> p (c t)"), bank[0 if j == 3 else 4][:, 0:P * w],
                                            mTH[:, c0:c0 + w, :].bitcast(F32).rearrange("p c t -> p (c t)"),
                                            ALU.subtract).then_inc(mTL_ready, 1)
                        for j in range(MBLK):
                            for x in range(3):
                                split_low(M + 4 * j + x, n, MPER)
                            dve.wait_ge(msilu_ready, n * 4 + (j + 1))
                            dve.wait_ge(piece_done, count(AT["moe"] + 4 * j + 4, n, MPER))
                            V.tensor_tensor(mh[:, MB * j:MB * j + MB], sg[:, j % 2, :], bank[2 * (j % 2) + 1][:, 0:MB],
                                            ALU.mult).then_inc(mh_ready, 1)
                            split_low(M + 4 * j + 3, n, MPER)
                            if j:
                                copy_hidden(j - 1)
                        with dve.If(e < E - 1):
                            copy_tokens(n + 1, 0)
                        with dve.Else():
                            dve.wait_ge(my_stored, n * 16)
                            dve.sem_inc(dve_passed, 1)
                        copy_hidden(3)
                        for x in range(16, 20):
                            split_low(M + x, n, MPER)
                        with dve.If(e < E - 1):
                            copy_tokens(n + 1, 1)
                        split_low(M + 20, n, MPER)
                        with dve.If(e < E - 1):
                            for x in range(21, 24):
                                split_low(M + x, n, MPER)
                        dve.wait_ge(piece_done, count(AT["moe"] + 24, n, MPER))
                        V.tensor_copy(yev[:, 512:1024], bank[6][:, :]).then_inc(my_copied, 1)
                    dve.wait_ge(my_stored, (r * E + E) * 16)
                    with dve.If(most > r * P + P):
                        for x in range(21, 24):
                            split_low(AT["moe"] + SPL + x, r * E + (E - 1), MPER)
            for i, (t0, r) in enumerate(TT):
                dve.wait_ge(hT_done, i + 1)
                dve.wait_ge(y12_loaded[i % 2], 16 * (i // 2 + 1))
                if i >= 2:
                    dve.wait_ge(y_out[i % 2], 16 * (i // 2))
                for hf in range(2):
                    V.scalar_tensor_tensor(yo[0:r, i % 2, 512 * hf:512 * hf + 512], y12[0:r, i % 2, 512 * hf:512 * hf + 512],
                                           gcol[0:r, i:i + 1], bank[2 * (i % 2) + hf][0:r, :], ALU.mult, ALU.add
                                           ).then_inc(y_half, 1)
                dve.wait_ge(y_half, 2 * i + 2)
                V.scalar_tensor_tensor(yo[0:r, i % 2, :], y12[0:r, i % 2, D:2 * D], gcol[0:r, 4 + i:5 + i], yo[0:r, i % 2, :],
                                       ALU.mult, ALU.add).then_inc(y_ready, 1)


def kernel(**inputs):
    import concourse.bacc as bacc
    from concourse.bass_utils import run_bass_kernel_spmd

    x = {k: np.asarray(v) for k, v in inputs.items()}
    c = np.ascontiguousarray

    def tiles(w):
        return c(w.reshape(-1, P, w.shape[-1]).transpose(1, 0, 2)).reshape(P, -1)

    A = H * HD
    tok = np.concatenate([x["meta_tokens"], x["x_prompt"][0], x["x_sample"].reshape(TSM, D)], axis=0)
    params, vf, col, wo = [], [], [], []
    p = np.arange(P)
    sinks = x["sinks"]
    for l in range(DEPTH):
        w = x["w_in"][l]
        q_a, k_a, v_a, f_a, q_b, k_b, v_b = np.split(w, [A, 2 * A, 3 * A, 3 * A + H, 4 * A + H, 4 * A + H + P], axis=1)
        w648 = np.concatenate([v_a, v_b, f_a], axis=1)
        vf.append(np.stack([tiles(w648[2 * P * i:2 * P * i + 2 * P]) for i in range(4)]))
        pair_cols = [np.r_[HD * j:HD * j + HD, HD * (4 + j):HD * (4 + j) + HD] for j in range(NPAIR)]
        heads = [tiles(q_a[:, P * i:P * i + P]) for i in range(4)] + [tiles(k_a[:, P * i:P * i + P]) for i in range(4)]
        heads += [tiles(k_b)] + [tiles(q_b[:, pc]) for pc in pair_cols]
        col.append(np.stack([heads[i] for i in COLS]))
        rows = np.concatenate([np.arange(A)] + [A + pc for pc in pair_cols])
        w_o = x["w_out"][l][rows]
        wo.append(np.stack([tiles(w_o[:, P * m:P * m + P]) for m in range(KD)]))
        sk = np.zeros((P, NPAIR, 4), sinks.dtype)
        for j in range(NPAIR):
            sk[:, j, 0], sk[:, j, 1] = sinks[l, j], sinks[l, 4 + j]
            sk[:, j, 2] = sinks[l][np.where(p < 64, j, 4 + j)]
            sk[:, j, 3] = sinks[l][np.where((p // 16) % 2 == 0, j, 4 + j)]
        cols = [x["g_attn"][l].reshape(KD, P).T, x["g_ffn"][l].reshape(KD, P).T]
        cols += [np.tile(x[n][l], 2)[:, None] for n in ("qn_a", "kn_a", "qn_b", "kn_b")]
        cols += [np.tile(x["b_f"][l], (P, 1)), sk.reshape(P, -1), np.tile(x["b_router"][0], (P, 1))]
        params.append(np.concatenate(cols, axis=1))
    gu = np.stack([tiles(x[n][0][:, P * i:P * i + P]) for i in range(FCH) for n in ("w_gate", "w_up")])
    wd = np.stack([tiles(x["w_down"][0][FF // 2 * hf:FF // 2 * (hf + 1), P * m:P * m + P]) for m in range(KD)
                   for hf in range(2)])
    egu = np.stack([x[n][0].reshape(E, 2, KD // 2, P, MBLK, MB).transpose(0, 4, 1, 3, 2, 5) for n in ("we_gate", "we_up")],
                   axis=2).reshape(E * 16, P, MGW)
    ed = x["we_down"][0].reshape(E, MCH, P, 4, 256).transpose(0, 3, 2, 1, 4)
    ed0, ed1 = (c(a).reshape(E * 4, P, -1) for a in (ed[:, :, :, :MD0], ed[:, :, :, MD0:]))

    kf, vf_c = x["cache_fox_k"], x["cache_fox_v"]
    ck = c(kf.reshape(DEPTH, BS, PAST, NPAIR, P).transpose(0, 3, 4, 1, 2)).reshape(DEPTH, NPAIR, P, -1)
    cv = c(vf_c.reshape(DEPTH, BS, 2, P, NPAIR, P).transpose(0, 4, 3, 1, 2, 5)).reshape(DEPTH, NPAIR, P, -1)
    cl = c(x["cache_fox_logf"].reshape(DEPTH, BS, 2, P, H).transpose(0, 3, 2, 1, 4)).reshape(DEPTH, P, -1)
    cks = c(x["cache_swa_k"].reshape(DEPTH, BS, P, P).transpose(0, 3, 1, 2)).reshape(DEPTH, P, -1)
    cvs = c(x["cache_swa_v"].reshape(DEPTH, BS, P, P).transpose(0, 2, 1, 3)).reshape(DEPTH, P, -1)
    arrays = {
        "xT": c(tok.T.reshape(KD, P, T).transpose(1, 0, 2)), "params": np.stack(params),
        "w_vf": np.stack(vf), "w_col": np.stack(col), "w_o": np.stack(wo), "w_gu": gu, "w_d": wd,
        "w_egu": egu, "w_ed0": ed0, "w_ed1": ed1, "w_r": tiles(x["w_router"][0]),
        "ck_fox": ck, "cv_fox": cv, "clf": cl, "ck_swa": cks, "cv_swa": cvs, "tables": _TABLES, "selt": _SEL,
    }
    nc = bacc.Bacc("TRN2", target_bir_lowering=False, num_devices=1)
    args = {}
    for name, a in arrays.items():
        arrays[name] = c(a)
        args[name] = nc.dram_tensor(name, a.shape, mybir.dt.from_np(a.dtype), kind="ExternalInput").ap()
    outs = {"o_kfox": (DEPTH, NPAIR, P, T), "o_vfox": (DEPTH, T, A), "o_lf": (DEPTH, T, H), "o_kswa": (DEPTH, P, T),
            "o_vswa": (DEPTH, T, P), "o_y": (T, D)}
    for name, shape in outs.items():
        args[name] = nc.dram_tensor(name, shape, F32, kind="ExternalOutput").ap()
    build(nc, **args)
    r = run_bass_kernel_spmd(nc, [arrays], core_ids=[0]).results[0]
    y = r["o_y"]
    kf = r["o_kfox"].reshape(DEPTH, H, HD, T).transpose(0, 3, 1, 2)
    vf_o = r["o_vfox"].reshape(DEPTH, T, H, HD)
    ks = r["o_kswa"].reshape(DEPTH, 2, HD, T).transpose(0, 3, 1, 2)
    vs = r["o_vswa"].reshape(DEPTH, T, 2, HD)
    lf = r["o_lf"]
    W = 128

    def prompt(a):
        return c(a[:, None, :TP])

    def sample(a):
        return c(a[:, TP:].reshape((DEPTH, BS, TSEQ) + a.shape[2:]))

    return (c(y[NMETA:TP][None]), c(y[TP:].reshape(BS, TSEQ, D)), prompt(kf), prompt(vf_o), prompt(lf),
            c(ks[:, None, TP - W:TP]), c(vs[:, None, TP - W:TP]), sample(kf), sample(vf_o), sample(lf),
            sample(ks), sample(vs))
```

```python
from contextlib import ExitStack

import numpy as np

import concourse.bass as bass
from concourse import mybir

ALU = mybir.AluOpType
ACT = mybir.ActivationFunctionType
F32 = mybir.dt.float32
F32R = mybir.dt.float32r
U32 = mybir.dt.uint32
I32 = mybir.dt.int32
AX_X = mybir.AxisListType.X

P = 128
DEPTH = 2
D = 1024
KD = D // P
HD = 64
NMETA, SEQ = 16, 256
TP = NMETA + SEQ
BS, TSEQ = 8, 16
TSM = BS * TSEQ
T = TP + TSM
PAST = 256
CHUNK = 64
H = 8
NPAIR = 4
FF = 2816
FCH = FF // P
E = 8
MFF = 1408
MCH = MFF // P
MBLK = 4
MB = MFF // MBLK
EPS = 1e-6
BIG = 1e33
OOB = 8192
NEG = -1e30

RAW = 4
SPL = 3
PIECE = 6 * 256
MD0 = 5

QT = [(0, 128), (128, 128), (256, 16), (TP, TSM)]
TT = [(0, 128), (128, 128), (256, 128), (384, 16)]
TLAST = [TT[3], TT[0], TT[1], TT[2]]
YB = [(0, 1), (2, 3), (4, 7), (0, 1)]
MAXR = -(-T // P)

PC = {}
_o = 0
for _n, _w in (("g_attn", KD), ("g_ffn", KD), ("qn_a", 1), ("kn_a", 1), ("qn_b", 1), ("kn_b", 1), ("b_f", H),
               ("sink", 16), ("b_r", E)):
    PC[_n] = _o
    _o += _w
NPAR = _o

DA, DB, DC, DS = 0, 80, 80 + 208, 80 + 208 + TP
NDIST = DS + 2 * 256


def shape_tables():
    f = np.float32
    ident = np.eye(P, dtype=f)
    pm = np.zeros((P, P), f)
    pm[:HD, :HD] = 1.0 / HD
    pm[HD:, HD:] = 1.0 / HD
    p = np.arange(P)
    t = np.arange(TP)
    negtri = np.zeros((P, 3, TP), f)
    for i in range(3):
        negtri[:, i, :] = -1.0 * ((128 * i + p)[:, None] <= t[None, :])
    b, q = p // TSEQ, p % TSEQ
    newtri = -1.0 * ((b[:, None] == b[None, :]) & (q[:, None] <= q[None, :]))
    cmask = np.where(p[None, :] > p[:, None], NEG, 0.0)
    row_b4, row_h, row_q = p // 32, (p // 16) % 2, p % 16
    smask = np.zeros((P, 2, P), f)
    dist = np.full((P, NDIST), BIG, f)
    chunk = (t + CHUNK - NMETA) // CHUNK

    def prompt_dist(rows, keys):
        ok = (chunk[keys][None] <= chunk[rows][:, None]) & (chunk[keys][None] >= chunk[rows][:, None] - 2)
        return np.where(ok, np.abs(rows[:, None] - keys[None]), BIG)
    dist[:80, DA:DA + 80] = prompt_dist(t[:80], t[:80])
    dist[:, DB:DB + 208] = prompt_dist(t[80:208], t[:208])
    dist[:, DC:DC + TP] = prompt_dist(np.concatenate([t[208:], t[208:]]), t)
    for s in range(2):
        same = (4 * s + row_b4)[:, None] == b[None, :]
        smask[:, s, :] = np.where(same & (q[None, :] <= row_q[:, None]), 0.0, NEG)
        dist[:, DS + 256 * s:DS + 256 * s + 128] = 128 + row_q[:, None] - p[None, :]
        dist[:, DS + 256 * s + 128:DS + 256 * s + 256] = np.where(same, np.abs(row_q[:, None] - q[None, :]), BIG)
    negslope = np.zeros((P, NPAIR, 4), f)
    for j in range(NPAIR):
        lo, hi = -2.0 ** -(j + 1), -2.0 ** -(j + 5)
        negslope[:, j, 0] = lo
        negslope[:, j, 1] = hi
        negslope[:, j, 2] = np.where(p < 64, lo, hi)
        negslope[:, j, 3] = np.where(row_h == 0, lo, hi)
    bmask = (np.arange(TSM)[:, None] // TSEQ == np.arange(64)[None, :] // 2 % BS).astype(f)
    tri_strict = (p[:, None] < p[None, :]).astype(f)
    iota = np.broadcast_to(p[None, :], (P, P))
    first = np.broadcast_to((np.arange(E)[None, :] < np.arange(E)[:, None]).reshape(1, 64), (P, 64))
    valid = ((np.arange(4) * P)[None, :] + p[:, None] < T)
    tokid = (np.arange(4) * P)[None, :] + p[:, None]
    parts = [("ident", ident), ("pm", pm), ("ones", np.ones((P, P))),
             ("mean", np.full((P, P), 1.0 / D)),
             ("negtri", negtri), ("newtri", newtri), ("cmask", cmask), ("smask", smask), ("dist", dist),
             ("negslope", negslope), ("bmask", bmask), ("tris", tri_strict), ("iota", iota), ("first", first),
             ("valid", valid), ("tokid", tokid), ("tok2", 2 * tokid + 1)]
    off, cols, at = {}, [], 0
    for name, a in parts:
        a = np.asarray(a, f).reshape(P, -1)
        off[name] = (at, a.shape[1])
        cols.append(a)
        at += a.shape[1]
    return np.concatenate(cols, axis=1), off


_TABLES, TO = shape_tables()
NTAB = _TABLES.shape[1]
NTAB_ATT = TO["tris"][0]
NTAB_NORM = TO["negtri"][0]


def unit_plan():
    units = []
    for l in range(DEPTH):
        for kind in ("swa", "fox"):
            for pr in range(NPAIR):
                for s in range(2):
                    units.append(dict(l=l, kind=kind, pr=pr, what="sample", h2=0, s=s, rows=128,
                                      keys=384 if kind == "fox" else 256, d0=DS + 256 * s))
                units[-1]["last_sample"] = True
                for h2 in range(2):
                    tiles = [(0, 128, 128), (128, 128, 256), (256, 16, 272)] if kind == "fox" else \
                            [(0, 80, 80), (80, 128, 208)]
                    for q0, rows, keys in tiles:
                        units.append(dict(l=l, kind=kind, pr=pr, what="prompt", h2=h2, q0=q0, rows=rows, keys=keys,
                                          d0=DA if q0 == 0 else DB))
                if kind == "swa":
                    units.append(dict(l=l, kind=kind, pr=pr, what="both", h2=0, q0=208, rows=128, keys=TP, d0=DC))
                units[-1]["last"] = True
    g = 0
    for n, u in enumerate(units):
        u["n"], u["g"] = n, g
        g += u.get("last", False)
    return units


UNITS = unit_plan()
NU = len(UNITS) // DEPTH
NG = 2 * NPAIR
NCOL = NPAIR * 3 + 1


COLS = [0, 4, 1, 5, 2, 6, 3, 7, 8, 9, 10, 11, 12]
CBODY = 6
LOOP0, LOOP1 = CBODY, 3 * CBODY
OUTS_PER_LAYER = 17
SQ_PER_LAYER = 2 * KD + NCOL
LAG = 4

VWID, DWID, MGW = 2 * 648, FCH // 2 * P, KD // 2 * MB
WIDTH, AT = [], {}
for _l in range(DEPTH):
    AT["v", _l] = len(WIDTH)
    WIDTH += [VWID] * 4
    AT["col", _l] = len(WIDTH)
    WIDTH += [KD * P] * NCOL
    AT["wo", _l] = len(WIDTH)
    WIDTH += [KD * P] * KD
    if _l % 2 == 0:
        AT["gu"] = len(WIDTH)
        WIDTH += [KD * P] * (2 * FCH)
        AT["down"] = len(WIDTH)
        WIDTH += [DWID] * (2 * KD)
AT["moe"] = len(WIDTH)
MPRE = RAW + SPL
MPER = 24
MWIDTH = [MGW] * 16 + [MD0 * 256, (MCH - MD0) * 256] * 4
WIDTH += MWIDTH + MWIDTH[:MPRE]


def build(nc, xT, params, w_vf, w_col, w_o, w_gu, w_d, w_egu, w_ed0, w_ed1, w_r, ck_fox, cv_fox, clf,
          ck_swa, cv_swa, tables, o_kfox, o_vfox, o_lf, o_kswa, o_vswa, o_y):
    with ExitStack() as ctx:
        def sb(name, shape, dt=F32):
            return ctx.enter_context(nc.sbuf_tensor(name, shape, dt))

        def sem(name):
            return ctx.enter_context(nc.semaphore(name))

        bank = [ctx.enter_context(nc.psum_tensor(f"bank{i}", [P, 512], F32)) for i in range(8)]
        c_rows = nc.dram_tensor("c_rows", [T, D], F32).ap()
        nf_rows = nc.dram_tensor("nf_rows", [DEPTH, H, TP], F32).ap()
        nf_seqs = nc.dram_tensor("nf_seqs", [DEPTH, BS * H, 384], F32).ap()
        y_rows = nc.dram_tensor("y_rows", [2 * T + 1, D], F32).ap()

        AREA = 2 * FCH * T
        area_at = nc.sbuf_base + (-nc.sbuf_base) % 64
        sb("area_fence", [P, AREA + 16])

        def place(name, o, shape, dt=F32):
            n = int(np.prod(shape[1:]))
            assert o + n <= AREA, (name, o + n)
            return nc.alloc_sbuf_tensor_at(name, shape, dt, offset=area_at + 4 * o), o + n

        hT = sb("hT", [P, KD, T])
        aH = sb("aH", [P, KD, T], F32R)
        aL = sb("aL", [P, KD, T], F32R)
        raw = sb("raw", [P, RAW, PIECE])
        WH = sb("WH", [P, SPL, PIECE], F32R)
        WL = sb("WL", [P, SPL, PIECE], F32R)
        tab = sb("tab", [P, NTAB])
        nf_smp = sb("nf_smp", [P, 2, 384])
        par = sb("par", [P, NPAR])
        gq = sb("gq", [P, 2])
        nsink = sb("nsink", [P, 16])
        sq = sb("sq", [P, 2, T])
        rt = sb("rt", [P, 2, T])
        rs = sb("rs", [P, 2, T])
        prob = sb("prob", [P, 4, 384])
        probT = sb("probT", [P, 3, 384])
        small = sb("small", [P, 32])
        eps_col = sb("eps_col", [P, 1])
        lf = sb("lf", [P, 4, H])
        lz = sb("lz", [P, 4, H])
        le = sb("le", [P, 4, H])

        aT, _ = place("aT", 0, [P, KD, T])
        qk, _o = place("qk", 0, [P, NCOL, T])
        qbd, _o = place("qbd", _o, [P, 8, 256])
        v_tok, _o = place("v_tok", _o, [P, 4, 512])
        vb_tok, _o = place("vb_tok", _o, [P, 4, P])
        NFp, _o = place("NFp", _o, [P, TP])
        NFs, _o = place("NFs", _o, [P, 384])
        clf_sb, _o = place("clf_sb", _o, [P, 2, 64])
        lbd, _o = place("lbd", _o, [P, 64])
        kc, _o = place("kc", _o, [P, 2048])
        vc, _o = place("vc", _o, [P, 2048])
        ksw, _o = place("ksw", _o, [P, 1024])
        vsw, _o = place("vsw", _o, [P, 1024])
        nf_pmt, _o = place("nf_pmt", _o, [P, 2 * TP])
        osm, _o = place("osm", _o, [P, 256])
        hidH, _o = place("hidH", 0, [P, FCH * T], F32R)
        hidL, _o = place("hidL", _o, [P, FCH * T], F32R)
        xg, _o = place("xg", KD * T, [P, D])
        sg, _o = place("sg", _o, [P, 2, MB])
        mh, _o = place("mh", _o, [P, MFF])
        yev, _o = place("yev", _o, [P, D])
        lgT, _o = place("lgT", _o, [E, T])
        onehot, _o = place("onehot", _o, [P, 2, 512], F32R)
        cmp1, _o = place("cmp1", _o, [P, 4, 64])
        cmp2, _o = place("cmp2", _o, [P, 4, 64])
        ctk, _ = place("ctk", _o, [P, 4, D])
        xTH, _o = place("xTH", _o, [P, KD, P], F32R)
        xTL, _o = place("xTL", _o, [P, KD, P], F32R)
        mTH, _o = place("mTH", _o, [P, MCH, P], F32R)
        mTL, _o = place("mTL", _o, [P, MCH, P], F32R)
        y12, _o = place("y12", 0, [P, 4, 2 * D])
        yo, _o = place("yo", _o, [P, 4, D])
        wr = sb("wr", [P, KD, E])
        lg = sb("lg", [P, 4, E])
        rank = sb("rank", [P, 4, E])
        gate = sb("gate", [P, 4, E])
        mem = sb("mem", [P, 4, E])
        memv = sb("memv", [P, 4, E])
        sel1 = sb("sel1", [P, 4, E])
        sel2 = sb("sel2", [P, 4, E])
        posm = sb("posm", [P, 4, E])
        tmp8 = sb("tmp8", [P, 4, E])
        rden = sb("rden", [P, 8])
        gcol = sb("gcol", [P, 8])
        slot_of = sb("slot_of", [P, 4, E, 2], F32R)
        empty = sb("empty", [P, E])
        slot_tok = sb("slot_tok", [P, 2 * E], U32)
        gidx = sb("gidx", [P, 1], U32)
        didx = sb("didx", [P, 1], U32)
        cnt = sb("cnt", [1, 8])
        cnt_i = sb("cnt_i", [1, 2], I32)

        def table(name, *dims):
            o, n = TO[name]
            v = tab[:, o:o + n]
            if len(dims) == 2:
                v = v.rearrange("p (a b) -> p a b", a=dims[0])
            return v

        ident, pm, ones, mean = (table(x) for x in ("ident", "pm", "ones", "mean"))
        negtri = table("negtri", 3, TP)
        negones = negtri[:, 0, P:2 * P]
        newtri, cmask = table("newtri"), table("cmask")
        smask = table("smask", 2, P)
        dist = table("dist")
        negslope = table("negslope", NPAIR, 4)
        bmask, tris, iota = table("bmask"), table("tris"), table("iota")
        first, valid, tokid, tok2 = table("first"), table("valid"), table("tokid"), table("tok2")

        raw_full = [sem(f"raw_full{i}") for i in range(RAW)]
        hi_ready, lo_ready, piece_done = sem("hi_ready"), sem("lo_ready"), sem("piece_done")
        aH_ready, aL_ready, yH_ready = sem("aH_ready"), [sem("aL_even"), sem("aL_odd")], sem("yH_ready")
        htmp_ready, hH_ready = sem("htmp_ready"), sem("hH_ready")
        xTH_ready, xTL_ready, mTH_ready, mTL_ready = (sem(x) for x in ("xTH_ready", "xTL_ready", "mTH_ready", "mTL_ready"))
        x_loaded, tab0_loaded, tab_loaded = sem("x_loaded"), sem("tab0_loaded"), sem("tab_loaded")
        act_passed, dve_passed, pool_passed = sem("act_passed"), sem("dve_passed"), sem("pool_passed")
        tab2_loaded, eps_ready, lz_zeroed = sem("tab2_loaded"), sem("eps_ready"), sem("lz_zeroed")
        kc_loaded, vc_loaded, clf_loaded = sem("kc_loaded"), sem("vc_loaded"), sem("clf_loaded")
        va_copied, vb_copied, pe_in, pe_exp = sem("va_copied"), sem("vb_copied"), sem("pe_in"), sem("pe_exp")
        ctka_copied, ctkb_copied = sem("ctka_copied"), sem("ctkb_copied")
        par_loaded = sem("par_loaded")
        swc_loaded = sem("swc_loaded")
        gains_ready = sem("gains_ready")
        sq_ready, sq_used = sem("sq_ready"), sem("sq_used")
        root_ready, recip_ready, a_ready = sem("root_ready"), sem("recip_ready"), sem("a_ready")
        za_ready, ze_ready, zl_ready, logf_ready = (sem(x) for x in ("za_ready", "ze_ready", "zl_ready", "logf_ready"))
        lbd_ready, nf_done, nf_copied = sem("lbd_ready"), sem("nf_done"), sem("nf_copied")
        colroot_ready, colrecip_ready, col_done = sem("colroot_ready"), sem("colrecip_ready"), sem("col_done")
        qbd_zeroed, qbd_ready = sem("qbd_zeroed"), sem("qbd_ready")
        out_done = sem("out_done")
        scores_ready, biased, max_ready, negmax_ready = (sem(x) for x in (
            "scores_ready", "biased", "max_ready", "negmax_ready"))
        exp_ready, den_ready, recipd_ready, norm_ready = (sem(x) for x in (
            "exp_ready", "den_ready", "recipd_ready", "norm_ready"))
        probT_done, probT_copied, av_done, y_copied = (sem(x) for x in (
            "probT_done", "probT_copied", "av_done", "y_copied"))
        h_added = sem("h_added")
        nf_stored, nfs_loaded, nfp_loaded, nf_added = (sem(x) for x in ("nf_stored", "nfs_loaded", "nfp_loaded", "nf_added"))
        osm_copied, osT_done, sH_ready, s_copied = (sem(x) for x in ("osm_copied", "osT_done", "sH_ready", "s_copied"))
        silu_ready, hid_ready = sem("silu_ready"), sem("hid_ready")
        h_added2 = sem("h_added2")
        ctT_done, ctk_stored = sem("ctT_done"), sem("ctk_stored")
        logits_done, memv_ready, pos_done, route = sem("logits_done"), sem("memv_ready"), sem("pos_done"), sem("route")
        cnt_ready = sem("cnt_ready")
        oneh_ready, oneh_used, sidx_ready = sem("oneh_ready"), sem("oneh_used"), sem("sidx_ready")
        lgT_copied = sem("lgT_copied")
        iota_ready, empty_ready = sem("iota_ready"), sem("empty_ready")
        gidx_ready, didx_ready, xg_loaded, xgT_done = (sem(x) for x in ("gidx_ready", "didx_ready", "xg_loaded", "xgT_done"))
        msilu_ready, mh_ready, mhT_done = sem("msilu_ready"), sem("mh_ready"), sem("mhT_done")
        my_copied, my_stored = sem("my_copied"), sem("my_stored")
        y12_loaded = [sem(f"y12_loaded{x}") for x in range(4)]
        rows_stored, hT_done, y_half, y_ready, y_out = (sem(x) for x in (
            "rows_stored", "hT_done", "y_half", "y_ready", "y_out"))

        SB = [4, 5, 6, 2]
        block = ctx.enter_context(nc.Block())
        last_of_g = {u["g"]: u["n"] for u in UNITS if u.get("last")}
        last_sample_of_g = {u["g"]: u["n"] for u in UNITS if u.get("last_sample")}
        nfox = sum(u["kind"] == "fox" for u in UNITS) // DEPTH

        def pair_tile(g):
            return (g + NPAIR) % NG

        def fox_index(n):
            return n // NU * nfox + n % NU - (NU - nfox)

        def swa_index(n):
            return n // NU * (NU - nfox) + n % NU
        after_sample = {u["n"]: u["g"] for u in UNITS if u.get("last_sample")}
        after_last = {u["n"]: u["g"] for u in UNITS if u.get("last")}

        def sink_col(u, t=None):
            x = 4 * u["pr"] + (2 if u["what"] == "both" else 3 if u["what"] == "sample" else u["h2"])
            if t is None:
                return par[0:u["rows"], PC["sink"] + x:PC["sink"] + x + 1]
            return t[0:u["rows"], x:x + 1]

        def nsink_col(u):
            return sink_col(u, nsink)

        groups = [[0, 1], [2, 3, 4], [5, 6, 7], [8, 9, 10]]

        def count(c, it, per):
            return c if it is None else it * per + c

        def split_high(p, it=None, per=0):
            w = WIDTH[p]
            nc.scalar.wait_ge(raw_full[p % RAW], count(16 * (p // RAW + 1), it, 16 * (per // RAW)))
            if p >= SPL:
                nc.scalar.wait_ge(piece_done, count(p - SPL + 1, it, per))
            nc.scalar.activation(WH[:, p % SPL, 0:w], raw[:, p % RAW, 0:w], ACT.Copy).then_inc(hi_ready, 1)

        def split_low(p, it=None, per=0):
            w = WIDTH[p]
            nc.vector.wait_ge(hi_ready, count(p + 1, it, per))
            nc.vector.tensor_tensor(WL[:, p % SPL, 0:w], raw[:, p % RAW, 0:w], WH[:, p % SPL, 0:w].bitcast(F32),
                                    ALU.subtract).then_inc(lo_ready, 1)

        def piece(p, n):
            return (WH[:, p % SPL, 0:WIDTH[p]].rearrange("p (a b) -> p a b", a=n),
                    WL[:, p % SPL, 0:WIDTH[p]].rearrange("p (a b) -> p a b", a=n))

        @block.sync
        def _(sp):
            def load(src, p, it=None, per=0):
                if p >= RAW:
                    sp.wait_ge(lo_ready, count(p - RAW + 1, it, per))
                sp.dma_start(raw[:, p % RAW, 0:WIDTH[p]], src).then_inc(raw_full[p % RAW], 16)

            sp.dma_start(tab[:, 0:NTAB_NORM], tables[:, 0:NTAB_NORM]).then_inc(tab0_loaded, 16)
            for k in range(KD):
                sp.dma_start(hT[:, k, :], xT[:, k, :]).then_inc(x_loaded, 16)
            for l in range(DEPTH):
                for i in range(4):
                    load(w_vf[l, i], AT["v", l] + i)
                    if l == 0 and i == 1:
                        sp.dma_start(tab[:, NTAB_NORM:NTAB_ATT], tables[:, NTAB_NORM:NTAB_ATT]).then_inc(tab_loaded, 16)
                if l:
                    sp.wait_ge(h_added2, KD * l)
                sp.dma_start(clf_sb[:, :, :].rearrange("p c n -> p (c n)"), clf[l]).then_inc(clf_loaded, 16)
                for x in range(NCOL):
                    load(w_col[l, x], AT["col", l] + x)
                    if x == 6:
                        sp.dma_start(ksw[:, :], ck_swa[l]).then_inc(swc_loaded, 16)
                        sp.dma_start(vsw[:, :], cv_swa[l]).then_inc(swc_loaded, 16)
                        sp.dma_start(kc[:, :], ck_fox[l, 0]).then_inc(kc_loaded, 16)
                        sp.dma_start(vc[:, :], cv_fox[l, 0]).then_inc(vc_loaded, 16)
                    if l == 0 and x == 4:
                        sp.dma_start(tab[:, NTAB_ATT:NTAB], tables[:, NTAB_ATT:NTAB]).then_inc(tab2_loaded, 16)
                        sp.dma_start(wr[:, :, :].rearrange("p k e -> p (k e)"), w_r[:, :]).then_inc(tab2_loaded, 16)
                for m in range(RAW):
                    load(w_o[l, m], AT["wo", l] + m)
                sp.wait_ge(nf_copied, 2 * l + 2)
                sp.dma_start(nf_rows[l], NFp[0:H, :]).then_inc(nf_stored, 16)
                sp.dma_start(nf_seqs[l], NFs[0:64, :]).then_inc(nf_stored, 16)
                sp.wait_ge(nf_stored, 32 * (l + 1))
                for pr in range(NPAIR):
                    prev = last_sample_of_g[l * NG + NPAIR + pr - 1]
                    if pr:
                        sp.wait_ge(scores_ready, prev + 1)
                        sp.dma_start(kc[:, :], ck_fox[l, pr]).then_inc(kc_loaded, 16)
                        sp.wait_ge(nf_added, fox_index(prev) + 1)
                    for s in range(2):
                        rows = nf_seqs[l, 16 * pr + 8 * s:16 * pr + 8 * s + 8, :]
                        sp.dma_start(nf_smp[:, s, :], rows.unsqueeze(1).to_broadcast([8, TSEQ, 384])).then_inc(nfs_loaded, 16)
                    if pr:
                        sp.wait_ge(av_done, prev + 1)
                        sp.dma_start(vc[:, :], cv_fox[l, pr]).then_inc(vc_loaded, 16)
                        sp.wait_ge(nf_added, fox_index(last_of_g[l * NG + NPAIR + pr - 1]) + 1)
                    sp.dma_start(nf_pmt[:, :], nf_rows[l, 2 * pr:2 * pr + 2, :].rearrange("(o h) t -> o (h t)", o=1)
                                 .to_broadcast([P, 2 * TP])).then_inc(nfp_loaded, 16)
                for m in range(RAW, KD):
                    load(w_o[l, m], AT["wo", l] + m)
                if l % 2 == 0:
                    for x in range(2 * LOOP0):
                        load(w_gu[x], AT["gu"] + x)
                    with sp.Fori(0, (LOOP1 - LOOP0) // CBODY) as i:
                        for x in range(2 * LOOP0, 2 * LOOP0 + 2 * CBODY):
                            load(w_gu[bass.ds(i * (2 * CBODY) + x, 1)].rearrange("o p n -> (o p) n"), AT["gu"] + x,
                                 i, 2 * CBODY)
                    for x in range(2 * LOOP1, 2 * FCH):
                        load(w_gu[x], AT["gu"] + x)
                    for x in range(2 * KD):
                        load(w_d[x], AT["down"] + x)

            def load_expert(e, x, n):
                if x % MPER < 16:
                    src = w_egu[bass.ds(e * 16 + x % MPER, 1)].rearrange("o p n -> (o p) n")
                elif x % 2 == 0:
                    src = w_ed0[bass.ds(e * 4 + (x - 16) // 2, 1)].rearrange("o p n -> (o p) n")
                else:
                    src = w_ed1[bass.ds(e * 4 + (x - 16) // 2, 1)].rearrange("o p n -> (o p) n")
                load(src, AT["moe"] + x, n, MPER)

            for x in range(MPRE):
                load(w_egu[x], AT["moe"] + x)
            for i, (t0, r) in enumerate(TT):
                sp.wait_ge(ctka_copied, i + 1)
                sp.wait_ge(ctkb_copied, i + 1)
                sp.dma_start(c_rows[t0:t0 + r, :], ctk[0:r, i, :]).then_inc(ctk_stored, 16)
            sp.wait_ge(cnt_ready, 1)
            most = sp.value_load(cnt_i[0:1, 0:1], min_val=0, max_val=T)
            with sp.Fori(0, MAXR) as r:
                with sp.If(most > r * P):
                    with sp.Fori(0, E - 1) as e:
                        for x in range(MPRE, MPER):
                            load_expert(e, x, r * E + e)
                        for x in range(MPER, MPER + MPRE):
                            load_expert(e + 1, x, r * E + e)
                    for x in range(MPRE, MPER):
                        load_expert(E - 1, x, r * E + (E - 1))
                    with sp.If(most > r * P + P):
                        for x in range(MPER, MPER + MPRE):
                            load_expert(0, x, r * E + (E - 1))

            sp.wait_ge(rows_stored, 1)
            for x, (t0, r) in enumerate(TLAST):
                sp.dma_start(y12[0:r, x, :], y_rows[1 + 2 * t0:1 + 2 * t0 + 2 * r, :].rearrange("(t w) d -> t (w d)", w=2)
                             ).then_inc(y12_loaded[x], 16)

        @block.gpsimd
        def _(pool):
            def low_parts(i):
                for k in range(0, KD, 2):
                    pool.wait_ge(aH_ready, i * KD + k + 1)
                    nc.gpsimd.tensor_tensor(aL[:, k, :], aT[:, k, :], aH[:, k, :].bitcast(F32), ALU.subtract
                                            ).then_inc(aL_ready[0], 1)

            for l in range(DEPTH):
                if l:
                    pool.wait_ge(h_added2, KD * l)
                pool.dma_start(par[:, :], params[l]).then_inc(par_loaded, 16)
                nc.gpsimd.memset(qbd[:, :, :], 0.0).then_inc(qbd_zeroed, 1)
                low_parts(2 * l)
                pool.wait_ge(va_copied, 4 * (l + 1))
                pool.wait_ge(vb_copied, 4 * (l + 1))
                for i, (t0, r) in enumerate(QT):
                    pool.dma_start(o_vfox[l, t0:t0 + r, :], v_tok[0:r, i, :]).then_inc(out_done, 16)
                    pool.dma_start(o_vswa[l, t0:t0 + r, :], vb_tok[0:r, i, :]).then_inc(out_done, 16)
                pool.wait_ge(logf_ready, l + 1)
                for i, (t0, r) in enumerate(QT):
                    pool.dma_start(o_lf[l, t0:t0 + r, :], lf[0:r, i, :]).then_inc(out_done, 16)
                pool.wait_ge(qbd_zeroed, l + 1)
                for x, c in enumerate(COLS):
                    pool.wait_ge(col_done, l * NCOL + x + 1)
                    if c < 4 or c > 8:
                        dst = qbd[:, c if c < 4 else c - 5, :].rearrange("p (b h q) -> p b h q", b=BS, h=2)
                        for h2 in range(2):
                            last = nc.gpsimd.tensor_copy(
                                dst[64 * h2:64 * h2 + 64, :, h2, :],
                                qk[64 * h2:64 * h2 + 64, c, TP:T].rearrange("p (b q) -> p b q", b=BS))
                        last.then_inc(qbd_ready, 1)
                    elif c < 8:
                        pool.dma_start(o_kfox[l, c - 4], qk[:, c, :]).then_inc(out_done, 16)
                    else:
                        pool.dma_start(o_kswa[l], qk[:, c, :]).then_inc(out_done, 16)
                pool.wait_ge(qbd_ready, 8 * (l + 1))
                for u in UNITS[l * NU:(l + 1) * NU]:
                    n, rows, keys = u["n"], u["rows"], u["keys"]
                    pool.wait_ge(recipd_ready, n + 1)
                    nc.gpsimd.tensor_scalar(prob[0:rows, n % 4, 0:keys], prob[0:rows, n % 4, 0:keys],
                                            small[0:rows, 12 + n % 4:13 + n % 4], None, ALU.mult).then_inc(norm_ready, 1)
                if l % 2 == 0:
                    low_parts(2 * l + 1)
            pool.wait_ge(ctk_stored, 16 * len(TT))
            pool.wait_ge(cnt_ready, 1)
            most = pool.value_load(cnt_i[0:1, 0:1], min_val=0, max_val=T)

            def store_rows(e, n):
                pool.wait_ge(my_copied, n * 2 + 2)
                pool.sem_inc(pool_passed, 1)
                nc.gpsimd.tensor_copy(didx[:, 0:1], slot_tok[:, bass.ds(e + E, 1)]).then_inc(didx_ready, 1)
                pool.wait_ge(didx_ready, n + 1)
                pool.sem_inc(pool_passed, 1)
                nc.gpsimd.indirect_dma_start(
                    out=y_rows[:, :], out_offset=bass.IndirectOffsetOnAxis(ap=didx[:, 0:1], axis=0), in_=yev[:, :],
                    in_offset=None, bounds_check=2 * T, oob_is_err=False).then_inc(my_stored, 16)
                pool.wait_ge(my_stored, n * 16 + 16)
                pool.sem_inc(pool_passed, 1)

            def gather(e, n):
                if not isinstance(e, int):
                    pool.wait_ge(xgT_done, n * 2)
                    pool.sem_inc(pool_passed, 1)
                nc.gpsimd.tensor_copy(gidx[:, 0:1], slot_tok[:, bass.ds(e, 1)]).then_inc(gidx_ready, 1)
                pool.wait_ge(gidx_ready, n + 1)
                pool.sem_inc(pool_passed, 1)
                nc.gpsimd.indirect_dma_start(
                    out=xg[:, :], out_offset=None, in_=c_rows[:, :],
                    in_offset=bass.IndirectOffsetOnAxis(ap=gidx[:, 0:1], axis=0)).then_inc(xg_loaded, 16)

            with pool.Fori(0, MAXR) as r:
                with pool.If(most > r * P):
                    pool.wait_ge(sidx_ready, r + 1)
                    pool.sem_inc(pool_passed, 1)
                    gather(0, r * E)
                    with pool.Fori(1, E) as e:
                        gather(e, r * E + e)
                        store_rows(e - 1, r * E + e - 1)
                    store_rows(E - 1, r * E + (E - 1))
            pool.sem_inc(rows_stored, 1)
            pool.wait_ge(y_out, 16 * len(TLAST))
            pool.wait_ge(out_done, 16 * DEPTH * OUTS_PER_LAYER)

        @block.tensor
        def _(pe):
            mm = nc.tensor.matmul

            def mm3(out, aw, bw, start, stop):
                mm(out, aw[0], bw[0], start=start, stop=False)
                mm(out, aw[0], bw[1], start=False, stop=False)
                return mm(out, aw[1], bw[0], start=False, stop=stop)

            def act_parts(k, t0=0, t1=T):
                return aH[:, k, t0:t1], aL[:, k, t0:t1]

            def split(p, it=None, per=0):
                pe.wait_ge(lo_ready, count(p + 1, it, per))

            def act_split(i, k):
                pe.wait_ge(aL_ready[k % 2], i * (KD // 2) + k // 2 + 1)

            def all_features(out, p, it=None, per=0, norm_i=None):
                split(p, it, per)
                wh, wl = piece(p, KD)
                for k in range(KD):
                    if norm_i is not None:
                        act_split(norm_i, k)
                    last = mm3(out[:, 0:T], (wh[:, k, :], wl[:, k, :]), act_parts(k), k == 0, k == KD - 1)
                last.then_inc(piece_done, 1)

            def norm(l, w, ks=range(KD)):
                for k in ks:
                    i = l * SQ_PER_LAYER + (KD + NCOL) * w + k
                    pe.wait_ge(sq_ready, i + 1)
                    mm(bank[2][:, 0:T], mean, sq[:, i % 2, :], start=(k == 0), stop=(k == KD - 1)).then_inc(sq_used, 1)

            def scores(u):
                n, l, pr, rows, keys = u["n"], u["l"], u["pr"], u["rows"], u["keys"]
                S = bank[SB[n % 4]]
                fox = u["kind"] == "fox"
                qc, kk = (pr, 4 + pr) if fox else (9 + pr, 8)
                if n % NU >= 4:
                    pe.wait_ge(exp_ready, n - 3)
                if u["what"] == "prompt":
                    h0, q0 = 64 * u["h2"], u["q0"]
                    last = mm(S[0:rows, 0:keys], qk[h0:h0 + 64, qc, q0:q0 + rows], qk[h0:h0 + 64, kk, 0:keys],
                              start=True, stop=True)
                elif u["what"] == "both":
                    for h2 in range(2):
                        h0 = 64 * h2
                        last = mm(S[h0:h0 + 64, 0:keys], qk[h0:h0 + 64, qc, 208:TP], qk[h0:h0 + 64, kk, 0:keys],
                                  start=True, stop=True)
                else:
                    s = u["s"]
                    past = PAST if fox else 128
                    d = pr if fox else 4 + pr
                    if fox:
                        pe.wait_ge(kc_loaded, 16 * (l * NPAIR + pr + 1))
                    else:
                        pe.wait_ge(swc_loaded, 32 * (l + 1))
                    pe.wait_ge(qbd_ready, l * 8 + d + 1)
                    mm(S[:, past:past + P], qbd[:, d, 128 * s:128 * s + 128], qk[:, kk, TP:T], start=True, stop=True)
                    for b4 in range(4):
                        b = 4 * s + b4
                        keysT = kc[:, 256 * b:256 * b + 256] if fox else ksw[:, 128 * b:128 * b + 128]
                        last = mm(S[32 * b4:32 * b4 + 32, 0:past], qbd[:, d, 32 * b:32 * b + 32], keysT,
                                  start=True, stop=True, tile_position=(0, 32 * b4))
                last.then_inc(scores_ready, 1)

            def transposes(u):
                n, rows, keys = u["n"], u["rows"], u["keys"]
                pe.wait_ge(norm_ready, n + 1)
                if n >= 2:
                    pe.wait_ge(probT_copied, n - 1)
                PT = bank[7 if n % 2 else 3]
                for i in range(-(-keys // P)):
                    w = min(P, keys - P * i)
                    last = nc.tensor.transpose(PT[0:w, P * i:P * i + rows], prob[0:rows, n % 4, P * i:P * i + w],
                                               ident[0:rows, 0:rows])
                last.then_inc(probT_done, 1)

            def av(u):
                n, l, pr, rows, keys = u["n"], u["l"], u["pr"], u["rows"], u["keys"]
                fox = u["kind"] == "fox"
                pe.wait_ge(probT_copied, n + 1)
                if u["g"] and u["g"] != UNITS[n - 1]["g"]:
                    pe.wait_ge(s_copied, u["g"])
                if u["g"] and UNITS[n - 1].get("last_sample"):
                    pe.wait_ge(y_copied, u["g"])
                pT = probT[:, n % 3, :]
                values = v_tok if fox else vb_tok
                c0 = 128 * pr if fox else 0
                if u["what"] != "sample":
                    nk = -(-keys // P)
                    for h2 in ((0, 1) if u["what"] == "both" else (u["h2"],)):
                        h0, cols, x0 = 64 * h2, rows, 0
                        if u["what"] == "both":
                            cols, x0 = 64, 64 * h2
                        for i in range(nk):
                            w = min(P, keys - P * i)
                            last = mm(bank[0][h0:h0 + 64, u["q0"]:u["q0"] + cols],
                                      values[0:w, i, c0 + h0:c0 + h0 + 64], pT[0:w, P * i + x0:P * i + x0 + cols],
                                      start=(i == 0), stop=(i == nk - 1))
                else:
                    s = u["s"]
                    nk = 3 if fox else 2
                    if fox:
                        pe.wait_ge(vc_loaded, 16 * (l * NPAIR + pr + 1))
                    mm(bank[1][:, 128 * s:128 * s + 128], pT[:, P * (nk - 1):P * nk], values[:, 3, c0:c0 + 128],
                       start=True, stop=False)
                    for i in range(nk - 1):
                        for b4 in range(4):
                            b = 4 * s + b4
                            vals = vc[:, (2 * b + i) * 128:(2 * b + i) * 128 + 128] if fox else vsw[:, 128 * b:128 * b + 128]
                            last = mm(bank[1][32 * b4:32 * b4 + 32, 128 * s:128 * s + 128],
                                      pT[:, P * i + 32 * b4:P * i + 32 * b4 + 32], vals,
                                      start=False, stop=(i == nk - 2), tile_position=(0, 32 * b4))
                last.then_inc(av_done, 1)

            def samples_T(g):
                pe.wait_ge(osm_copied, g + 1)
                for s in range(2):
                    last = nc.tensor.transpose(bank[1][:, 256 + 128 * s:256 + 128 * s + 128], osm[:, 128 * s:128 * s + 128], ident)
                last.then_inc(osT_done, 1)

            pe.wait_ge(tab0_loaded, 16)
            norm(0, 0)
            pe.wait_ge(tab_loaded, 16)
            for l in range(DEPTH):
                for i in range(4):
                    p = AT["v", l] + i
                    split(p)
                    wh, wl = piece(p, 2)
                    act_split(2 * l, 2 * i)
                    act_split(2 * l, 2 * i + 1)
                    for x, (t0, r) in enumerate(QT):
                        t1 = max(t0, min(t0, T - P)) + P
                        for w, (c0, c1) in enumerate(((0, 512), (512, 648))):
                            for k in range(2):
                                last = mm3(bank[x + 4 * w][:, 0:c1 - c0], act_parts(2 * i + k, t0, t1),
                                           (wh[:, k, c0:c1], wl[:, k, c0:c1]), i + k == 0, i + k == 4)
                    last.then_inc(piece_done, 1)

                def head_mean(x):
                    i = l * SQ_PER_LAYER + KD + x
                    pe.wait_ge(sq_ready, i + 1)
                    if x >= 2:
                        pe.wait_ge(colroot_ready, l * NCOL + x - 1)
                    elif x == 0:
                        pe.wait_ge(vb_copied, 4 * (l + 1))
                    mm(bank[4 + x % 2][:, 0:T], pm, sq[:, i % 2, :], start=True, stop=True).then_inc(sq_used, 1)

                for x in range(NCOL):
                    if x < 4:
                        pe.wait_ge(va_copied, 4 * l + x + 1)
                    else:
                        pe.wait_ge(col_done, l * NCOL + x - 3)
                    all_features(bank[x % 4], AT["col", l] + x)
                    if x:
                        head_mean(x - 1)
                head_mean(NCOL - 1)
                pe.wait_ge(logf_ready, l + 1)
                pe.wait_ge(va_copied, 4 * (l + 1))
                for i, (t0, r) in enumerate(QT[:3]):
                    last = mm(bank[6][0:H, 0:TP], lf[0:r, i, :], negtri[0:r, i, :], start=(i == 0), stop=(i == 2))
                last.then_inc(nf_done, 1)
                pe.wait_ge(clf_loaded, 16 * (l + 1))
                pe.wait_ge(lbd_ready, l + 1)
                for c in range(2):
                    mm(bank[7][0:64, 0:PAST], clf_sb[:, c, :], negtri[:, c, 0:PAST], start=(c == 0), stop=(c == 1))
                for c in range(2):
                    mm(bank[7][0:64, PAST:384], clf_sb[:, c, :], negones, start=(c == 0), stop=False)
                mm(bank[7][0:64, PAST:384], lbd[:, :], newtri, start=False, stop=True).then_inc(nf_done, 1)

                if l == 0:
                    pe.wait_ge(tab2_loaded, 32)
                pe.wait_ge(nf_copied, 2 * (l + 1))
                pe.wait_ge(col_done, (l + 1) * NCOL)
                units = UNITS[l * NU:(l + 1) * NU]
                for i in range(NU + LAG + 1):
                    if i < NU:
                        scores(units[i])
                    if LAG <= i < NU + LAG:
                        transposes(units[i - LAG])
                    if i >= LAG + 1:
                        av(units[i - LAG - 1])
                    if l * NU + i - LAG - 3 in after_sample and i >= LAG + 3:
                        samples_T(after_sample[l * NU + i - LAG - 3])

                pe.wait_ge(y_copied, (l + 1) * NG)
                pe.wait_ge(s_copied, (l + 1) * NG)
                for m in range(KD):
                    if m >= 2:
                        pe.wait_ge(h_added, l * KD + m - 1)
                    all_features(bank[m % 2], AT["wo", l] + m)
                    if m:
                        norm(l, 1, [m - 1])
                norm(l, 1, [KD - 1])
                if l % 2 == 0:
                    def chunk(c, it=None):
                        if c >= 2:
                            pe.wait_ge(hid_ready, count(c - 1, it, CBODY))
                        for w in range(2):
                            all_features(bank[2 * (c % 2) + w], AT["gu"] + 2 * c + w, it, 2 * CBODY,
                                         2 * l + 1 if it is None and c + w == 0 else None)
                    for c in range(LOOP0):
                        chunk(c)
                    with pe.Fori(0, (LOOP1 - LOOP0) // CBODY) as i:
                        for c in range(LOOP0, LOOP0 + CBODY):
                            chunk(c, i)
                    for c in range(LOOP1, FCH):
                        chunk(c)
                    pe.wait_ge(hid_ready, FCH)
                    for m in range(KD):
                        if m >= 4:
                            pe.wait_ge(h_added2, m - 3)
                        for hf in range(2):
                            p = AT["down"] + 2 * m + hf
                            split(p)
                            wh, wl = piece(p, FCH // 2)
                            for c in range(FCH // 2):
                                o = (hf * (FCH // 2) + c) * T
                                last = mm3(bank[4 + m % 4][:, 0:T], (wh[:, c, :], wl[:, c, :]),
                                           (hidH[:, o:o + T], hidL[:, o:o + T]),
                                           hf + c == 0, hf == 1 and c == FCH // 2 - 1)
                            last.then_inc(piece_done, 1)
                        if m:
                            norm(l + 1, 0, [m - 1])
                    norm(l + 1, 0, [KD - 1])

            for k in range(KD):
                pe.wait_ge(a_ready, (2 * DEPTH - 1) * KD + k + 1)
                last = mm(bank[4][0:E, 0:T], wr[:, k, :], aT[:, k, :], start=(k == 0), stop=(k == KD - 1))
            last.then_inc(logits_done, 1)
            pe.wait_ge(lgT_copied, 1)
            for i, (t0, r) in enumerate(TT):
                last = nc.tensor.transpose(bank[5][0:r, E * i:E * i + E], lgT[:, t0:t0 + r], ident[0:E, 0:E])
            last.then_inc(logits_done, 1)

            def rows_of(i):
                t0, r = TT[i]
                for hf in range(2):
                    if i >= 2:
                        pe.wait_ge(ctkb_copied if hf else ctka_copied, i - 1)
                    for k in range(4):
                        last = nc.tensor.transpose(bank[2 * (i % 2) + hf][0:r, P * k:P * k + P],
                                                   aT[:, 4 * hf + k, t0:t0 + r], ident)
                    last.then_inc(ctT_done, 1)
            rows_of(0)
            rows_of(1)
            pe.wait_ge(memv_ready, 1)
            for i in range(4):
                mm(bank[6][0:1, 0:E], ones[:, 0:1], memv[:, i, :], start=(i == 0), stop=(i == 3))
            for i in range(4):
                for j in range(i + 1):
                    last = mm(bank[7][:, E * i:E * i + E], tris if i == j else ones, memv[:, j, :], start=(j == 0), stop=(j == i))
            last.then_inc(pos_done, 1)
            rows_of(2)
            rows_of(3)
            pe.wait_ge(cnt_ready, 1)
            most = pe.value_load(cnt_i[0:1, 0:1], min_val=0, max_val=T)

            def tokens_T(n, hf):
                if hf:
                    pe.wait_ge(xTL_ready, n * 2 + 1)
                else:
                    pe.wait_ge(xg_loaded, n * 16 + 16)
                for k in range(4):
                    last = nc.tensor.transpose(bank[7][:, P * k:P * k + P], xg[:, P * (4 * hf + k):P * (4 * hf + k) + P], ident)
                last.then_inc(xgT_done, 1)

            with pe.Fori(0, MAXR) as r:
                with pe.If(most > r * P):
                    for e in range(E):
                        pe.wait_ge(oneh_ready, r * E + e + 1)
                        for i in range(4):
                            last = mm(bank[6][:, 2 * e:2 * e + 2], onehot[:, e % 2, P * i:P * i + P], slot_of[:, i, e, :],
                                      start=(i == 0), stop=(i == 3))
                        last.then_inc(oneh_used, 1)
                    tokens_T(r * E, 0)
                    tokens_T(r * E, 1)
                    with pe.Fori(0, E) as e:
                        n = r * E + e

                        def hidden_T(j):
                            pe.wait_ge(mh_ready, n * 4 + (j + 1))
                            if j in (1, 2):
                                pe.wait_ge(mTL_ready, n * 4 + j)
                            for x, c in enumerate(groups[j]):
                                last = nc.tensor.transpose(bank[0 if j == 3 else 4][:, P * x:P * x + P], mh[:, P * c:P * c + P], ident)
                            last.then_inc(mhT_done, 1)

                        def down(m, hf):
                            x = 16 + 2 * m + hf
                            split(AT["moe"] + x, n, MPER)
                            wh, wl = piece(AT["moe"] + x, MCH - MD0 if hf else MD0)
                            c0, c1 = (MD0, MCH) if hf else (0, MD0)
                            for c in range(c0, c1):
                                if m == 0 and c in (MD0, groups[3][0]):
                                    pe.wait_ge(mTL_ready, n * 4 + (3 if c == MD0 else 4))
                                last = mm3(bank[5 + m // 2][:, 256 * (m % 2):256 * (m % 2) + 256],
                                           (mTH[:, c, :], mTL[:, c, :]), (wh[:, c - c0, :], wl[:, c - c0, :]),
                                           c == 0, c == MCH - 1)
                            last.then_inc(piece_done, 1)

                        pe.wait_ge(xTL_ready, n * 2 + 2)
                        for j in range(MBLK):
                            if j >= 2:
                                pe.wait_ge(mh_ready, n * 4 + (j - 1))
                            for w in range(2):
                                for hf in range(2):
                                    p = AT["moe"] + 4 * j + 2 * w + hf
                                    split(p, n, MPER)
                                    wh, wl = piece(p, KD // 2)
                                    for k in range(KD // 2):
                                        kk = hf * (KD // 2) + k
                                        last = mm3(bank[2 * (j % 2) + w][:, 0:MB], (xTH[:, kk, :], xTL[:, kk, :]),
                                                   (wh[:, k, :], wl[:, k, :]), kk == 0, kk == KD - 1)
                                    last.then_inc(piece_done, 1)
                            if j:
                                hidden_T(j - 1)
                        with pe.If(e < E - 1):
                            tokens_T(n + 1, 0)
                        pe.wait_ge(mTL_ready, n * 4 + 2)
                        down(0, 0)
                        hidden_T(3)
                        down(0, 1)
                        down(1, 0)
                        down(1, 1)
                        with pe.If(e < E - 1):
                            tokens_T(n + 1, 1)
                        for m in (2, 3):
                            down(m, 0)
                            down(m, 1)
            for x, (t0, r) in enumerate(TLAST):
                if x == 3:
                    pe.wait_ge(y_half, 2)
                for k in range(KD):
                    last = nc.tensor.transpose(bank[YB[x][k // 4]][0:r, P * (k % 4):P * (k % 4) + P],
                                               hT[:, k, t0:t0 + r], ident)
                last.then_inc(hT_done, 1)

        @block.scalar
        def _(act):
            A = nc.scalar.activation

            def square(i, src):
                if i >= 2:
                    act.wait_ge(sq_used, i - 1)
                A(sq[:, i % 2, :], src, ACT.Square).then_inc(sq_ready, 1)

            def norm_square(l, w, k):
                if w:
                    act.wait_ge(h_added, l * KD + k + 1)
                elif l:
                    act.wait_ge(h_added2, (l - 1) * KD + k + 1)
                square(l * SQ_PER_LAYER + (KD + NCOL) * w + k, hT[:, k, :])

            def norm_rest(l, w):
                act.wait_ge(sq_used, l * SQ_PER_LAYER + (KD + NCOL) * w + KD)
                A(rt[:, 0, :], bank[2][:, 0:T], ACT.Sqrt, bias=eps_col[:, 0:1]).then_inc(root_ready, 1)
                for k in range(KD if 2 * l + w < 3 else 0):
                    act.wait_ge(a_ready, (2 * l + w) * KD + k + 1)
                    A(aH[:, k, :], aT[:, k, :], ACT.Copy).then_inc(aH_ready, 1)

            act.wait_ge(eps_ready, 1)
            act.wait_ge(x_loaded, 16 * KD)
            for k in range(KD):
                norm_square(0, 0, k)
            split_high(0)
            for l in range(DEPTH):
                norm_rest(l, 0)
                if l == 0:
                    for p in range(1, SPL):
                        split_high(p)
                v = AT["v", l]
                for i in range(3):
                    split_high(v + i + SPL)
                act.wait_ge(piece_done, v + 4)
                for i, (t0, r) in enumerate(QT):
                    A(v_tok[0:r, i, :], bank[i][0:r, :], ACT.Copy).then_inc(va_copied, 1)
                split_high(v + 3 + SPL)
                act.wait_ge(za_ready, l + 1)
                A(le[:, :, :], le[:, :, :], ACT.Exp, scale=-1.0).then_inc(ze_ready, 1)
                act.wait_ge(ze_ready, l + 1)
                A(le[:, :, :], le[:, :, :], ACT.Ln, bias=1.0).then_inc(zl_ready, 1)

                def head_root(x):
                    act.wait_ge(sq_used, l * SQ_PER_LAYER + KD + x + 1)
                    if x >= 2:
                        act.wait_ge(colrecip_ready, l * NCOL + x - 1)
                    A(rt[:, x % 2, :], bank[4 + x % 2][:, 0:T], ACT.Sqrt, bias=eps_col[:, 0:1]).then_inc(colroot_ready, 1)

                act.wait_ge(recip_ready, 2 * l + 1)
                for x in range(NCOL):
                    act.wait_ge(piece_done, AT["col", l] + x + 1)
                    square(l * SQ_PER_LAYER + KD + x, bank[x % 4][:, 0:T])
                    split_high(AT["col", l] + x + SPL)
                    if x:
                        head_root(x - 1)
                head_root(NCOL - 1)

                def exps(u):
                    n, rows, keys = u["n"], u["rows"], u["keys"]
                    nm = small[0:rows, 4 + n % 4:5 + n % 4]
                    act.wait_ge(negmax_ready, n + 1)
                    if n >= 4:
                        act.wait_ge(probT_done, n - 3)
                    if u["kind"] == "swa":
                        A(small[0:rows, 16 + n % 4:17 + n % 4], sink_col(u), ACT.Exp, bias=nm)
                    A(prob[0:rows, n % 4, 0:keys], bank[SB[n % 4]][0:rows, 0:keys], ACT.Exp, bias=nm,
                      accum_out=small[0:rows, 8 + n % 4:9 + n % 4]).then_inc(exp_ready, 1)

                def copy_T(u):
                    n, rows, keys = u["n"], u["rows"], u["keys"]
                    act.wait_ge(probT_done, n + 1)
                    if n >= 3:
                        act.wait_ge(av_done, n - 2)
                    PT = bank[7 if n % 2 else 3]
                    nk = keys // P
                    if nk:
                        last = A(probT[:, n % 3, 0:nk * P].rearrange("p (i w) -> p i w", i=nk)[:, :, 0:rows],
                                 PT[:, 0:nk * P].rearrange("p (i w) -> p i w", i=nk)[:, :, 0:rows], ACT.Copy)
                    if keys % P:
                        w = keys % P
                        last = A(probT[0:w, n % 3, nk * P:nk * P + rows], PT[0:w, nk * P:nk * P + rows], ACT.Copy)
                    last.then_inc(probT_copied, 1)

                def copy_samples(g):
                    act.wait_ge(av_done, last_sample_of_g[g] + 1)
                    A(osm[:, :], bank[1][:, 0:256], ACT.Copy).then_inc(osm_copied, 1)

                def take_samples(g):
                    act.wait_ge(osT_done, g + 1)
                    smp = bank[1][:, 256:512].rearrange("p (b h q) -> p b h q", b=BS, h=2)
                    for h2 in range(2):
                        last = A(aH[64 * h2:64 * h2 + 64, pair_tile(g), TP:T].rearrange("p (b q) -> p b q", b=BS),
                                 smp[64 * h2:64 * h2 + 64, :, h2, :], ACT.Copy)
                    last.then_inc(sH_ready, 1)

                def take_prompt(g):
                    act.wait_ge(av_done, last_of_g[g] + 1)
                    A(aH[:, pair_tile(g), 0:TP], bank[0][:, 0:TP], ACT.Copy).then_inc(yH_ready, 1)

                units = UNITS[l * NU:(l + 1) * NU]
                for i in range(NU + LAG + 2):
                    if i < NU:
                        exps(units[i])
                    if LAG <= i < NU + LAG:
                        copy_T(units[i - LAG])
                    for ago, of, do in ((LAG + 2, after_sample, copy_samples), (LAG + 4, after_sample, take_samples),
                                        (LAG + 1, after_last, take_prompt)):
                        if i >= ago and l * NU + i - ago in of:
                            do(of[l * NU + i - ago])
                for m in range(KD):
                    if AT["wo", l] + m + SPL < len(WIDTH):
                        split_high(AT["wo", l] + m + SPL)
                    norm_square(l, 1, m)
                norm_rest(l, 1)
                if l % 2 == 0:
                    def chunk(c, it=None):
                        p = AT["gu"] + 2 * c
                        split_high(p + SPL, it, 2 * CBODY)
                        act.wait_ge(piece_done, count(p + 1, it, 2 * CBODY))
                        if c >= 2:
                            act.wait_ge(hid_ready, count(c - 1, it, CBODY))
                        A(sq[:, c % 2, :], bank[2 * (c % 2)][:, 0:T], ACT.Silu).then_inc(silu_ready, 1)
                        split_high(p + 1 + SPL, it, 2 * CBODY)
                    for c in range(LOOP0):
                        chunk(c)
                    with act.Fori(0, (LOOP1 - LOOP0) // CBODY) as i:
                        for c in range(LOOP0, LOOP0 + CBODY):
                            chunk(c, i)
                    for c in range(LOOP1, FCH):
                        chunk(c)
                    for m in range(KD):
                        for hf in range(2):
                            split_high(AT["down"] + 2 * m + hf + SPL)
                        norm_square(l + 1, 0, m)
            act.wait_ge(out_done, 16 * DEPTH * OUTS_PER_LAYER)
            for i, (t0, r) in enumerate(TT):
                act.wait_ge(ctT_done, 2 * i + 1)
                A(ctk[0:r, i, 0:512], bank[2 * (i % 2)][0:r, :], ACT.Copy).then_inc(ctka_copied, 1)
                if i == 1:
                    act.wait_ge(pe_in, 1)
                    A(gate[:, :, :], tmp8[:, :, :], ACT.Exp).then_inc(pe_exp, 1)
            act.wait_ge(cnt_ready, 1)
            most = act.value_load(cnt_i[0:1, 0:1], min_val=0, max_val=T)
            with act.Fori(0, MAXR) as r:
                with act.If(most > r * P):
                    def copy_tokens(n, hf):
                        act.wait_ge(xgT_done, n * 2 + (hf + 1))
                        A(xTH[:, 4 * hf:4 * hf + 4, :].rearrange("p k t -> p (k t)"), bank[7][:, :], ACT.Copy).then_inc(xTH_ready, 1)
                    copy_tokens(r * E, 0)
                    copy_tokens(r * E, 1)
                    with act.Fori(0, E) as e:
                        n = r * E + e
                        M = AT["moe"] + SPL

                        def copy_hidden(j):
                            act.wait_ge(mhT_done, n * 4 + (j + 1))
                            c0, w = groups[j][0], len(groups[j])
                            A(mTH[:, c0:c0 + w, :].rearrange("p c t -> p (c t)"), bank[0 if j == 3 else 4][:, 0:P * w],
                              ACT.Copy).then_inc(mTH_ready, 1)
                        for j in range(MBLK):
                            split_high(M + 4 * j, n, MPER)
                            split_high(M + 4 * j + 1, n, MPER)
                            act.wait_ge(piece_done, count(AT["moe"] + 4 * j + 2, n, MPER))
                            if j >= 2:
                                act.wait_ge(mh_ready, n * 4 + (j - 1))
                            A(sg[:, j % 2, :], bank[2 * (j % 2)][:, 0:MB], ACT.Silu).then_inc(msilu_ready, 1)
                            split_high(M + 4 * j + 2, n, MPER)
                            split_high(M + 4 * j + 3, n, MPER)
                            if j:
                                copy_hidden(j - 1)
                        with act.If(e < E - 1):
                            copy_tokens(n + 1, 0)
                        with act.Else():
                            act.wait_ge(my_stored, n * 16)
                            act.sem_inc(act_passed, 1)
                        copy_hidden(3)
                        for x in range(16, 20):
                            split_high(M + x, n, MPER)
                        with act.If(e < E - 1):
                            copy_tokens(n + 1, 1)
                        act.wait_ge(piece_done, count(AT["moe"] + 20, n, MPER))
                        A(yev[:, 0:512], bank[5][:, :], ACT.Copy).then_inc(my_copied, 1)
                        split_high(M + 20, n, MPER)
                        with act.If(e < E - 1):
                            for x in range(21, 24):
                                split_high(M + x, n, MPER)
                    with act.If(most > r * P + P):
                        for x in range(21, 24):
                            split_high(AT["moe"] + SPL + x, r * E + (E - 1), MPER)
            for x, (t0, r) in enumerate(TLAST):
                act.wait_ge(y_ready, x + 1)
                act.dma_start(o_y[t0:t0 + r, :], yo[0:r, x, :]).then_inc(y_out, 16)

        @block.vector
        def _(dve):
            V = nc.vector
            nc.vector.memset(eps_col[:, 0:1], EPS).then_inc(eps_ready, 1)
            nc.vector.memset(lz[:, :, :], 0.0).then_inc(lz_zeroed, 1)
            nc.vector.memset(lg[:, :, :], 0.0).then_inc(lz_zeroed, 1)

            def low_part(i, k):
                dve.wait_ge(aH_ready, i * KD + k + 1)
                V.tensor_tensor(aL[:, k, :], aT[:, k, :], aH[:, k, :].bitcast(F32), ALU.subtract
                                ).then_inc(aL_ready[1], 1)

            def norm(l, w):
                i = 2 * l + w
                g0 = PC["g_ffn" if w else "g_attn"]
                dve.wait_ge(root_ready, i + 1)
                V.reciprocal(rs[:, 0, :], rt[:, 0, :]).then_inc(recip_ready, 1)
                dve.wait_ge(recip_ready, i + 1)
                for k in range(KD):
                    V.scalar_tensor_tensor(aT[:, k, :], hT[:, k, :], par[:, g0 + k:g0 + k + 1], rs[:, 0, :],
                                           ALU.mult, ALU.mult).then_inc(a_ready, 1)
                    if i < 3 and k in (2, 4, 6):
                        low_part(i, k - 1)
                if i < 3:
                    low_part(i, KD - 1)

            split_low(0)
            for l in range(DEPTH):
                dve.wait_ge(par_loaded, 16 * (l + 1))
                for x, nm in enumerate(("qn_a", "qn_b")):
                    V.tensor_scalar(gq[:, x:x + 1], par[:, PC[nm]:PC[nm] + 1], HD ** -0.5, None, ALU.mult)
                V.tensor_scalar(nsink[:, :], par[:, PC["sink"]:PC["sink"] + 16], -1.0, None, ALU.mult).then_inc(gains_ready, 1)
                dve.wait_ge(gains_ready, l + 1)
                if l == 0:
                    dve.wait_ge(x_loaded, 16 * KD)
                norm(l, 0)
                if l == 0:
                    for p in range(1, SPL):
                        split_low(p)
                v = AT["v", l]
                for i in range(3):
                    split_low(v + i + SPL)
                if l == 0:
                    dve.wait_ge(lz_zeroed, 2)
                dve.wait_ge(piece_done, v + 4)
                bf = par[:, PC["b_f"]:PC["b_f"] + H]
                for i, (t0, r) in enumerate(QT):
                    V.tensor_tensor(lz[0:r, i, :], bank[4 + i][0:r, 128:136], bf[0:r, :], ALU.add)
                    V.tensor_copy(vb_tok[0:r, i, :], bank[4 + i][0:r, 0:128]).then_inc(vb_copied, 1)
                split_low(v + 3 + SPL)
                dve.wait_ge(vb_copied, 4 * (l + 1))
                V.scalar_tensor_tensor(le[:, :, :], lz[:, :, :], -1.0, lz[:, :, :], ALU.mult, ALU.max).then_inc(za_ready, 1)
                dve.wait_ge(zl_ready, l + 1)
                V.scalar_tensor_tensor(lf[:, :, :], lz[:, :, :], 0.0, le[:, :, :], ALU.min, ALU.subtract).then_inc(logf_ready, 1)
                dve.wait_ge(logf_ready, l + 1)
                V.tensor_tensor(lbd[:, :].rearrange("p (j b h) -> p j b h", j=NPAIR, b=BS),
                                bmask.rearrange("p (j b h) -> p j b h", j=NPAIR, b=BS),
                                lf[:, 3, :].rearrange("p (j h) -> p j h", j=NPAIR).unsqueeze(2).to_broadcast([P, NPAIR, BS, 2]),
                                ALU.mult).then_inc(lbd_ready, 1)
                for x in range(-1, NCOL):
                    if x + 1 < NCOL:
                        split_low(AT["col", l] + x + 1 + SPL)
                    if x < 0:
                        continue
                    c = COLS[x]
                    i = l * NCOL + x
                    dve.wait_ge(colroot_ready, i + 1)
                    V.reciprocal(rs[:, x % 2, :], rt[:, x % 2, :]).then_inc(colrecip_ready, 1)
                    dve.wait_ge(colrecip_ready, i + 1)
                    g = (gq[:, 0:1] if c < 4 else par[:, PC["kn_a"]:PC["kn_a"] + 1] if c < 8 else
                         par[:, PC["kn_b"]:PC["kn_b"] + 1] if c == 8 else gq[:, 1:2])
                    V.scalar_tensor_tensor(qk[:, c, :], bank[x % 4][:, 0:T], g, rs[:, x % 2, :],
                                           ALU.mult, ALU.mult).then_inc(col_done, 1)
                dve.wait_ge(nf_done, 2 * l + 1)
                V.tensor_copy(NFp[0:H, :], bank[6][0:H, 0:TP]).then_inc(nf_copied, 1)
                dve.wait_ge(nf_done, 2 * l + 2)
                V.tensor_copy(NFs[0:64, :], bank[7][0:64, 0:384]).then_inc(nf_copied, 1)
                if l == 0:
                    dve.wait_ge(tab2_loaded, 32)

                def add_bias(u):
                    n, rows, keys = u["n"], u["rows"], u["keys"]
                    S = bank[SB[n % 4]]
                    dve.wait_ge(scores_ready, n + 1)
                    if u["kind"] == "fox":
                        if u["what"] == "prompt":
                            dve.wait_ge(nfp_loaded, 16 * (u["l"] * NPAIR + u["pr"] + 1))
                            nf = nf_pmt[0:rows, u["h2"] * TP:u["h2"] * TP + keys]
                        else:
                            dve.wait_ge(nfs_loaded, 32 * (u["l"] * NPAIR + u["pr"] + 1))
                            nf = nf_smp[:, u["s"], :]
                        V.tensor_tensor(S[0:rows, 0:keys], S[0:rows, 0:keys], nf, ALU.add).then_inc(nf_added, 1)
                    else:
                        col = 2 if u["what"] == "both" else 3 if u["what"] == "sample" else u["h2"]
                        V.scalar_tensor_tensor(S[0:rows, 0:keys], dist[0:rows, u["d0"]:u["d0"] + keys],
                                               negslope[0:rows, u["pr"], col:col + 1], S[0:rows, 0:keys],
                                               ALU.mult, ALU.add).then_inc(biased, 1)

                def add_mask(u):
                    n, rows, keys = u["n"], u["rows"], u["keys"]
                    S = bank[SB[n % 4]]
                    dve.wait_ge(nf_added, fox_index(n) + 1)
                    w = rows if u["what"] == "prompt" else P
                    m = cmask[0:rows, 0:w] if u["what"] == "prompt" else smask[:, u["s"], :]
                    V.tensor_tensor(S[0:rows, keys - w:keys], S[0:rows, keys - w:keys], m, ALU.add).then_inc(biased, 1)

                def row_max(u):
                    n, rows, keys = u["n"], u["rows"], u["keys"]
                    S = bank[SB[n % 4]]
                    dve.wait_ge(biased, n + 1)
                    if u["kind"] == "fox":
                        V.tensor_reduce(small[0:rows, 4 + n % 4:5 + n % 4], S[0:rows, 0:keys], AX_X, ALU.max,
                                        negate=True).then_inc(negmax_ready, 1)
                    else:
                        V.tensor_reduce(small[0:rows, n % 4:n % 4 + 1], S[0:rows, 0:keys], AX_X, ALU.max,
                                        negate=True).then_inc(max_ready, 1)

                def max_with_sink(u):
                    n, rows = u["n"], u["rows"]
                    dve.wait_ge(max_ready, swa_index(n) + 1)
                    V.tensor_tensor(small[0:rows, 4 + n % 4:5 + n % 4], small[0:rows, n % 4:n % 4 + 1],
                                    nsink_col(u), ALU.min).then_inc(negmax_ready, 1)

                def add_sink(u):
                    n, rows = u["n"], u["rows"]
                    dve.wait_ge(exp_ready, n + 1)
                    V.tensor_tensor(small[0:rows, 20 + n % 4:21 + n % 4], small[0:rows, 8 + n % 4:9 + n % 4],
                                    small[0:rows, 16 + n % 4:17 + n % 4], ALU.add).then_inc(den_ready, 1)

                def reciprocal(u):
                    n, rows = u["n"], u["rows"]
                    x = 8 if u["kind"] == "fox" else 20
                    if u["kind"] == "fox":
                        dve.wait_ge(exp_ready, n + 1)
                    else:
                        dve.wait_ge(den_ready, swa_index(n) + 1)
                    V.reciprocal(small[0:rows, 12 + n % 4:13 + n % 4], small[0:rows, x + n % 4:x + n % 4 + 1]
                                 ).then_inc(recipd_ready, 1)

                def take_samples(g):
                    dve.wait_ge(sH_ready, g + 1)
                    smp = bank[1][:, 256:512].rearrange("p (b h q) -> p b h q", b=BS, h=2)
                    for h2 in range(2):
                        hs = slice(64 * h2, 64 * h2 + 64)
                        last = V.tensor_tensor(aL[hs, pair_tile(g), TP:T].rearrange("p (b q) -> p b q", b=BS), smp[hs, :, h2, :],
                                               aH[hs, pair_tile(g), TP:T].bitcast(F32).rearrange("p (b q) -> p b q", b=BS),
                                               ALU.subtract)
                    last.then_inc(s_copied, 1)

                def take_prompt(g):
                    dve.wait_ge(yH_ready, g + 1)
                    V.tensor_tensor(aL[:, pair_tile(g), 0:TP], bank[0][:, 0:TP], aH[:, pair_tile(g), 0:TP].bitcast(F32),
                                    ALU.subtract).then_inc(y_copied, 1)

                units = UNITS[l * NU:(l + 1) * NU]
                for i in range(NU + LAG + 2):
                    new, old = (units[i] if i < NU else None), (units[i - 2] if 2 <= i < NU + 2 else None)
                    if new:
                        add_bias(new)
                    if old and old["kind"] == "swa":
                        add_sink(old)
                    if old and old["kind"] == "fox":
                        reciprocal(old)
                    if new and new["kind"] == "fox":
                        add_mask(new)
                    if new:
                        row_max(new)
                    if old and old["kind"] == "swa":
                        reciprocal(old)
                    if new and new["kind"] == "swa":
                        max_with_sink(new)
                    for ago, of, do in ((LAG + 5, after_sample, take_samples), (LAG + 1, after_last, take_prompt)):
                        if i >= ago and l * NU + i - ago in of:
                            do(of[l * NU + i - ago])
                for m in range(KD):
                    p = AT["wo", l] + m
                    dve.wait_ge(piece_done, p + 1)
                    V.tensor_tensor(hT[:, m, :], hT[:, m, :], bank[m % 2][:, 0:T], ALU.add).then_inc(h_added, 1)
                    if p + SPL < len(WIDTH):
                        split_low(p + SPL)
                dve.wait_ge(h_added, (l + 1) * KD)
                dve.wait_ge(out_done, 16 * OUTS_PER_LAYER * (l + 1))
                norm(l, 1)
                if l % 2 == 0:
                    for x in range(2):
                        dve.wait_ge(aL_ready[x], (2 * l + 2) * (KD // 2))

                    def chunk(c, it=None):
                        p = AT["gu"] + 2 * c
                        split_low(p + SPL, it, 2 * CBODY)
                        dve.wait_ge(silu_ready, count(c + 1, it, CBODY))
                        dve.wait_ge(piece_done, count(p + 2, it, 2 * CBODY))
                        up = bank[2 * (c % 2) + 1][:, 0:T]
                        if it is None:
                            high, low = hidH[:, c * T:c * T + T], hidL[:, c * T:c * T + T]
                        else:
                            at = bass.ds((it * CBODY + c) * T, T)
                            high, low = hidH[:, at], hidL[:, at]
                        V.tensor_tensor(high, sq[:, c % 2, :], up, ALU.mult).then_inc(hH_ready, 1)
                        V.tensor_tensor(rt[:, c % 2, :], sq[:, c % 2, :], up, ALU.mult).then_inc(htmp_ready, 1)
                        split_low(p + 1 + SPL, it, 2 * CBODY)
                        dve.wait_ge(hH_ready, count(c + 1, it, CBODY))
                        dve.wait_ge(htmp_ready, count(c + 1, it, CBODY))
                        V.tensor_tensor(low, rt[:, c % 2, :], high.bitcast(F32), ALU.subtract).then_inc(hid_ready, 1)
                    for c in range(LOOP0):
                        chunk(c)
                    with dve.Fori(0, (LOOP1 - LOOP0) // CBODY) as i:
                        for c in range(LOOP0, LOOP0 + CBODY):
                            chunk(c, i)
                    for c in range(LOOP1, FCH):
                        chunk(c)
                    for m in range(KD):
                        split_low(AT["down"] + 2 * m + SPL)
                        dve.wait_ge(piece_done, AT["down"] + 2 * m + 2)
                        V.tensor_tensor(hT[:, m, :], hT[:, m, :], bank[4 + m % 4][:, 0:T], ALU.add).then_inc(h_added2, 1)
                        split_low(AT["down"] + 2 * m + 1 + SPL)
                    dve.wait_ge(h_added2, KD)

            steps = [0]

            def step(ins):
                steps[0] += 1
                ins.then_inc(route, 1)
                dve.wait_ge(route, steps[0])

            def b4(ap, shape):
                return ap.to_broadcast(shape)

            dve.wait_ge(out_done, 16 * DEPTH * OUTS_PER_LAYER)
            br = par[:, PC["b_r"]:PC["b_r"] + E]
            dve.wait_ge(logits_done, 1)
            V.tensor_copy(lgT[:, :], bank[4][0:E, 0:T]).then_inc(lgT_copied, 1)
            for i, (t0, r) in enumerate(TT):
                dve.wait_ge(logits_done, 2)
                V.tensor_tensor(lg[0:r, i, :], bank[5][0:r, E * i:E * i + E], br[0:r, :], ALU.add).then_inc(route, 1)
            steps[0] = len(TT)
            dve.wait_ge(route, len(TT))
            lge = lg[:, :, :].unsqueeze(3).to_broadcast([P, 4, E, E])
            lgo = lg[:, :, :].unsqueeze(2).to_broadcast([P, 4, E, E])
            c1 = cmp1[:, :, :].rearrange("p t (e o) -> p t e o", e=E)
            c2 = cmp2[:, :, :].rearrange("p t (e o) -> p t e o", e=E)
            step(V.tensor_tensor(c1, lgo, lge, ALU.is_gt))
            step(V.tensor_tensor(c2, lgo, lge, ALU.is_equal))
            step(V.tensor_tensor(cmp2[:, :, :], cmp2[:, :, :], first.unsqueeze(1).to_broadcast([P, 4, 64]), ALU.mult))
            step(V.tensor_tensor(cmp1[:, :, :], cmp1[:, :, :], cmp2[:, :, :], ALU.add))
            step(V.tensor_reduce(rank[:, :, :], c1, AX_X, ALU.add))
            step(V.tensor_scalar(mem[:, :, :], rank[:, :, :], 1.5, None, ALU.is_lt))
            V.tensor_tensor(memv[:, :, :], mem[:, :, :], valid.unsqueeze(2).to_broadcast([P, 4, E]), ALU.mult).then_inc(memv_ready, 1)

            def rows_of(i):
                r = TT[i][1]
                dve.wait_ge(ctT_done, 2 * i + 2)
                V.tensor_copy(ctk[0:r, i, 512:1024], bank[2 * (i % 2) + 1][0:r, :]).then_inc(ctkb_copied, 1)
            rows_of(0)
            rows_of(1)
            step(V.tensor_scalar(sel1[:, :, :], rank[:, :, :], 0.5, None, ALU.is_lt))
            step(V.tensor_tensor(sel2[:, :, :], mem[:, :, :], sel1[:, :, :], ALU.subtract))
            step(V.tensor_reduce(rden[:, 0:4], lg[:, :, :], AX_X, ALU.max))
            V.tensor_tensor(tmp8[:, :, :], lg[:, :, :], rden[:, 0:4].unsqueeze(2).to_broadcast([P, 4, E]),
                            ALU.subtract).then_inc(pe_in, 1)
            dve.wait_ge(pe_exp, 1)
            step(V.tensor_tensor(gate[:, :, :], gate[:, :, :], mem[:, :, :], ALU.mult))
            step(V.tensor_reduce(rden[:, 0:4], gate[:, :, :], AX_X, ALU.add))
            step(V.reciprocal(rden[:, 4:8], rden[:, 0:4]))
            step(V.tensor_tensor(gate[:, :, :], gate[:, :, :], rden[:, 4:8].unsqueeze(2).to_broadcast([P, 4, E]), ALU.mult))
            for w, sel in enumerate((sel1, sel2)):
                step(V.tensor_tensor(tmp8[:, :, :], gate[:, :, :], sel[:, :, :], ALU.mult))
                step(V.tensor_reduce(gcol[:, 4 * w:4 * w + 4], tmp8[:, :, :], AX_X, ALU.add))
            dve.wait_ge(pos_done, 1)
            step(V.tensor_reduce(cnt[0:1, 0:1], bank[6][0:1, 0:E], AX_X, ALU.max))
            V.tensor_copy(cnt_i[0:1, 0:1], cnt[0:1, 0:1]).then_inc(cnt_ready, 1)
            pos = bank[7][:, 0:4 * E].rearrange("p (t e) -> p t e", t=4)
            step(V.tensor_scalar(tmp8[:, :, :], rank[:, :, :], 0.5, None, ALU.is_gt))
            step(V.tensor_tensor(slot_of[:, :, :, 1], tmp8[:, :, :], tok2.unsqueeze(2).to_broadcast([P, 4, E]), ALU.add))
            step(V.tensor_copy(slot_of[:, :, :, 0], tokid.unsqueeze(2).to_broadcast([P, 4, E])))
            step(V.tensor_scalar(posm[:, :, :], memv[:, :, :], -1e6, 1e6, ALU.mult, ALU.add))
            step(V.tensor_tensor(posm[:, :, :], posm[:, :, :], pos, ALU.add))
            rows_of(2)
            rows_of(3)
            dve.wait_ge(cnt_ready, 1)
            most = dve.value_load(cnt_i[0:1, 0:1], min_val=0, max_val=T)
            with dve.Fori(0, MAXR) as r:
                with dve.If(most > r * P):
                    for e in range(E):
                        if e >= 2:
                            dve.wait_ge(oneh_used, r * E + (e - 1))
                        V.tensor_tensor(onehot[:, e % 2, :].rearrange("p (t s) -> p t s", t=4),
                                        iota.unsqueeze(1).to_broadcast([P, 4, P]),
                                        posm[:, :, e:e + 1].to_broadcast([P, 4, P]), ALU.is_equal).then_inc(oneh_ready, 1)
                    dve.wait_ge(oneh_ready, r * E + E)
                    V.tensor_scalar(posm[:, :, :], posm[:, :, :], -float(P), None, ALU.add).then_inc(iota_ready, 1)
                    dve.wait_ge(iota_ready, r + 1)
                    dve.wait_ge(oneh_used, r * E + E)
                    found = bank[6][:, 0:2 * E].rearrange("p (e w) -> p e w", w=2)
                    V.tensor_copy(slot_tok[:, 0:E], found[:, :, 0])
                    V.tensor_scalar(empty[:, :], found[:, :, 1], 0.5, float(OOB), ALU.is_lt, ALU.mult).then_inc(empty_ready, 1)
                    dve.wait_ge(empty_ready, r + 1)
                    V.tensor_tensor(slot_tok[:, E:2 * E], empty[:, :], found[:, :, 1], ALU.add).then_inc(sidx_ready, 1)

                    def copy_tokens(n, hf):
                        dve.wait_ge(xTH_ready, n * 2 + (hf + 1))
                        V.tensor_tensor(xTL[:, 4 * hf:4 * hf + 4, :].rearrange("p k t -> p (k t)"), bank[7][:, :],
                                        xTH[:, 4 * hf:4 * hf + 4, :].bitcast(F32).rearrange("p k t -> p (k t)"),
                                        ALU.subtract).then_inc(xTL_ready, 1)
                    copy_tokens(r * E, 0)
                    copy_tokens(r * E, 1)
                    with dve.Fori(0, E) as e:
                        n = r * E + e
                        M = AT["moe"] + SPL

                        def copy_hidden(j):
                            dve.wait_ge(mTH_ready, n * 4 + (j + 1))
                            c0, w = groups[j][0], len(groups[j])
                            V.tensor_tensor(mTL[:, c0:c0 + w, :].rearrange("p c t -> p (c t)"), bank[0 if j == 3 else 4][:, 0:P * w],
                                            mTH[:, c0:c0 + w, :].bitcast(F32).rearrange("p c t -> p (c t)"),
                                            ALU.subtract).then_inc(mTL_ready, 1)
                        for j in range(MBLK):
                            for x in range(3):
                                split_low(M + 4 * j + x, n, MPER)
                            dve.wait_ge(msilu_ready, n * 4 + (j + 1))
                            dve.wait_ge(piece_done, count(AT["moe"] + 4 * j + 4, n, MPER))
                            V.tensor_tensor(mh[:, MB * j:MB * j + MB], sg[:, j % 2, :], bank[2 * (j % 2) + 1][:, 0:MB],
                                            ALU.mult).then_inc(mh_ready, 1)
                            split_low(M + 4 * j + 3, n, MPER)
                            if j:
                                copy_hidden(j - 1)
                        with dve.If(e < E - 1):
                            copy_tokens(n + 1, 0)
                        with dve.Else():
                            dve.wait_ge(my_stored, n * 16)
                            dve.sem_inc(dve_passed, 1)
                        copy_hidden(3)
                        for x in range(16, 20):
                            split_low(M + x, n, MPER)
                        with dve.If(e < E - 1):
                            copy_tokens(n + 1, 1)
                        split_low(M + 20, n, MPER)
                        with dve.If(e < E - 1):
                            for x in range(21, 24):
                                split_low(M + x, n, MPER)
                        dve.wait_ge(piece_done, count(AT["moe"] + 24, n, MPER))
                        V.tensor_copy(yev[:, 512:1024], bank[6][:, :]).then_inc(my_copied, 1)
                    dve.wait_ge(my_stored, (r * E + E) * 16)
                    with dve.If(most > r * P + P):
                        for x in range(21, 24):
                            split_low(AT["moe"] + SPL + x, r * E + (E - 1), MPER)
            for x, (t0, r) in enumerate(TLAST):
                i = t0 // P
                dve.wait_ge(hT_done, x + 1)
                dve.wait_ge(y12_loaded[x], 16)
                for hf in range(2):
                    V.scalar_tensor_tensor(yo[0:r, x, 512 * hf:512 * hf + 512], y12[0:r, x, 512 * hf:512 * hf + 512],
                                           gcol[0:r, i:i + 1], bank[YB[x][hf]][0:r, :], ALU.mult, ALU.add
                                           ).then_inc(y_half, 1)
                dve.wait_ge(y_half, 2 * x + 2)
                V.scalar_tensor_tensor(yo[0:r, x, :], y12[0:r, x, D:2 * D], gcol[0:r, 4 + i:5 + i], yo[0:r, x, :],
                                       ALU.mult, ALU.add).then_inc(y_ready, 1)


def kernel(**inputs):
    import concourse.bacc as bacc
    from concourse.bass_utils import run_bass_kernel_spmd

    x = {k: np.asarray(v) for k, v in inputs.items()}
    c = np.ascontiguousarray

    def tiles(w):
        return c(w.reshape(-1, P, w.shape[-1]).transpose(1, 0, 2)).reshape(P, -1)

    A = H * HD
    tok = np.concatenate([x["meta_tokens"], x["x_prompt"][0], x["x_sample"].reshape(TSM, D)], axis=0)
    params, vf, col, wo = [], [], [], []
    p = np.arange(P)
    sinks = x["sinks"]
    for l in range(DEPTH):
        w = x["w_in"][l]
        q_a, k_a, v_a, f_a, q_b, k_b, v_b = np.split(w, [A, 2 * A, 3 * A, 3 * A + H, 4 * A + H, 4 * A + H + P], axis=1)
        w648 = np.concatenate([v_a, v_b, f_a], axis=1)
        vf.append(np.stack([tiles(w648[2 * P * i:2 * P * i + 2 * P]) for i in range(4)]))
        pair_cols = [np.r_[HD * j:HD * j + HD, HD * (4 + j):HD * (4 + j) + HD] for j in range(NPAIR)]
        heads = [tiles(q_a[:, P * i:P * i + P]) for i in range(4)] + [tiles(k_a[:, P * i:P * i + P]) for i in range(4)]
        heads += [tiles(k_b)] + [tiles(q_b[:, pc]) for pc in pair_cols]
        col.append(np.stack([heads[i] for i in COLS]))
        rows = np.concatenate([np.arange(A)] + [A + pc for pc in pair_cols])
        w_o = x["w_out"][l][rows]
        wo.append(np.stack([tiles(w_o[:, P * m:P * m + P]) for m in range(KD)]))
        sk = np.zeros((P, NPAIR, 4), sinks.dtype)
        for j in range(NPAIR):
            sk[:, j, 0], sk[:, j, 1] = sinks[l, j], sinks[l, 4 + j]
            sk[:, j, 2] = sinks[l][np.where(p < 64, j, 4 + j)]
            sk[:, j, 3] = sinks[l][np.where((p // 16) % 2 == 0, j, 4 + j)]
        cols = [x["g_attn"][l].reshape(KD, P).T, x["g_ffn"][l].reshape(KD, P).T]
        cols += [np.tile(x[n][l], 2)[:, None] for n in ("qn_a", "kn_a", "qn_b", "kn_b")]
        cols += [np.tile(x["b_f"][l], (P, 1)), sk.reshape(P, -1), np.tile(x["b_router"][0], (P, 1))]
        params.append(np.concatenate(cols, axis=1))
    gu = np.stack([tiles(x[n][0][:, P * i:P * i + P]) for i in range(FCH) for n in ("w_gate", "w_up")])
    wd = np.stack([tiles(x["w_down"][0][FF // 2 * hf:FF // 2 * (hf + 1), P * m:P * m + P]) for m in range(KD)
                   for hf in range(2)])
    egu = np.stack([x[n][0].reshape(E, 2, KD // 2, P, MBLK, MB).transpose(0, 4, 1, 3, 2, 5) for n in ("we_gate", "we_up")],
                   axis=2).reshape(E * 16, P, MGW)
    ed = x["we_down"][0].reshape(E, MCH, P, 4, 256).transpose(0, 3, 2, 1, 4)
    ed0, ed1 = (c(a).reshape(E * 4, P, -1) for a in (ed[:, :, :, :MD0], ed[:, :, :, MD0:]))

    kf, vf_c = x["cache_fox_k"], x["cache_fox_v"]
    ck = c(kf.reshape(DEPTH, BS, PAST, NPAIR, P).transpose(0, 3, 4, 1, 2)).reshape(DEPTH, NPAIR, P, -1)
    cv = c(vf_c.reshape(DEPTH, BS, 2, P, NPAIR, P).transpose(0, 4, 3, 1, 2, 5)).reshape(DEPTH, NPAIR, P, -1)
    cl = c(x["cache_fox_logf"].reshape(DEPTH, BS, 2, P, NPAIR, 2).transpose(0, 3, 2, 4, 1, 5)).reshape(DEPTH, P, -1)
    cks = c(x["cache_swa_k"].reshape(DEPTH, BS, P, P).transpose(0, 3, 1, 2)).reshape(DEPTH, P, -1)
    cvs = c(x["cache_swa_v"].reshape(DEPTH, BS, P, P).transpose(0, 2, 1, 3)).reshape(DEPTH, P, -1)
    arrays = {
        "xT": c(tok.T.reshape(KD, P, T).transpose(1, 0, 2)), "params": np.stack(params),
        "w_vf": np.stack(vf), "w_col": np.stack(col), "w_o": np.stack(wo), "w_gu": gu, "w_d": wd,
        "w_egu": egu, "w_ed0": ed0, "w_ed1": ed1, "w_r": tiles(x["w_router"][0]),
        "ck_fox": ck, "cv_fox": cv, "clf": cl, "ck_swa": cks, "cv_swa": cvs, "tables": _TABLES,
    }
    nc = bacc.Bacc("TRN2", target_bir_lowering=False, num_devices=1)
    args = {}
    for name, a in arrays.items():
        arrays[name] = c(a)
        args[name] = nc.dram_tensor(name, a.shape, mybir.dt.from_np(a.dtype), kind="ExternalInput").ap()
    outs = {"o_kfox": (DEPTH, NPAIR, P, T), "o_vfox": (DEPTH, T, A), "o_lf": (DEPTH, T, H), "o_kswa": (DEPTH, P, T),
            "o_vswa": (DEPTH, T, P), "o_y": (T, D)}
    for name, shape in outs.items():
        args[name] = nc.dram_tensor(name, shape, F32, kind="ExternalOutput").ap()
    build(nc, **args)
    r = run_bass_kernel_spmd(nc, [arrays], core_ids=[0]).results[0]
    y = r["o_y"]
    kf = r["o_kfox"].reshape(DEPTH, H, HD, T).transpose(0, 3, 1, 2)
    vf_o = r["o_vfox"].reshape(DEPTH, T, H, HD)
    ks = r["o_kswa"].reshape(DEPTH, 2, HD, T).transpose(0, 3, 1, 2)
    vs = r["o_vswa"].reshape(DEPTH, T, 2, HD)
    lf = r["o_lf"]
    W = 128

    def prompt(a):
        return c(a[:, None, :TP])

    def sample(a):
        return c(a[:, TP:].reshape((DEPTH, BS, TSEQ) + a.shape[2:]))

    return (c(y[NMETA:TP][None]), c(y[TP:].reshape(BS, TSEQ, D)), prompt(kf), prompt(vf_o), prompt(lf),
            c(ks[:, None, TP - W:TP]), c(vs[:, None, TP - W:TP]), sample(kf), sample(vf_o), sample(lf),
            sample(ks), sample(vs))
```
